# Optimizing a Trainium2 kernel written in Bass

```python
import math
import jax
import jax.numpy as jnp
from jax import lax
import numpy as np

D_MODEL = 1024
BATCH = 1
SEQ = 256
DEPTH = 2
DEC_BATCH = 8
DEC_SEQ = 8
PAST_LEN = 1024
PAGE_SIZE = 128

N_A_LAYERS = DEPTH // 2
N_B_LAYERS = DEPTH - N_A_LAYERS
H_A = 8
DK_A = D_MODEL // (2 * H_A)
DV_A = D_MODEL // H_A
QK_W = H_A * DK_A
V_W = H_A * DV_A
IN_A_W = 2 * QK_W + 2 * V_W + 2 * H_A
CHUNK = 64
H_B = 8
HD_B = D_MODEL // H_B
QB_W = H_B * HD_B
BLOCK = 256
TOPK = 3
Q_BLOCK = 64
D_FF = 4 * D_MODEL
ALPHA = (2.0 * DEPTH) ** 0.25
BETA = (8.0 * DEPTH) ** -0.25
LN_EPS = 1e-5
F32 = jnp.float32

kernel_name = "yoco_mlstm_moba_decoder_step"

def layer_norm(x, g, b):
    xf = x.astype(F32)
    mu = xf.mean(-1, keepdims=True)
    var = jnp.square(xf - mu).mean(-1, keepdims=True)
    return ((xf - mu) * lax.rsqrt(var + LN_EPS) * g.astype(F32) + b.astype(F32)).astype(x.dtype)

def sq_relu_mlp(x, w_up, w_down):
    return jnp.square(jax.nn.relu(x @ w_up)) @ w_down

def alibi_slopes(n):
    return 2.0 ** (-8.0 * jnp.arange(1, n + 1, dtype=F32) / n)

def mlstm_chunkwise(q, k, v, ig, lf, C0, n0, m0):
    B, L, H, DK = q.shape
    c = math.gcd(L, CHUNK)
    nc = L // c

    def to_chunks(a):
        a = a.reshape((B, nc, c, H) + a.shape[3:])
        return jnp.swapaxes(jnp.moveaxis(a, 1, 0), 2, 3)

    causal = jnp.tril(jnp.ones((c, c), dtype=bool))

    def step(carry, xs):
        C, n, m = carry
        qc, kc, vc, ic, fc = xs
        b = jnp.cumsum(fc, axis=-1)
        dmat = jnp.where(causal, b[..., :, None] - b[..., None, :] + ic[..., None, :], -jnp.inf)
        inter = b + m[..., None]
        m_t = jnp.maximum(inter, dmat.max(-1))
        w = jnp.exp(dmat - m_t[..., None])
        a = jnp.exp(inter - m_t)
        s = jnp.einsum('bhtd,bhsd->bhts', qc, kc) * w
        num = jnp.einsum('bhts,bhsv->bhtv', s, vc) + a[..., None] * jnp.einsum('bhtd,bhdv->bhtv', qc, C)
        den = s.sum(-1) + a * jnp.einsum('bhtd,bhd->bht', qc, n)
        h = num / jnp.maximum(jnp.abs(den), jnp.exp(-m_t))[..., None]
        g = b[..., -1:] - b + ic
        inter_end = b[..., -1] + m
        m_new = jnp.maximum(inter_end, g.max(-1))
        ws = jnp.exp(g - m_new[..., None])
        ae = jnp.exp(inter_end - m_new)
        C_new = ae[..., None, None] * C + jnp.einsum('bhs,bhsd,bhsv->bhdv', ws, kc, vc)
        n_new = ae[..., None] * n + jnp.einsum('bhs,bhsd->bhd', ws, kc)
        return (C_new, n_new, m_new), h

    carry0 = (C0.astype(F32), n0.astype(F32), m0.astype(F32))
    (C, n, m), h = lax.scan(step, carry0, (to_chunks(q), to_chunks(k), to_chunks(v), to_chunks(ig), to_chunks(lf)))
    h = jnp.moveaxis(jnp.swapaxes(h, 2, 3), 0, 1).reshape(B, L, H, v.shape[-1])
    return h, (C, n, m)

def mlstm_mixer(x, w_in, b_gate, w_out, C0, n0, m0):
    B, L, _ = x.shape
    proj = x @ w_in
    q, k, v, o, g = jnp.split(proj, [QK_W, 2 * QK_W, 2 * QK_W + V_W, 2 * QK_W + 2 * V_W], axis=-1)
    q = q.reshape(B, L, H_A, DK_A).astype(F32)
    k = k.reshape(B, L, H_A, DK_A).astype(F32) * (DK_A ** -0.5)
    v = v.reshape(B, L, H_A, DV_A).astype(F32)
    g = g.astype(F32) + b_gate.astype(F32)
    ig = g[..., :H_A]
    lf = jax.nn.log_sigmoid(g[..., H_A:])
    h, state = mlstm_chunkwise(q, k, v, ig, lf, C0, n0, m0)
    h = jax.nn.sigmoid(o.astype(F32)) * h.reshape(B, L, V_W)
    return h.astype(x.dtype) @ w_out, state

def moba_select(q, means, pos_q):
    nb = means.shape[1]
    own = pos_q // BLOCK
    scores = jnp.einsum('bqhd,bnhd->bqhn', q.astype(F32), means)
    past = jnp.arange(nb)[None, :] < own[:, None]
    scores = jnp.where(past[None, :, None, :], scores, -jnp.inf)
    kk = min(TOPK, nb)
    _, idx = lax.top_k(scores, kk)
    valid = jnp.arange(kk)[None, :] < own[:, None]
    return idx, valid

def moba_attend(q, pos_q, sel_k, sel_v, sel_idx, sel_valid, own_k, own_v, own_pos, slopes):
    B, Q, H, D = q.shape
    nsel = sel_k.shape[3]
    scale = D ** -0.5
    lg_sel = jnp.einsum('bqhd,bqhrkd->bqhrk', q, sel_k).astype(F32) * scale
    sel_pos = sel_idx[..., None] * BLOCK + jnp.arange(BLOCK)
    dist_sel = (pos_q[None, :, None, None, None] - sel_pos).astype(F32)
    lg_sel = jnp.where(sel_valid[None, :, None, :, None],
                       lg_sel - slopes[None, None, :, None, None] * dist_sel, -jnp.inf)
    lg_own = jnp.einsum('bqhd,bkhd->bqhk', q, own_k).astype(F32) * scale
    dist_own = pos_q[:, None] - own_pos[None, :]
    lg_own = jnp.where((dist_own >= 0)[None, :, None, :],
                       lg_own - slopes[None, None, :, None] * dist_own.astype(F32)[None, :, None, :], -jnp.inf)
    p = jax.nn.softmax(jnp.concatenate([lg_sel.reshape(B, Q, H, nsel * BLOCK), lg_own], axis=-1), axis=-1)
    p_sel = p[..., :nsel * BLOCK].reshape(B, Q, H, nsel, BLOCK).astype(q.dtype)
    p_own = p[..., nsel * BLOCK:].astype(q.dtype)
    return (jnp.einsum('bqhrk,bqhrkd->bqhd', p_sel, sel_v)
            + jnp.einsum('bqhk,bkhd->bqhd', p_own, own_v))

def moba_prompt_kv_side(k, v):
    B, S, H, D = k.shape
    nb = -(-S // BLOCK)
    widths = ((0, 0), (0, nb * BLOCK - S), (0, 0), (0, 0))
    k_blk = jnp.pad(k, widths).reshape(B, nb, BLOCK, H, D)
    v_blk = jnp.pad(v, widths).reshape(B, nb, BLOCK, H, D)
    means = k_blk.astype(F32).mean(2)
    return k_blk, v_blk, means

def moba_prompt_attend(q, ctx, slopes):
    k_blk, v_blk, means = ctx
    B, S, H, D = q.shape
    k_bh = jnp.transpose(k_blk, (0, 3, 1, 2, 4))
    v_bh = jnp.transpose(v_blk, (0, 3, 1, 2, 4))
    bi = jnp.arange(B)[:, None, None, None]
    hi = jnp.arange(H)[None, None, :, None]

    def one_block(start):
        qb = lax.dynamic_slice_in_dim(q, start, Q_BLOCK, axis=1)
        pos = start + jnp.arange(Q_BLOCK)
        idx, valid = moba_select(qb, means, pos)
        sel_k = k_bh[bi, hi, idx]
        sel_v = v_bh[bi, hi, idx]
        own = start // BLOCK
        own_k = lax.dynamic_index_in_dim(k_blk, own, axis=1, keepdims=False)
        own_v = lax.dynamic_index_in_dim(v_blk, own, axis=1, keepdims=False)
        own_pos = own * BLOCK + jnp.arange(BLOCK)
        return moba_attend(qb, pos, sel_k, sel_v, idx, valid, own_k, own_v, own_pos, slopes)

    out = lax.map(one_block, jnp.arange(0, S, Q_BLOCK))
    return jnp.moveaxis(out, 0, 1).reshape(B, S, H, D)

def moba_sample_kv_side(k_new, v_new, cache_k, cache_v, page_table):
    B, L, H, D = k_new.shape
    n_pages = page_table.shape[1]
    past_len = n_pages * PAGE_SIZE
    ppb = BLOCK // PAGE_SIZE
    n_blocks = past_len // BLOCK + 1
    k_past = cache_k[page_table]
    page_sums = k_past.astype(F32).sum(2)
    page_sums = jnp.pad(page_sums, ((0, 0), (0, n_blocks * ppb - n_pages), (0, 0), (0, 0)))
    means = page_sums.reshape(B, n_blocks, ppb, H, D).sum(2) / BLOCK
    own_start = (past_len // BLOCK) * BLOCK
    r_pages = (past_len - own_start) // PAGE_SIZE
    own_k_past = k_past[:, n_pages - r_pages:].reshape(B, r_pages * PAGE_SIZE, H, D)
    own_v_past = cache_v[page_table[:, n_pages - r_pages:]].reshape(B, r_pages * PAGE_SIZE, H, D)
    own_k = jnp.concatenate([own_k_past, k_new], axis=1)
    own_v = jnp.concatenate([own_v_past, v_new], axis=1)
    own_pos = own_start + jnp.arange(r_pages * PAGE_SIZE + L)
    return means, own_k, own_v, own_pos

def moba_sample_attend(q, ctx, cache_k, cache_v, page_table, slopes):
    means, own_k, own_v, own_pos = ctx
    B, L, H, D = q.shape
    n_pages = page_table.shape[1]
    past_len = n_pages * PAGE_SIZE
    ppb = BLOCK // PAGE_SIZE
    pos_q = past_len + jnp.arange(L)
    idx, valid = moba_select(q, means, pos_q)
    r = idx.shape[-1]
    lp = jnp.minimum(idx[..., None] * ppb + jnp.arange(ppb), n_pages - 1)
    phys = page_table[jnp.arange(B)[:, None, None, None, None], lp]
    hh = jnp.arange(H)[None, None, :, None, None]
    sel_k = cache_k[phys, :, hh].reshape(B, L, H, r, BLOCK, D)
    sel_v = cache_v[phys, :, hh].reshape(B, L, H, r, BLOCK, D)
    return moba_attend(q, pos_q, sel_k, sel_v, idx, valid, own_k, own_v, own_pos, slopes)

def trunk(x, C0, n0, m0, kv_side, attend, w_in_a, b_gate_a, w_out_a, w_q_b, w_out_b, w_kv,
          w_up, w_down, ln_g, ln_b):
    B, L, _ = x.shape
    Cs, ns, ms = [], [], []
    k = v = ctx = None
    for layer in range(DEPTH):
        if layer < N_A_LAYERS:
            h, (C, n, m) = mlstm_mixer(x, w_in_a[layer], b_gate_a[layer], w_out_a[layer],
                                       C0[layer], n0[layer], m0[layer])
            Cs.append(C)
            ns.append(n)
            ms.append(m)
        else:
            if layer == N_A_LAYERS:
                kv = x @ w_kv
                k = kv[..., :QB_W].reshape(B, L, H_B, HD_B)
                v = kv[..., QB_W:].reshape(B, L, H_B, HD_B)
                ctx = kv_side(k, v)
            j = layer - N_A_LAYERS
            q = (x @ w_q_b[j]).reshape(B, L, H_B, HD_B)
            h = attend(q, ctx).reshape(B, L, QB_W) @ w_out_b[j]
        x = layer_norm(ALPHA * x + h, ln_g[layer, 0], ln_b[layer, 0])
        x = layer_norm(ALPHA * x + sq_relu_mlp(x, w_up[layer], w_down[layer]), ln_g[layer, 1], ln_b[layer, 1])
    return x, jnp.stack(Cs), jnp.stack(ns), jnp.stack(ms), k, v

def setup_inputs(seed: int = 0) -> dict:
    key = jax.random.key(seed)
    ks = jax.random.split(key, 20)
    nrm = jax.random.normal
    n_pages = PAST_LEN // PAGE_SIZE
    n_used = DEC_BATCH * n_pages
    n_pool = (5 * n_used + 3) // 4
    page_table = jax.random.permutation(ks[0], n_pool)[:n_used].reshape(DEC_BATCH, n_pages).astype(jnp.int32)
    x_prompt = nrm(ks[1], (BATCH, SEQ, D_MODEL), F32)
    x_sample = nrm(ks[2], (DEC_BATCH, DEC_SEQ, D_MODEL), F32)
    state_C = 0.5 * nrm(ks[3], (N_A_LAYERS, DEC_BATCH, H_A, DK_A, DV_A), F32)
    state_n = nrm(ks[4], (N_A_LAYERS, DEC_BATCH, H_A, DK_A), F32)
    state_m = nrm(ks[5], (N_A_LAYERS, DEC_BATCH, H_A), F32)
    cache_k = nrm(ks[6], (n_pool, PAGE_SIZE, H_B, HD_B), F32)
    cache_v = nrm(ks[7], (n_pool, PAGE_SIZE, H_B, HD_B), F32)
    in_scale = jnp.concatenate([jnp.ones((2 * QK_W,), F32), jnp.full((V_W,), BETA, F32),
                                jnp.ones((V_W + 2 * H_A,), F32)]) * (D_MODEL ** -0.5)
    w_in_a = nrm(ks[8], (N_A_LAYERS, D_MODEL, IN_A_W), F32) * in_scale
    b_gate_a = jnp.concatenate([0.1 * nrm(ks[9], (N_A_LAYERS, H_A), F32),
                                3.0 + jax.random.uniform(ks[10], (N_A_LAYERS, H_A), F32, 0.0, 3.0)], axis=-1)
    w_out_a = nrm(ks[11], (N_A_LAYERS, V_W, D_MODEL), F32) * (V_W ** -0.5 * BETA)
    w_q_b = nrm(ks[12], (N_B_LAYERS, D_MODEL, QB_W), F32) * (D_MODEL ** -0.5)
    w_out_b = nrm(ks[13], (N_B_LAYERS, QB_W, D_MODEL), F32) * (QB_W ** -0.5 * BETA)
    kv_scale = jnp.concatenate([jnp.ones((QB_W,), F32), jnp.full((QB_W,), BETA, F32)]) * (D_MODEL ** -0.5)
    w_kv = nrm(ks[14], (D_MODEL, 2 * QB_W), F32) * kv_scale
    w_up = nrm(ks[15], (DEPTH, D_MODEL, D_FF), F32) * (D_MODEL ** -0.5)
    w_down = nrm(ks[16], (DEPTH, D_FF, D_MODEL), F32) * (D_FF ** -0.5 * BETA)
    ln_g = 1.0 + 0.02 * nrm(ks[17], (DEPTH, 2, D_MODEL), F32)
    ln_b = 0.02 * nrm(ks[18], (DEPTH, 2, D_MODEL), F32)
    return {"x_prompt": x_prompt, "x_sample": x_sample, "state_C": state_C, "state_n": state_n,
            "state_m": state_m, "cache_k": cache_k, "cache_v": cache_v, "page_table": page_table,
            "w_in_a": w_in_a, "b_gate_a": b_gate_a, "w_out_a": w_out_a, "w_q_b": w_q_b,
            "w_out_b": w_out_b, "w_kv": w_kv, "w_up": w_up, "w_down": w_down,
            "ln_g": ln_g, "ln_b": ln_b}

def reference(x_prompt, x_sample, state_C, state_n, state_m, cache_k, cache_v, page_table,
              w_in_a, b_gate_a, w_out_a, w_q_b, w_out_b, w_kv, w_up, w_down, ln_g, ln_b):
    slopes = alibi_slopes(H_B)
    bp = x_prompt.shape[0]
    zC = jnp.zeros((N_A_LAYERS, bp, H_A, DK_A, DV_A), F32)
    zn = jnp.zeros((N_A_LAYERS, bp, H_A, DK_A), F32)
    zm = jnp.zeros((N_A_LAYERS, bp, H_A), F32)
    y_prompt, p_C, p_n, p_m, p_k, p_v = trunk(
        x_prompt, zC, zn, zm, moba_prompt_kv_side,
        lambda q, ctx: moba_prompt_attend(q, ctx, slopes),
        w_in_a, b_gate_a, w_out_a, w_q_b, w_out_b, w_kv, w_up, w_down, ln_g, ln_b)
    y_sample, s_C, s_n, s_m, s_k, s_v = trunk(
        x_sample, state_C, state_n, state_m,
        lambda k, v: moba_sample_kv_side(k, v, cache_k, cache_v, page_table),
        lambda q, ctx: moba_sample_attend(q, ctx, cache_k, cache_v, page_table, slopes),
        w_in_a, b_gate_a, w_out_a, w_q_b, w_out_b, w_kv, w_up, w_down, ln_g, ln_b)
    return (y_prompt, y_sample, p_C, p_n, p_m, p_k, p_v, s_C, s_n, s_m, s_k, s_v)


_drawn_inputs = setup_inputs


def setup_inputs(seed=0):
    import zlib

    import numpy as np

    out = dict(_drawn_inputs(seed))
    spreads = {}
    factors = {}
    for name, (base, spread) in spreads.items():
        noise = np.random.default_rng([zlib.crc32(name.encode()), seed]).standard_normal(out[name].shape)
        drawn = base * np.exp(spread * noise) if base else spread * noise
        out[name] = jnp.asarray(drawn.astype(out[name].dtype))
    for name, factor in factors.items():
        out[name] = (out[name] * factor).astype(out[name].dtype)
    return out
```

```python
import numpy as np
import concourse.bass as bass
from concourse import mybir
from contextlib import ExitStack

F32 = mybir.dt.float32
F32R = mybir.dt.float32r
I32 = mybir.dt.int32
ALU = mybir.AluOpType
ACT = mybir.ActivationFunctionType
AX = mybir.AxisListType

DM = 1024
NC8 = DM // 128
TP, TS = 256, 64
T = TP + TS
NB, LS = 8, 8
H = 8
DK = 64
PAGES = 8
PG = 128
BIG = 1.0e30
ALPHA = 4.0 ** 0.25
EPS = 1e-5
QSCALE = 128.0 ** -0.5

Q_QK, Q_V, Q_O, Q_WOA, Q_MLP0, Q_WK, Q_WV, Q_WQ, Q_WOB, Q_MLP1, N_QUADS = 0, 1, 2, 3, 4, 12, 13, 14, 15, 16, 24
UPS = [Q_MLP0 + 2 * g for g in range(4)] + [Q_MLP1 + 2 * g for g in range(4)]
ACT_QUADS = sorted([Q_QK, Q_V, Q_O, Q_WK, Q_WV, Q_WQ] + UPS)
NT = 8 * N_QUADS
RAW, SPL = 4, 4

SLOPES = [2.0 ** -(h + 1) for h in range(H)]


def constants():
    p = np.arange(128)
    ident = np.eye(128, dtype=np.float32)
    ones = np.ones((128, 128), np.float32)
    m = np.full((128, 448), 0.0, np.float32)
    t = np.arange(256)
    m[:, 0:256] = np.where(p[:, None] <= t[None, :], 0, BIG)
    m[:, 256:384] = np.where(p[:, None] <= p[None, :], 0, BIG)
    s = np.arange(64)
    m[0:64, 384:448] = np.where((s[:, None] // 8 == s[None, :] // 8) & (s[:, None] <= s[None, :]), 0, BIG)
    start = np.zeros(T, bool)
    start[0] = True
    start[TP::LS] = True
    rows = np.zeros((128, 2 * T), np.float32)
    rows[:, 0:T] = np.where(start, 0, 1)
    rows[:, T:] = np.where(start, -BIG, 0)
    sel = np.zeros((128, 12 * 128), np.float32)
    for h in range(H):
        sel[h, h * 128:(h + 1) * 128] = 1
        sel[h, (8 + h // 2) * 128 + 64 * (h % 2):(8 + h // 2) * 128 + 64 * (h % 2) + 64] = 1
    d = np.zeros((128, 384), np.float32)
    d[:, 0:128] = np.where(p[None, :] <= p[:, None], p[None, :] - p[:, None], -BIG)
    d[:, 128:384] = np.where(t[None, :] <= 128 + p[:, None], t[None, :] - 128 - p[:, None], -BIG)
    sl = np.array(SLOPES)
    q = np.arange(LS)
    dist = PAGES * PG + q[None, None, :] - (PG * np.arange(PAGES)[None, :, None] + p[:, None, None])
    bs = -(sl[None, :, None, None] * dist[:, None]).reshape(128, 512).astype(np.float32)
    bo = np.zeros((128, 512), np.float32)
    sb, sk = s // 8, s % 8
    ok = (sb[:, None, None, None] == np.arange(NB)[None, None, :, None]) & (sk[:, None, None, None] <= q)
    dd = -(sl[None, :, None, None] * (q[None, None, None, :] - sk[:, None, None, None]))
    bo[0:64] = np.where(ok, dd, -BIG).reshape(64, 512)
    n = np.tile(np.repeat(np.arange(4) + 1.0, LS), H)[None, :].repeat(128, 0).astype(np.float32)
    bm = np.zeros((128, 8), np.float32)
    bm[0:64] = (sb[:, None] == np.arange(NB)[None, :])
    base = np.concatenate([ident, ones, bm], 1)
    return {"c_base": base, "c_mlstm": np.concatenate([m, rows], 1), "c_sel": sel[0:8].copy(),
            "c_attn": np.concatenate([d, bs, bo, n], 1)}


def bcast(ap, axis, n):
    v = ap.unsqueeze(axis)
    shape = list(v.shape)
    shape[axis] = n
    return v.to_broadcast(shape)


class Own:

    def __init__(self, eng, sem):
        self.eng, self.sem, self.n, self.shift = eng, sem, 0, 0

    def __call__(self, ins):
        self.n += 1
        ins.then_inc(self.sem, 1)
        self.eng.wait_ge(self.sem, self.shift + self.n)


def evac(t):
    q = t // 8
    mine = q in ACT_QUADS
    before = sum(1 for x in range(q) if (x in ACT_QUADS) == mine)
    return (0 if mine else 1), 8 * before + t % 8 + 1


def build(nc, x_prompt, x_sample, state_C, state_n, state_m, cache_k, cache_v, page_table,
          w_in_a, b_gate_a, w_out_a, w_q_b, w_out_b, w_kv, w_up, w_down, ln_g, ln_b,
          c_base, c_mlstm, c_sel, c_attn,
          y_prompt, y_sample, p_C, p_n, p_m, p_k, p_v, s_C, s_n, s_m, s_k_d, s_v_d):
    ctx = ExitStack()
    with ctx:
        at = [nc.sbuf_base + (-nc.sbuf_base) % 64]
        top = nc.sbuf_usable_end

        def put(name, shape, dt=F32, where=at):
            size = 4 * int(np.prod(shape[1:]))
            t = nc.alloc_sbuf_tensor_at(name, shape, dt, offset=where[0])
            where[0] += size + (-size) % 32
            assert where[0] <= top, (name, where[0], top)
            return t

        raw = [put(f"raw{i}", [128, 8, 256]) for i in range(RAW)]
        WH = [put(f"w_hi{i}", [128, 8, 128], F32R) for i in range(SPL)]
        WL = [put(f"w_lo{i}", [128, 8, 128], F32R) for i in range(SPL)]
        X = put("x", [128, NC8, T])
        XH = put("x_hi", [128, NC8, T], F32R)
        XL = put("x_lo", [128, NC8, T], F32R)
        qk_at = [at[0]]
        HH = put("h_hi", [128, NC8, T], F32R)
        HL = put("h_lo", [128, NC8, T], F32R)
        QA = put("q_attn", [128, H, T], F32, qk_at)
        KA = put("k_attn", [128, H, T], F32, qk_at)
        VT = put("v_tok", [128, 3, DM])
        FR = [put(f"fm{i}", [128, T]) for i in range(2)]
        FS = [put(f"sq{i}", [128, T]) for i in range(2)]
        A1 = put("sum_x", [128, T])
        A2 = put("sum_xx", [128, T])
        SQ = put("xx", [128, T])
        base = put("base", [128, 264])
        ident, ones, bmask = base[:, 0:128], base[:, 128:256], base[:, 256:264]
        lnT = put("ln_cols", [128, 64])
        bg = put("b_gate", [40, 1])
        table = put("page_table", [1, NB * PAGES], I32)
        phase_const = [at[0]]
        cat = put("attn_tables", [128, 384 + 512 + 512 + 256])
        dist, bias_past, bias_own, nidx = cat[:, 0:384], cat[:, 384:896], cat[0:64, 896:1408], cat[:, 1408:1664]
        cml = put("mlstm_tables", [128, 448 + 2 * T], F32, phase_const)
        n0 = put("n0", [8, H * DK], F32, phase_const)
        assert phase_const[0] <= at[0]
        phase = at[0]

        a = [phase]
        C0 = put("C", [128, 4, NB, 128], F32, a)
        ewk = [a[0]]
        E = [put(f"decay{i}", [128, 448], F32, a) for i in range(2)]
        W = [put(f"weight{i}", [128, 448], F32, a) for i in range(2)]
        wsK = put("wsk", [128, 3, 512], F32, a)
        wgraw = put("wg_raw", [128, 8, 16], F32, ewk)
        WGH = put("wg_hi", [128, 8, 128], F32R, ewk)
        WGL = put("wg_lo", [128, 8, 128], F32R, ewk)
        lnN = put("ln_rows", [64, 128], F32, ewk)
        assert ewk[0] <= a[0]
        wk2 = [a[0] - 6144 - 7168]
        wsKm = put("wsk_masked", [64, NB, 128], F32, wk2)
        Wst = put("c_prompt", [128, 512], F32, wk2)
        kT = put("k_mlstm", [128, 4, T], F32, a)
        npr_at = [a[0]]
        npr = put("n_prompt", [1, 512], F32, npr_at)
        qT = put("q_mlstm", [128, 4, T], F32, a)
        sel = put("sel", [8, 12 * 128], F32, a)
        aqT = put("aq", [128, 4, TS], F32, a)
        an = put("aqn", [128, 4, TS], F32, a)
        eo = [put(f"exp_o{i}", [128, T], F32, a) for i in range(2)]
        emS = put("exp_neg_m", [128, T], F32, a)
        rec = put("rec", [128, T], F32, a)
        hg = put("h_gated", [128, T], F32, a)
        R = [put(f"row{i}", [8, T], F32, a) for i in range(6)]
        cols = put("cols", [128, 64], F32, a)
        small = put("small", [8, 64], F32, a)
        m0 = small[:, 0:8]
        ael = small[:, 8:16]
        mnew = small[:, 16:25]
        atr = put("a_rows", [8, TS], F32, a)
        aeP = put("ae_pairs", [128, 4, NB], F32, a)
        nout = put("n_out", [8, 512], F32, a)

        b_ = [phase]
        Kp = [put(f"k_page{i}", [128, DM], F32, b_) for i in range(4)]
        vreg = b_[0]
        Vp = [put(f"v_page{i}", [128, DM], F32, b_) for i in range(4)]
        pr = [vreg]
        PL = [put(f"p_logit{i}", [128, 384], F32, pr) for i in range(2)]
        PTt = [put(f"p_turned{i}", [128, 384], F32, pr) for i in range(2)]
        pst = put("p_stats", [128, 8 * 8], F32, pr)
        assert pr[0] <= b_[0]
        ln_at = [vreg]
        LT = [put(f"ln_t{i}", [128, 2, T], F32, ln_at) for i in range(2)]
        mu = put("ln_mu", [128, T], F32, ln_at)
        var = put("ln_var", [128, T], F32, ln_at)
        rs = put("ln_rstd", [128, T], F32, ln_at)
        tmp = put("ln_tmp", [128, T], F32, ln_at)
        assert ln_at[0] <= b_[0]
        KT = [put(f"k_turned{i}", [128, H, 128], F32, b_) for i in range(2)]
        LO = put("own_logits", [64, 512], F32, b_)
        SL = put("scores", [128, 512], F32, b_)
        L = put("logits", [128, 512], F32, b_)
        P = put("probs", [128, 512], F32, b_)
        bsum = put("block_sums", [128, 256], F32, b_)[:, :]
        eqs = put("excluded", [128, 256], F32, b_)[:, :]
        s64 = put("small64", [128, 8 * 64], F32, b_)
        Mx, mn, ix, Ps, rc, dg, PO, QB = [s64[:, 64 * i:64 * i + 64] for i in range(8)]
        mcol = put("max_col", [64, 8], F32, b_)
        AT = put("attn_prompt", [128, H, TP], F32, b_)
        AO = put("attn_sample", [128, H, TS], F32, b_)
        KO = [put(f"turned{i}", [128, 3, 128], F32, b_) for i in range(2)]

        ps = [ctx.enter_context(nc.psum_tensor(f"ps{i}", [128, 512], F32)) for i in range(8)]

        def sem(name):
            return ctx.enter_context(nc.semaphore(name))

        s_raw = [sem(f"raw_loaded{i}") for i in range(RAW)]
        s_hi, s_lo, s_mm = sem("w_hi_split"), sem("w_lo_split"), sem("tile_done")
        s_ev = [sem("act_emptied"), sem("dve_emptied")]
        s_x, s_base, s_ml, s_gw, s_ln, s_n0, s_c0, s_at, s_tab = [
            sem(n) for n in ("x_in", "base_in", "mlstm_in", "gate_w_in", "ln_in", "n0_in", "c0_in", "attn_in", "table_in")]
        s_m0 = sem("m0_in")
        s_xt, s_xh, s_xl, s_xf = sem("x_turned"), sem("x_hi_done"), sem("x_lo_done"), sem("x_copied")
        s_lnt, s_lnc = sem("ln_turned"), sem("ln_copied")
        s_d, s_a, s_p = sem("dve_own"), sem("act_own"), sem("pool_own")
        s_gz, s_gh, s_gl, s_gp = sem("gate_zeroed"), sem("gate_hi"), sem("gate_lo"), sem("gate_done")
        s_gabs, s_gln, s_mt, s_emn, s_wsl, s_ws, s_al, s_aex = [
            sem(n) for n in ("gate_abs", "gate_log", "m_rows", "emn_rows", "ws_log", "ws_rows", "a_log", "a_rows_done")]
        s_colp, s_col = sem("cols_turned"), sem("cols_copied")
        s_bcp, s_bc = sem("pairs_cast"), sem("pairs_used")
        s_vt, s_vc = sem("v_turned"), sem("v_copied")
        s_sp, s_D, s_E, s_W = sem("mS_done"), sem("decay_log"), sem("decay_exp"), sem("weights_done")
        s_emp, s_emc, s_num, s_hg, s_hh, s_hl = [
            sem(n) for n in ("emn_cast", "emn_copied", "num_done", "gated", "h_hi_done", "h_lo_done")]
        s_kt, s_wk, s_km, s_cp, s_cadd, s_np, s_nadd = [
            sem(n) for n in ("k_tokens", "wsk_done", "wsk_masked_done", "c_product", "c_added", "n_product", "n_added")]
        s_cae = sem("c_decayed")
        s_sq = sem("relu_squared")
        s_st, s_lnp, s_var, s_rs, s_t, s_F, s_al2 = [
            sem(n) for n in ("sums_done", "stats_cast", "var_done", "rstd_guess", "centred", "ln_out", "x_scaled")]
        s_tp, s_tc, s_tv = sem("turn_done"), sem("turn_copied"), sem("v_turn_copied")
        s_to = [sem(f"turn_out{i}") for i in range(2)]
        s_pS, s_pmx, s_pex, s_pnm, s_pT, s_pTc, s_pV, s_pA = [
            sem(n) for n in ("pS_done", "p_max", "p_exp", "p_norm", "p_turn", "p_turn_copied", "p_out", "p_out_copied")]
        s_k = [sem(f"k_in{i}") for i in range(4)]
        s_v_ = [sem(f"v_in{i}") for i in range(4)]
        s_own, s_lo_ = sem("own_scores"), sem("own_logits_done")
        s_qb, s_ktr, s_kte, s_sc, s_sl, s_pg, s_mx, s_mtr, s_dg, s_mb, s_l3, s_pe, s_psum, s_den, s_pv, s_ao = [
            sem(n) for n in ("q_batch", "k_turned_page", "k_copied_page", "page_scored", "scores_copied", "page_sums",
                             "max_rows", "max_turned", "max_diag", "max_cast", "shifted", "exp_done", "prob_sums",
                             "den_done", "page_summed", "attn_out")]
        s_nm = sem("new_m")
        s_out = sem("stored")
        s_co, s_po = sem("c_stored"), sem("prompt_state_stored")

        block = ctx.enter_context(nc.Block())

        def lhs_k(w):
            return w.rearrange("(k p) n -> p k n", p=128)

        win = w_in_a[0]

        def wsrc(u):
            q, j = u // 4, u % 4
            c = 256 * j
            w, c0 = {Q_QK: (win, 0), Q_V: (win, 1024), Q_O: (win, 2048), Q_WOA: (w_out_a[0], 0),
                     Q_WK: (w_kv, 0), Q_WV: (w_kv, 1024), Q_WQ: (w_q_b[0], 0), Q_WOB: (w_out_b[0], 0)}[q]
            return lhs_k(w[:, c0 + c:c0 + c + 256])

        @block.sync
        def _(sp):
            def load_unit(u, src, more=0):
                if isinstance(more, int) and u < RAW:
                    pass
                else:
                    sp.wait_ge(s_lo, 2 * (u - RAW) + 2 + 2 * more)
                sp.dma_start(raw[u % RAW][:, :, :], src).then_inc(s_raw[u % RAW], 16)

            sp.dma_start(base[:, :], c_base).then_inc(s_base, 16)
            sp.dma_start(VT[:, 0:2, :], x_prompt[0].rearrange("(t p) c -> p t c", p=128)).then_inc(s_x, 16)
            sp.dma_start(VT[0:64, 2, :], x_sample.rearrange("b t c -> (b t) c")).then_inc(s_x, 16)
            sp.dma_start(wgraw[:, :, :], lhs_k(win[:, 3072:3088])).then_inc(s_gw, 16)
            load_unit(0, wsrc(0))
            load_unit(1, wsrc(1))
            sp.dma_start(cml[:, :], c_mlstm).then_inc(s_ml, 16)
            sp.dma_start(sel[:, :], c_sel).then_inc(s_ml, 16)
            sp.dma_start(m0, state_m[0].rearrange("b h -> h b"), allow_slow_non_contiguous=True).then_inc(s_m0, 16)
            sp.dma_start(bg[0:8, :], b_gate_a[0:1, 0:8].rearrange("a h -> h a"), allow_slow_non_contiguous=True).then_inc(s_m0, 16)
            sp.dma_start(bg[32:40, :], b_gate_a[0:1, 8:16].rearrange("a h -> h a"), allow_slow_non_contiguous=True).then_inc(s_m0, 16)
            load_unit(2, wsrc(2))
            load_unit(3, wsrc(3))
            sp.dma_start(lnN[0:32, :], ln_g.rearrange("l w (c p) -> (l w c) p", p=128)).then_inc(s_ln, 16)
            sp.dma_start(lnN[32:64, :], ln_b.rearrange("l w (c p) -> (l w c) p", p=128)).then_inc(s_ln, 16)
            sp.dma_start(n0[:, :], state_n[0].rearrange("b h k -> b (h k)")).then_inc(s_n0, 16)
            sp.dma_start(table[:, :], page_table.rearrange("b p -> (b p)").unsqueeze(0)).then_inc(s_tab, 16)
            for j in range(4):
                for h2 in range(2):
                    sp.dma_start(C0[64 * h2:64 * h2 + 64, j, :, :],
                                 state_C[0, :, 2 * j + h2].rearrange("b k v -> k b v")).then_inc(s_c0, 16)
            for u in range(4, 16):
                load_unit(u, wsrc(u))

            def mlp_loads(first, m):
                with sp.Fori(0, 4) as g:
                    for j in range(4):
                        load_unit(4 * first + j, lhs_k(w_up[m][:, bass.ds(g * 1024 + 256 * j, 256)]), 8 * g)
                    for j in range(4):
                        load_unit(4 * first + 4 + j,
                                  lhs_k(w_down[m][bass.ds(g * 1024, 1024), 256 * j:256 * j + 256]), 8 * g)

            mlp_loads(Q_MLP0, 0)
            for u in range(4 * Q_WK, 4 * Q_WK + 4):
                load_unit(u, wsrc(u))
            sp.wait_ge(s_co, 16 * 8)
            sp.wait_ge(s_po, 16 * 4)
            sp.dma_start(cat[:, :], c_attn).then_inc(s_at, 16)

            def load_k(b, p, freed=None):
                page = sp.value_load(table[0:1, bass.ds(b * PAGES + p, 1)], min_val=0, max_val=cache_k.shape[0] - 1)
                if freed is not None:
                    sp.wait_ge(s_ktr, freed)
                sp.dma_start(Kp[p % 4][:, :], cache_k[bass.ds(page, 1)].rearrange("a t h d -> (a t) (h d)"))\
                    .then_inc(s_k[p % 4], 16)

            sp.wait_ge(s_tab, 16)
            for p in range(4):
                load_k(0, p)
            for u in range(4 * Q_WV, 4 * Q_WOB + 4):
                load_unit(u, wsrc(u))
            for p in range(4, 8):
                load_k(0, p, p - 4 + 1)
            with sp.Fori(0, NB - 1) as i:
                for p in range(8):
                    load_k(i + 1, p, 8 * i + 8 + p - 4 + 1)
            mlp_loads(Q_MLP1, 1)

        @block.tensor
        def _(pe):
            mm = nc.tensor.matmul

            def dense(t, hi, lo, chunk_ready=None, turn=0, ev_shift=0, wait_ev=True):
                if wait_ev and t >= 2:
                    e, n = evac(t - 2)
                    pe.wait_ge(s_ev[e], n + ev_shift)
                pe.wait_ge(s_lo, t + 1 + 16 * turn)
                out = ps[t % 2][:, 0:T]
                for k in range(8):
                    if chunk_ready is not None:
                        pe.wait_ge(*chunk_ready(k))
                    mm(out, WH[t % SPL][:, k, :], hi[:, k, :], start=(k == 0), stop=False)
                    mm(out, WH[t % SPL][:, k, :], lo[:, k, :], start=False, stop=False)
                    last = mm(out, WL[t % SPL][:, k, :], hi[:, k, :], start=False, stop=(k == 7))
                last.then_inc(s_mm, 1)

            def turn3(bank, src):
                nc.tensor.transpose(bank[:, 0:128], src[:, 0:128], ident)
                nc.tensor.transpose(bank[:, 128:256], src[:, 128:256], ident)
                return nc.tensor.transpose(bank[0:64, 256:384], src[:, 256:320], ident)

            pe.wait_ge(s_base, 16)
            pe.wait_ge(s_x, 32)
            for n in range(8):
                if n >= 2:
                    pe.wait_ge(s_xf, n - 1)
                c = slice(128 * n, 128 * n + 128)
                bank = ps[2 + n % 2]
                nc.tensor.transpose(bank[:, 0:128], VT[:, 0, c], ident)
                nc.tensor.transpose(bank[:, 128:256], VT[:, 1, c], ident)
                nc.tensor.transpose(bank[:, 256:320], VT[0:64, 2, c], ident[0:64, 0:64]).then_inc(s_xt, 1)
            pe.wait_ge(s_ln, 32)
            nc.tensor.transpose(ps[4][:, 0:64], lnN[:, :], ident[0:64, 0:64]).then_inc(s_lnt, 1)
            pe.wait_ge(s_gl, 1)
            for k in range(8):
                pe.wait_ge(s_xl, k + 1)
                mm(ps[5][:, 0:T], WGH[:, k, :], XH[:, k, :], start=(k == 0), stop=False)
                mm(ps[5][:, 0:T], WGH[:, k, :], XL[:, k, :], start=False, stop=False)
                last = mm(ps[5][:, 0:T], WGL[:, k, :], XH[:, k, :], start=False, stop=(k == 7))
            last.then_inc(s_gp, 1)
            for n in range(8):
                dense(8 * Q_QK + n, XH, XL)
            pe.wait_ge(s_n0, 16)
            for j in range(4):
                last = nc.tensor.transpose(ps[7][:, 352 + 8 * j:360 + 8 * j], n0[:, 128 * j:128 * j + 128],
                                           ident[0:8, 0:8])
            pe.wait_ge(s_ws, 1)
            for i in range(3):
                w = 128 if i < 2 else 64
                nc.tensor.transpose(ps[7][0:w, 8 * i:8 * i + 8], R[4][:, 128 * i:128 * i + w], ident[0:8, 0:8])
                nc.tensor.transpose(ps[7][0:w, 24 + 8 * i:32 + 8 * i], R[5][:, 128 * i:128 * i + w], ident[0:8, 0:8])
            pe.wait_ge(s_aex, 2)
            nc.tensor.transpose(ps[7][0:8, 48:56], ael, ident[0:8, 0:8])
            for j in range(4):
                s = sel[:, (8 + j) * 128:(9 + j) * 128]
                mm(ps[7][:, 64 + 64 * j:128 + 64 * j], s, atr[:, :], start=True, stop=True)
                last = mm(ps[7][:, 320 + 8 * j:328 + 8 * j], s, ael, start=True, stop=True)
            last.then_inc(s_colp, 1)
            for n in range(8):
                dense(8 * Q_V + n, XH, XL)
                if n >= 1:
                    pe.wait_ge(*((s_ev[0]), evac(8 * Q_V + n - 1)[1]))
                    if n >= 3:
                        pe.wait_ge(s_vc, n - 2)
                    turn3(ps[4 + (n - 1) % 2], FR[(n - 1) % 2]).then_inc(s_vt, 1)
            pe.wait_ge(s_ev[0], evac(8 * Q_V + 7)[1])
            pe.wait_ge(s_vc, 6)
            turn3(ps[4 + 7 % 2], FR[7 % 2]).then_inc(s_vt, 1)

            pe.wait_ge(s_ml, 32)
            pe.wait_ge(s_col, 1)
            for h in range(H):
                j, r = h // 2, slice(64 * (h % 2), 64 * (h % 2) + 64)
                hs = sel[:, 128 * h:128 * h + 128]
                S, MB, EM, DEN, NUM = ps[2], ps[3], ps[4], ps[5], ps[6]
                if h == 0:
                    pe.wait_ge(s_bc, 2)
                if h >= 1:
                    pe.wait_ge(s_W, h)
                mm(MB[:, 0:T], hs, R[2][:, :], start=True, stop=True)
                mm(S[:, 0:256], kT[r, j, 0:128], qT[r, j, 0:256], start=True, stop=True)
                mm(S[:, 256:384], kT[r, j, 128:256], qT[r, j, 128:256], start=True, stop=True)
                mm(S[0:64, 384:448], kT[r, j, 256:320], qT[r, j, 256:320], start=True, stop=True).then_inc(s_sp, 1)
                dense(8 * Q_O + h, XH, XL)
                if h == 0:
                    pe.wait_ge(s_vc, 8)
                    pe.wait_ge(s_c0, 16 * 8)
                if h >= 1:
                    pe.wait_ge(s_emc, h)
                mm(EM[:, 0:T], hs, R[1][:, :], start=True, stop=True).then_inc(s_emp, 1)
                if h >= 1:
                    pe.wait_ge(s_hg, h)
                w = W[h % 2]
                pe.wait_ge(s_W, h + 1)
                c = slice(128 * h, 128 * h + 128)
                for dst, v0, v1, v2 in ((NUM, VT[:, 0, c], VT[:, 1, c], VT[:, 2, c]), (DEN, ones, ones, ones)):
                    mm(dst[:, 0:256], v0, w[:, 0:256], start=True, stop=True)
                    mm(dst[:, 128:256], v1, w[:, 256:384], start=False, stop=True, skip_group_check=True)
                    mm(dst[:, 256:320], v2, w[:, 384:448], start=False, stop=True, skip_group_check=True)
                for b in range(NB):
                    mm(NUM[:, 256 + 8 * b:264 + 8 * b], C0[r, j, b, :], aqT[r, j, 8 * b:8 * b + 8],
                       start=False, stop=True, skip_group_check=True)
                mm(DEN[:, 256:320], ones[r, :], an[r, j, :], start=False, stop=True, skip_group_check=True)\
                    .then_inc(s_num, 1)

            def state_step(i):
                if i < 4:
                    pe.wait_ge(s_num, H)
                    if i >= 1:
                        pe.wait_ge(s_wk, 2 * i)
                    turn3(ps[2], kT[:, i, :]).then_inc(s_kt, 1)
                if i == 4:
                    pe.wait_ge(s_wk, 8)
                    for h in range(H):
                        o = ps[3][64 * (h % 2):64 * (h % 2) + 64, 128 * (h // 2):128 * (h // 2) + 128]
                        for q in range(2):
                            mm(o, wsK[:, q, 64 * h:64 * h + 64], VT[:, q, 128 * h:128 * h + 128],
                               start=(q == 0), stop=(q == 1), skip_group_check=True)
                    for q in range(2):
                        mm(ps[4][0:1, :], ones[:, 0:1], wsK[:, q, :], start=(q == 0), stop=(q == 1))
                    mm(ps[5][0:8, :], bmask[0:64, :], wsK[0:64, 2, :], start=True, stop=True).then_inc(s_np, 1)
                if 4 <= i < 8:
                    j = i - 4
                    pe.wait_ge(s_km, j + 1)
                    for half in range(2):
                        bank = ps[6 + half]
                        if j >= 1:
                            pe.wait_ge(s_cadd, 2 * j - 1 + half)
                        for bb in range(4):
                            b = 4 * half + bb
                            for h2 in range(2):
                                h = 2 * j + h2
                                last = mm(bank[64 * h2:64 * h2 + 64, 128 * bb:128 * bb + 128],
                                          wsKm[:, b, 64 * h2:64 * h2 + 64], VT[0:64, 2, 128 * h:128 * h + 128],
                                          start=True, stop=True, skip_group_check=True)
                        last.then_inc(s_cp, 1)

            for n in range(8):
                dense(8 * Q_WOA + n, HH, HL, (lambda k: (s_hl, k + 1)) if n == 0 else None)
                state_step(n)

            def ln_stats(l):
                pe.wait_ge(s_st, l + 1)
                if l == 0:
                    pe.wait_ge(s_nadd, 2)
                mm(ps[2][:, 0:T], ones, A1[:, :], start=True, stop=True)
                mm(ps[3][:, 0:T], ones, A2[:, :], start=True, stop=True).then_inc(s_lnp, 1)

            def mlp(q0, xl0, hl0):
                up0, dn0 = 8 * q0, 8 * q0 + 8
                with pe.Fori(0, 4) as g:
                    for n in range(8):
                        dense(up0 + n, XH, XL, (lambda k: (s_xl, xl0 + k + 1)) if n == 0 else None, g, 8 * g)
                    for n in range(8):
                        t = dn0 + n
                        dense(t, HH, HL, (lambda k: (s_hl, hl0 + k + 1 + 8 * g)) if n == 0 else None, g, 8 * g)

            ln_stats(0)
            mlp(Q_MLP0, 8, 8)
            ln_stats(1)

            def kv_turn(i):
                n = i % 8
                if i < 8:
                    pe.wait_ge(s_ev[0], evac(8 * Q_WK + n)[1])
                    src = KA[:, n, :]
                else:
                    pe.wait_ge(s_ev[0], evac(8 * Q_WV + n)[1])
                    src = FR[n % 2]
                if i >= 2:
                    pe.wait_ge(*((s_tc, i - 1) if i < 10 else (s_tv, i - 9)))
                turn3(ps[4 + i % 2], src).then_inc(s_tp, 1)

            for n in range(8):
                dense(8 * Q_WK + n, XH, XL, (lambda k: (s_xl, 16 + k + 1)) if n == 0 else None)
                if n >= 1:
                    kv_turn(n - 1)
            for n in range(8):
                dense(8 * Q_WV + n, XH, XL)
                kv_turn(7 + n)

            def p_scores(h):
                if h >= 1:
                    pe.wait_ge(s_pmx, h)
                pe.wait_ge(s_ev[0], evac(8 * Q_WQ + h)[1])
                mm(ps[2][:, 0:128], QA[:, h, 0:128], KA[:, h, 0:128], start=True, stop=True)
                mm(ps[2][:, 128:384], QA[:, h, 128:256], KA[:, h, 0:256], start=True, stop=True).then_inc(s_pS, 1)

            def p_turn(h):
                pe.wait_ge(s_pnm, 2 * h + 2)
                if h >= 1:
                    pe.wait_ge(s_pTc, h)
                pl = PL[h % 2]
                nc.tensor.transpose(ps[3][:, 0:128], pl[:, 0:128], ident)
                nc.tensor.transpose(ps[3][:, 128:256], pl[:, 128:256], ident)
                nc.tensor.transpose(ps[3][:, 256:384], pl[:, 256:384], ident).then_inc(s_pT, 1)

            def p_out(h):
                pe.wait_ge(s_pTc, h + 1)
                pe.wait_ge(s_tv, 8)
                if h >= 1:
                    pe.wait_ge(s_pA, h)
                c = slice(128 * h, 128 * h + 128)
                mm(ps[6][:, 0:256], VT[:, 0, c], PTt[h % 2][:, 0:256], start=True, stop=True)
                mm(ps[6][:, 128:256], VT[:, 1, c], PTt[h % 2][:, 256:384], start=False, stop=True,
                   skip_group_check=True).then_inc(s_pV, 1)

            def p_step(i):
                if 0 <= i - 2 < H:
                    p_out(i - 2)
                if 0 <= i - 1 < H:
                    p_turn(i - 1)
                if 0 <= i < H:
                    p_scores(i)

            for n in range(8):
                dense(8 * Q_WQ + n, XH, XL)
                if n == 0:
                    kv_turn(15)
                p_step(n - 1)
            pe.wait_ge(s_ev[0], evac(8 * Q_WQ + 7)[1])
            for h in range(H):
                last = mm(ps[7][0:64, 64 * h:64 * h + 64], KA[:, h, 256:320], QA[:, h, 256:320], start=True, stop=True)
            last.then_inc(s_own, 1)
            for i in range(7, 10):
                p_step(i)
            pe.wait_ge(s_pA, H)

            def k_page(b, p, extra=None):
                g = 8 * b + p
                if p < 8:
                    pe.wait_ge(s_k[p % 4], 16 * (2 * b + p // 4 + 1))
                    if not (isinstance(b, int) and g < 2):
                        pe.wait_ge(s_kte, 2 * (g - 2) + 2)
                    for h in range(H):
                        last = nc.tensor.transpose(ps[2 * (p % 2) + h // 4][:, 128 * (h % 4):128 * (h % 4) + 128],
                                                   Kp[p % 4][:, 128 * h:128 * h + 128], ident)
                    last.then_inc(s_ktr, 1)
                if p >= 1:
                    q = p - 1
                    pe.wait_ge(s_kte, 2 * (g - 1) + 2)
                    if q == 0:
                        pe.wait_ge(s_qb, b + 1)
                        if not isinstance(b, int):
                            pe.wait_ge(s_sl, b)
                    for h in range(H):
                        last = mm(ps[4][:, 64 * h + 8 * q:64 * h + 8 * q + 8], KT[q % 2][:, h, :],
                                  QB[:, 8 * h:8 * h + 8], start=True, stop=True)
                    last.then_inc(s_sc, 1)

            def page_sums(b):
                pe.wait_ge(s_sl, b + 1)
                mm(ps[5][:, :], ones, SL[:, :], start=True, stop=True).then_inc(s_pg, 1)

            def max_turn(b):
                pe.wait_ge(s_mx, b + 1)
                nc.tensor.transpose(ps[6][:, 0:128], s64[:, 0:128], ident).then_inc(s_mtr, 1)

            def max_cast(b):
                pe.wait_ge(s_dg, b + 1)
                mm(ps[6][:, 128:192], ones[0:64, :], dg[0:64, :], start=True, stop=True).then_inc(s_mb, 1)

            def values(b):
                pe.wait_ge(s_pe, 2 * b + 2)
                O = ps[7]
                for h in range(H):
                    mm(O[:, 8 * h:8 * h + 8], VT[0:64, 2, 128 * h:128 * h + 128], PO[0:64, 8 * h:8 * h + 8],
                       start=(h == 0), stop=True, skip_group_check=True)
                pe.wait_ge(s_psum, b + 1)
                mm(ps[6][:, 192:256], ones, Ps, start=True, stop=False)
                mm(ps[6][:, 192:256], ones[0:64, :], PO[0:64, :], start=False, stop=True).then_inc(s_den, 1)
                for p in range(8):
                    pe.wait_ge(s_v_[p % 4], 16 * (2 * b + p // 4 + 1))
                    for h in range(H):
                        last = mm(O[:, 8 * h:8 * h + 8], Vp[p % 4][:, 128 * h:128 * h + 128],
                                  P[:, 64 * h + 8 * p:64 * h + 8 * p + 8], start=False, stop=True,
                                  skip_group_check=True)
                    last.then_inc(s_pv, 1)

            for p in range(9):
                k_page(0, p)
            with pe.Fori(0, NB - 1) as i:
                for p in range(9):
                    k_page(i + 1, p)
                    if p == 0:
                        page_sums(i)
                    if p == 4:
                        max_turn(i)
                    if p == 6:
                        max_cast(i)
                values(i)
            page_sums(NB - 1)
            max_turn(NB - 1)
            max_cast(NB - 1)
            values(NB - 1)
            for n in range(8):
                dense(8 * Q_WOB + n, XH, XL, (lambda k: (s_xl, 24 + k + 1)) if n == 0 else None)
            ln_stats(2)
            mlp(Q_MLP1, 32, 40)
            ln_stats(3)
            for n in range(8):
                pe.wait_ge(s_F, 24 + n + 1)
                if n >= 2:
                    pe.wait_ge(s_tc, 8 + n - 1)
                turn3(ps[4 + n % 2], X[:, n, :]).then_inc(s_tp, 1)

        @block.scalar
        def _(act):
            A = nc.scalar.activation
            own = Own(act, s_a)

            def split(t, turn=0):
                u = t // 2
                if t % 2 == 0:
                    act.wait_ge(s_raw[u % RAW], 16 * (u // RAW + 1) + 32 * turn)
                if t >= SPL:
                    act.wait_ge(s_mm, t - SPL + 1 + 16 * turn)
                A(WH[t % SPL][:, :, :], raw[u % RAW][:, :, 128 * (t % 2):128 * (t % 2) + 128], ACT.Copy)\
                    .then_inc(s_hi, 1)

            def tile(t, turn=0):
                act.wait_ge(s_mm, t + 1 + 16 * turn)
                return ps[t % 2][:, 0:T]

            act.wait_ge(s_gw, 16)
            act.wait_ge(s_gz, 1)
            A(WGH[:, :, 0:8], wgraw[:, :, 0:8], ACT.Copy)
            A(WGH[:, :, 32:40], wgraw[:, :, 8:16], ACT.Copy).then_inc(s_gh, 1)
            for n in range(8):
                act.wait_ge(s_xf, n + 1)
                A(XH[:, n, :], X[:, n, :], ACT.Copy).then_inc(s_xh, 1)
                if n < 4:
                    split(n)
            def rows_log():
                act.wait_ge(s_gabs, 1)
                own(A(R[2][:, :], R[2][:, :], ACT.Exp, scale=-1.0))
                A(R[2][:, :], R[2][:, :], ACT.Ln, bias=1.0).then_inc(s_gln, 1)

            def rows_exp():
                act.wait_ge(s_mt, 1)
                A(R[1][:, :], R[1][:, :], ACT.Exp, scale=-1.0).then_inc(s_emn, 1)
                act.wait_ge(s_wsl, 1)
                A(R[5][:, :], R[5][:, :], ACT.Exp).then_inc(s_ws, 1)
                act.wait_ge(s_al, 2)
                A(atr[:, :], atr[:, :], ACT.Exp).then_inc(s_aex, 1)
                A(ael, ael, ACT.Exp).then_inc(s_aex, 1)

            for n in range(8):
                t = 8 * Q_QK + n
                if n == 0:
                    rows_log()
                if n == 2:
                    rows_exp()
                if n < 4:
                    A(qT[:, n, :], tile(t), ACT.Copy).then_inc(s_ev[0], 1)
                else:
                    A(kT[:, n - 4, :], tile(t), ACT.Copy, scale=DK ** -0.5).then_inc(s_ev[0], 1)
                split(t + 4)
            for n in range(8):
                t = 8 * Q_V + n
                o = tile(t)
                if n >= 2:
                    act.wait_ge(s_vt, n - 1)
                A(FR[n % 2][:, :], o, ACT.Copy).then_inc(s_ev[0], 1)
                split(t + 4)

            def h_rounded(h):
                act.wait_ge(s_hg, h + 1)
                A(HH[:, h, :], hg[:, :], ACT.Copy).then_inc(s_hh, 1)

            for h in range(H):
                t = 8 * Q_O + h
                act.wait_ge(s_D, h + 1)
                e = E[h % 2]
                A(e[:, 0:256], e[:, 0:256], ACT.Exp, bias=cols[:, h:h + 1], scale=-1.0)
                A(e[:, 256:384], e[:, 256:384], ACT.Exp, bias=cols[:, 8 + h:9 + h], scale=-1.0)
                A(e[0:64, 384:448], e[0:64, 384:448], ACT.Exp, bias=cols[0:64, 16 + h:17 + h], scale=-1.0)\
                    .then_inc(s_E, 1)
                if h >= 1:
                    h_rounded(h - 1)
                o = tile(t)
                if h >= 2:
                    act.wait_ge(s_hg, h - 1)
                A(eo[h % 2][:, :], o, ACT.Exp, scale=-1.0).then_inc(s_ev[0], 1)
                act.wait_ge(s_emp, h + 1)
                if h >= 1:
                    act.wait_ge(s_hg, h)
                A(emS[:, :], ps[4][:, 0:T], ACT.Copy).then_inc(s_emc, 1)
                split(t + 4)
            h_rounded(H - 1)
            outs = [0]

            def store(dst, src):
                act.dma_start(dst, src, allow_slow_non_contiguous=True).then_inc(s_out, 16)
                outs[0] += 1

            for n in range(8):
                t = 8 * Q_WOA + n
                split(t + 4)
                if n == 5:
                    act.wait_ge(s_np, 1)
                    A(npr[:, :], ps[4][0:1, :], ACT.Copy)
                    A(Wst[:, :], ps[3][:, :], ACT.Copy).then_inc(s_nadd, 1)
                    act.wait_ge(s_nadd, 2)
                    for h2 in range(2):
                        act.dma_start(p_C[0, 0].rearrange("(j t) k v -> t k j v", t=2)[h2],
                                      Wst[64 * h2:64 * h2 + 64, :].rearrange("p (j v) -> p j v", j=4)).then_inc(s_po, 16)
                    act.dma_start(p_n[0, 0].rearrange("h k -> (h k)").unsqueeze(0), npr[:, :]).then_inc(s_po, 16)
                    act.dma_start(s_n[0].rearrange("b h k -> b (h k)"), nout[:, :]).then_inc(s_po, 16)
                if n == 2:
                    act.wait_ge(s_nm, 1)
                    store(p_m[0, 0:1, :].rearrange("a h -> h a"), mnew[:, 0:1])
                    store(s_m[0].rearrange("b h -> h b"), mnew[:, 1:9])
            for j in range(4):
                act.wait_ge(s_cadd, 2 * j + 2)
                for h2 in range(2):
                    act.dma_start(s_C[0, :, 2 * j + h2].rearrange("b k v -> k b v"),
                                  C0[64 * h2:64 * h2 + 64, j, :, :]).then_inc(s_co, 16)

            def ln(l, last=False):
                act.wait_ge(s_var, l + 1)
                own(A(rs[:, :], var[:, :], ACT.Ln))
                A(rs[:, :], rs[:, :], ACT.Exp, scale=-0.5).then_inc(s_rs, 1)
                for n in range(8):
                    if n % 2 == 0:
                        act.wait_ge(s_t, 4 * l + n // 2 + 1)
                    g, b = lnT[:, 8 * l + n:8 * l + n + 1], lnT[:, 32 + 8 * l + n:33 + 8 * l + n]
                    src = LT[(n // 2) % 2][:, n % 2, :]
                    if last:
                        A(X[:, n, :], src, ACT.Identity, bias=b, scale=g).then_inc(s_F, 1)
                    else:
                        A(XH[:, n, :], src, ACT.Identity, bias=b, scale=g).then_inc(s_xh, 1)
                        if n >= 2:
                            act.wait_ge(s_al2, 8 * l + n - 1)
                            act.wait_ge(s_xl, (8, 16, 32)[l] + n - 1)
                        A(FR[n % 2][:, :], src, ACT.Identity, bias=b, scale=g).then_inc(s_F, 1)

            def mlp(q0):
                with act.Fori(0, 4) as g:
                    mlp_round(8 * q0, q0, g, 8)

            def mlp_last(q0):
                with act.Fori(0, 3) as g:
                    mlp_round(8 * q0, q0, g, 8)
                mlp_round(8 * q0, q0, 3, 4)

            def mlp_round(up0, q0, g, splits):
                sq0 = 8 * UPS.index(q0)
                for n in range(8):
                    t = up0 + n
                    o = tile(t, g)
                    if n >= 2:
                        act.wait_ge(s_sq, (sq0 + n - 1) + 8 * g)
                    A(FR[n % 2][:, :], o, ACT.Relu).then_inc(s_ev[0], 1)
                    split(t + 4, g)
                    act.wait_ge(s_sq, sq0 + n + 1 + 8 * g)
                    A(HH[:, n, :], FS[n % 2][:, :], ACT.Copy).then_inc(s_hh, 1)
                for n in range(splits):
                    split(up0 + 8 + n + 4, g)

            ln(0)
            act.wait_ge(s_al2, 8)
            mlp(Q_MLP0)
            ln(1)
            act.wait_ge(s_al2, 16)
            act.wait_ge(s_po, 16 * 4)
            act.wait_ge(s_out, 16 * outs[0])

            def kv_out(i):
                act.wait_ge(s_tp, i + 1)
                if i >= 2:
                    act.wait_ge(s_to[i % 2], 32 * (i // 2))
                A(KO[i % 2][:, 0:2, :], ps[4 + i % 2][:, 0:256].rearrange("p (t c) -> p t c", t=2), ACT.Copy)
                A(KO[i % 2][0:64, 2, :], ps[4 + i % 2][0:64, 256:384], ACT.Copy).then_inc(s_tc, 1)
                act.wait_ge(s_tc, i + 1)
                act.dma_start(p_k[0, :, i, :].rearrange("(t p) d -> p t d", p=128), KO[i % 2][:, 0:2, :])\
                    .then_inc(s_to[i % 2], 16)
                act.dma_start(s_k_rows[:, i, :], KO[i % 2][0:64, 2, :]).then_inc(s_to[i % 2], 16)

            s_k_rows = s_k_d.rearrange("b t h d -> (b t) h d")
            for n in range(8):
                t = 8 * Q_WK + n
                A(KA[:, n, :], tile(t), ACT.Copy).then_inc(s_ev[0], 1)
                split(t + 4)
                if n >= 1:
                    kv_out(n - 1)
            for n in range(8):
                t = 8 * Q_WV + n
                o = tile(t)
                if n >= 2:
                    act.wait_ge(s_tp, 8 + n - 1)
                A(FR[n % 2][:, :], o, ACT.Copy).then_inc(s_ev[0], 1)
                split(t + 4)
                if n == 0:
                    kv_out(7)

            def p_exp(h):
                act.wait_ge(s_pmx, h + 1)
                pl, st = PL[h % 2], pst[:, 8 * h:8 * h + 8]
                A(pl[:, 0:128], pl[:, 0:128], ACT.Exp, bias=st[:, 0:1], accum_out=st[:, 2:3])
                A(pl[:, 128:384], pl[:, 128:384], ACT.Exp, bias=st[:, 1:2], accum_out=st[:, 3:4]).then_inc(s_pex, 1)

            def p_copy(h):
                act.wait_ge(s_pT, h + 1)
                if h >= 2:
                    act.wait_ge(s_pV, h - 1)
                A(PTt[h % 2][:, :], ps[3][:, 0:384], ACT.Copy).then_inc(s_pTc, 1)

            def p_step(i):
                if 0 <= i - 2 < H:
                    act.wait_ge(s_pV, i - 2 + 1)
                    A(AT[:, i - 2, :], ps[6][:, 0:256], ACT.Copy).then_inc(s_pA, 1)
                if 0 <= i - 1 < H:
                    p_copy(i - 1)
                if 0 <= i < H:
                    p_exp(i)

            for n in range(8):
                t = 8 * Q_WQ + n
                A(QA[:, n, :], tile(t), ACT.Copy, scale=QSCALE).then_inc(s_ev[0], 1)
                split(t + 4)
                p_step(n - 1)
                if n == 3:
                    act.wait_ge(s_tv, 8)
                    store(p_v[0].rearrange("(t p) h d -> p t (h d)", p=128), VT[:, 0:2, :])
                    store(s_v_d.rearrange("b t h d -> (b t) (h d)"), VT[0:64, 2, :])
            for i in range(7, 10):
                p_step(i)

            def q_batch(b):
                if not isinstance(b, int):
                    act.wait_ge(s_sc, 8 * b)
                A(QB.rearrange("p (h q) -> p h q", h=8), QA[:, :, bass.ds(TP + 8 * b, 8)], ACT.Copy).then_inc(s_qb, 1)

            def k_copy(b, p):
                g = 8 * b + p
                act.wait_ge(s_ktr, g + 1)
                if not (isinstance(b, int) and p < 2):
                    act.wait_ge(s_sc, g - 1)
                for half in range(2):
                    A(KT[p % 2][:, 4 * half:4 * half + 4, :],
                      ps[2 * (p % 2) + half][:, :].rearrange("p (h t) -> p h t", h=4), ACT.Copy).then_inc(s_kte, 1)

            def probs(b):
                act.wait_ge(s_l3, 2 * b + 2)
                A(P[:, :], L[:, :], ACT.Exp).then_inc(s_pe, 1)
                A(PO[0:64, :], PO[0:64, :], ACT.Exp).then_inc(s_pe, 1)

            q_batch(0)
            for p in range(8):
                k_copy(0, p)
            with act.Fori(0, NB - 1) as i:
                for p in range(8):
                    k_copy(i + 1, p)
                    if p == 0:
                        q_batch(i + 1)
                probs(i)
            probs(NB - 1)
            act.wait_ge(s_ao, NB)
            for n in range(8):
                A(XH[:, n, 0:TP], AT[:, n, :], ACT.Copy)
                A(XH[:, n, TP:T], AO[:, n, :], ACT.Copy).then_inc(s_xh, 1)
            for n in range(8):
                split(8 * Q_WOB + n + 4)
            ln(2)
            act.wait_ge(s_al2, 24)
            mlp_last(Q_MLP1)
            ln(3, True)
            ys = y_sample.rearrange("b t c -> (b t) c")
            for n in range(8):
                i = 16 + n
                act.wait_ge(s_tp, i + 1)
                act.wait_ge(s_to[n % 2], 32 * 4 + 32 * (n // 2))
                A(KO[n % 2][:, 0:2, :], ps[4 + n % 2][:, 0:256].rearrange("p (t c) -> p t c", t=2), ACT.Copy)
                A(KO[n % 2][0:64, 2, :], ps[4 + n % 2][0:64, 256:384], ACT.Copy).then_inc(s_tc, 1)
                act.wait_ge(s_tc, 8 + n + 1)
                act.dma_start(y_prompt[0, :, 128 * n:128 * n + 128].rearrange("(t p) d -> p t d", p=128),
                              KO[n % 2][:, 0:2, :]).then_inc(s_to[n % 2], 16)
                act.dma_start(ys[:, 128 * n:128 * n + 128], KO[n % 2][0:64, 2, :]).then_inc(s_to[n % 2], 16)
            for i in range(2):
                act.wait_ge(s_to[i], 32 * 8)
            act.wait_ge(s_out, 16 * outs[0])

        @block.vector
        def _(dve):
            V = nc.vector
            own = Own(dve, s_d)

            def split(t, turn=0):
                dve.wait_ge(s_hi, t + 1 + 16 * turn)
                V.tensor_tensor(WL[t % SPL][:, :, :], raw[(t // 2) % RAW][:, :, 128 * (t % 2):128 * (t % 2) + 128],
                                WH[t % SPL][:, :, :].bitcast(F32), ALU.subtract).then_inc(s_lo, 1)

            V.memset(VT[64:128, 2, :], 0.0)
            V.memset(WGH[:, :, :].bitcast(F32), 0.0)
            V.memset(WGL[:, :, :].bitcast(F32), 0.0).then_inc(s_gz, 1)
            for n in range(8):
                dve.wait_ge(s_xt, n + 1)
                V.tensor_copy(X[:, n, :], ps[2 + n % 2][:, 0:T]).then_inc(s_xf, 1)
                dve.wait_ge(s_xf, n + 1)
                dve.wait_ge(s_xh, n + 1)
                V.tensor_tensor(XL[:, n, :], X[:, n, :], XH[:, n, :].bitcast(F32), ALU.subtract).then_inc(s_xl, 1)
                if n == 3:
                    dve.wait_ge(s_gh, 1)
                    dve.wait_ge(s_gz, 1)
                    V.tensor_tensor(WGL[:, :, 0:8], wgraw[:, :, 0:8], WGH[:, :, 0:8].bitcast(F32), ALU.subtract)
                    V.tensor_tensor(WGL[:, :, 32:40], wgraw[:, :, 8:16], WGH[:, :, 32:40].bitcast(F32),
                                    ALU.subtract).then_inc(s_gl, 1)
            for t in range(3):
                split(t)
            dve.wait_ge(s_lnt, 1)
            V.tensor_copy(lnT[:, :], ps[4][:, 0:64]).then_inc(s_lnc, 1)

            dve.wait_ge(s_gp, 1)
            for w in W:
                V.memset(w[64:128, 384:448], 0.0)
            dve.wait_ge(s_m0, 48)
            dve.wait_ge(s_ml, 32)
            ends = slice(TP + LS - 1, T, LS)
            starts = slice(TP, T, LS)
            V.tensor_scalar(R[0][:, :], ps[5][0:8, 0:T], bg[0:8, 0:1], None, ALU.add)
            own(V.tensor_scalar(R[1][:, :], ps[5][32:40, 0:T], bg[32:40, 0:1], None, ALU.add))
            V.scalar_tensor_tensor(R[2][:, :], R[1][:, :], -1.0, R[1][:, :], ALU.mult, ALU.max).then_inc(s_gabs, 1)
            dve.wait_ge(s_gln, 1)
            own(V.scalar_tensor_tensor(R[1][:, :], R[1][:, :], 0.0, R[2][:, :], ALU.min, ALU.subtract))
            rst, neg = cml[0:8, 448:448 + T], cml[0:8, 448 + T:448 + 2 * T]
            own(V.tensor_tensor_scan(R[3][:, :], rst, R[1][:, :], 0.0, ALU.mult, ALU.add))
            own(V.tensor_tensor(R[4][:, :], R[0][:, :], R[3][:, :], ALU.subtract))
            own(V.tensor_copy(R[0][:, :], R[4][:, :]))
            V.tensor_scalar(R[0][:, 0:1], R[4][:, 0:1], 0.0, None, ALU.max)
            own(V.tensor_tensor(R[0][:, starts], R[4][:, starts], m0, ALU.max))
            own(V.tensor_tensor_scan(R[2][:, :], neg, R[0][:, :], 0.0, ALU.add, ALU.max))
            V.tensor_tensor(R[1][:, :], R[3][:, :], R[2][:, :], ALU.add).then_inc(s_mt, 1)
            V.tensor_scalar(R[5][:, 0:TP], R[4][:, 0:TP], R[2][:, TP - 1:TP], None, ALU.subtract)
            V.tensor_tensor(R[5][:, TP:T].rearrange("p (b t) -> p b t", t=LS),
                            R[4][:, TP:T].rearrange("p (b t) -> p b t", t=LS),
                            bcast(R[2][:, ends], 2, LS), ALU.subtract).then_inc(s_wsl, 1)
            V.tensor_tensor(atr[:, :].rearrange("p (b t) -> p b t", t=LS), bcast(m0, 2, LS),
                            R[2][:, TP:T].rearrange("p (b t) -> p b t", t=LS), ALU.subtract).then_inc(s_al, 1)
            V.tensor_tensor(ael, m0, R[2][:, ends], ALU.subtract).then_inc(s_al, 1)
            V.tensor_tensor(mnew[:, 0:1], R[3][:, TP - 1:TP], R[2][:, TP - 1:TP], ALU.add)
            V.tensor_tensor(mnew[:, 1:9], R[3][:, ends], R[2][:, ends], ALU.add).then_inc(s_nm, 1)

            for n in range(8):
                split(8 * Q_QK + n + 3)
            dve.wait_ge(s_colp, 1)
            c7 = ps[7]
            V.tensor_copy(cols[:, 0:16], c7[:, 0:16])
            V.tensor_copy(cols[0:64, 16:24], c7[0:64, 16:24])
            V.tensor_copy(cols[:, 24:40], c7[:, 24:40])
            V.tensor_copy(cols[0:64, 40:48], c7[0:64, 40:48])
            V.tensor_copy(cols[0:8, 48:56], c7[0:8, 48:56]).then_inc(s_col, 1)
            V.tensor_copy(aeP[:, :, :], c7[:, 320:352].rearrange("p (j b) -> p j b", j=4))
            dve.wait_ge(s_ev[0], evac(8 * Q_QK + 3)[1])
            V.tensor_tensor(aqT[:, :, :], qT[:, :, TP:T], c7[:, 64:320].rearrange("p (j t) -> p j t", j=4),
                            ALU.mult).then_inc(s_bc, 1)
            dve.wait_ge(s_bc, 1)
            V.tensor_tensor(an[:, :, :].rearrange("p j (b t) -> p (j b) t", t=LS),
                            aqT[:, :, :].rearrange("p j (b t) -> p (j b) t", t=LS),
                            bcast(c7[:, 352:384], 2, LS), ALU.mult).then_inc(s_bc, 1)

            def v_copy(n, done, bank):
                c = slice(128 * n, 128 * n + 128)
                V.tensor_copy(VT[:, 0:2, c], bank[:, 0:256].rearrange("p (t c) -> p t c", t=2))
                V.tensor_copy(VT[0:64, 2, c], bank[0:64, 256:384]).then_inc(done, 1)

            for n in range(8):
                split(8 * Q_V + n + 3)
                if n >= 1:
                    dve.wait_ge(s_vt, n)
                    v_copy(n - 1, s_vc, ps[4 + (n - 1) % 2])
            dve.wait_ge(s_vt, 8)
            v_copy(7, s_vc, ps[5])

            def decay(h):
                dve.wait_ge(s_sp, h + 1)
                e = E[h % 2]
                V.tensor_tensor(e[:, 0:256], ps[3][:, 0:256], cml[:, 0:256], ALU.add)
                V.tensor_tensor(e[:, 256:384], ps[3][:, 128:256], cml[:, 256:384], ALU.add)
                V.tensor_tensor(e[0:64, 384:448], ps[3][0:64, 256:320], cml[0:64, 384:448], ALU.add)\
                    .then_inc(s_D, 1)

            def weights(h):
                dve.wait_ge(s_E, h + 1)
                if h >= 2:
                    dve.wait_ge(s_num, h - 1)
                w, e = W[h % 2], E[h % 2]
                V.tensor_tensor(w[:, 0:384], ps[2][:, 0:384], e[:, 0:384], ALU.mult)
                V.tensor_tensor(w[0:64, 384:448], ps[2][0:64, 384:448], e[0:64, 384:448], ALU.mult)\
                    .then_inc(s_W, 1)

            def gated(h):
                dve.wait_ge(s_emc, h + 1)
                dve.wait_ge(s_num, h + 1)
                own(V.scalar_tensor_tensor(rec[:, :], ps[5][:, 0:T], -1.0, emS[:, :], ALU.mult, ALU.max))
                own(V.tensor_tensor(rec[:, :], ps[5][:, 0:T], rec[:, :], ALU.max))
                own(V.scalar_tensor_tensor(rec[:, :], eo[h % 2][:, :], 1.0, rec[:, :], ALU.add, ALU.mult))
                own(V.reciprocal(rec[:, :], rec[:, :]))
                if h >= 1:
                    dve.wait_ge(s_hh, h)
                V.tensor_tensor(hg[:, :], ps[6][:, 0:T], rec[:, :], ALU.mult).then_inc(s_hg, 1)

            def h_rest(h):
                dve.wait_ge(s_hh, h + 1)
                V.tensor_tensor(HL[:, h, :], hg[:, :], HH[:, h, :].bitcast(F32), ALU.subtract).then_inc(s_hl, 1)

            for h in range(H):
                decay(h)
                if h >= 1:
                    gated(h - 1)
                weights(h)
                if h >= 1:
                    h_rest(h - 1)
                split(8 * Q_O + h + 3)
            gated(H - 1)
            h_rest(H - 1)

            def residual(t, turn=0, scale=None):
                n = t % 8
                dve.wait_ge(s_mm, t + 1 + 16 * turn)
                if scale is None:
                    ins = V.tensor_tensor(X[:, n, :], X[:, n, :], ps[t % 2][:, 0:T], ALU.add)
                else:
                    ins = V.scalar_tensor_tensor(X[:, n, :], X[:, n, :], scale, ps[t % 2][:, 0:T], ALU.mult, ALU.add)
                ins.then_inc(s_ev[1], 1)

            def state(i):
                if i < 4:
                    dve.wait_ge(s_kt, i + 1)
                    for w, bt, lo in ((128, slice(0, 2), 24), (64, slice(2, 3), 40)):
                        nt = bt.stop - bt.start
                        V.tensor_tensor(
                            wsK[0:w, bt, 128 * i:128 * i + 128].rearrange("p t (h d) -> p t h d", h=2),
                            ps[2][0:w, 128 * bt.start:128 * bt.stop].rearrange("p (t h d) -> p t h d", t=nt, h=2),
                            bcast(cols[0:w, lo:lo + 8 * nt].rearrange("p (t h) -> p t h", t=nt)[:, :, 2 * i:2 * i + 2],
                                  3, 64), ALU.mult).then_inc(s_wk, 1)
                if i == 5:
                    dve.wait_ge(s_np, 1)
                    own(V.tensor_tensor(nout[:, :].rearrange("p (h k) -> p h k", h=8),
                                        n0[:, :].rearrange("p (h k) -> p h k", h=8),
                                        bcast(cols[0:8, 48:56], 2, DK), ALU.mult))
                    V.tensor_tensor(nout[:, :], nout[:, :], ps[5][0:8, :], ALU.add).then_inc(s_nadd, 1)
                if i >= 5:
                    c_add(i - 5)

            def c_add(j):
                dve.wait_ge(s_cae, 4)
                for half in range(2):
                    dve.wait_ge(s_cp, 2 * j + half + 1)
                    c = C0[:, j, 4 * half:4 * half + 4, :]
                    V.tensor_tensor(c, c, ps[6 + half][:, :].rearrange("p (b v) -> p b v", b=4), ALU.add)\
                        .then_inc(s_cadd, 1)

            for n in range(8):
                residual(8 * Q_WOA + n, 0, ALPHA)
                split(8 * Q_WOA + n + 3)
                state(n)
            c_add(3)

            def ln(l, last=False):
                dve.wait_ge(s_lnp, l + 1)
                if l == 0:
                    dve.wait_ge(s_po, 16 * 4)
                own(V.tensor_scalar(mu[:, :], ps[2][:, 0:T], 1.0 / DM, None, ALU.mult))
                own(V.tensor_tensor(tmp[:, :], mu[:, :], mu[:, :], ALU.mult))
                own(V.scalar_tensor_tensor(var[:, :], ps[3][:, 0:T], 1.0 / DM, tmp[:, :], ALU.mult, ALU.subtract))
                V.tensor_scalar(var[:, :], var[:, :], 0.0, EPS, ALU.max, ALU.add).then_inc(s_var, 1)
                dve.wait_ge(s_rs, l + 1)
                own(V.scalar_tensor_tensor(tmp[:, :], rs[:, :], -0.5, var[:, :], ALU.mult, ALU.mult))
                own(V.tensor_tensor(tmp[:, :], tmp[:, :], rs[:, :], ALU.mult))
                own(V.scalar_tensor_tensor(rs[:, :], tmp[:, :], 1.5, rs[:, :], ALU.add, ALU.mult))

                def rest(n):
                    dve.wait_ge(s_F, 8 * l + n + 1)
                    V.tensor_tensor(XL[:, n, :], FR[n % 2][:, :], XH[:, n, :].bitcast(F32), ALU.subtract)\
                        .then_inc(s_xl, 1)

                for m in range(4):
                    if m >= 2:
                        dve.wait_ge(s_F, 8 * l + 2 * m - 2)
                    own(V.tensor_tensor(LT[m % 2][:, :, :], X[:, 2 * m:2 * m + 2, :], bcast(mu[:, :], 1, 2),
                                        ALU.subtract))
                    V.tensor_tensor(LT[m % 2][:, :, :], LT[m % 2][:, :, :], bcast(rs[:, :], 1, 2), ALU.mult)\
                        .then_inc(s_t, 1)
                    if m >= 1 and not last:
                        rest(2 * m - 2)
                        rest(2 * m - 1)
                if not last:
                    rest(6)
                    rest(7)
                    dve.wait_ge(s_al2, 8 * l + 8)

            def mlp_round(q0, g, splits):
                c0 = 8 * UPS.index(q0)
                for n in range(8):
                    t = 8 * q0 + n
                    dve.wait_ge(s_ev[0], evac(t)[1] + 8 * g)
                    if n >= 2:
                        dve.wait_ge(s_hh, 8 + c0 + n - 1 + 8 * g)
                    V.tensor_tensor(FS[n % 2][:, :], FR[n % 2][:, :], FR[n % 2][:, :], ALU.mult).then_inc(s_sq, 1)
                    split(t + 3, g)
                    dve.wait_ge(s_hh, 8 + c0 + n + 1 + 8 * g)
                    V.tensor_tensor(HL[:, n, :], FS[n % 2][:, :], HH[:, n, :].bitcast(F32), ALU.subtract)\
                        .then_inc(s_hl, 1)
                for n in range(8):
                    residual(8 * q0 + 8 + n, g)
                    if n < splits:
                        split(8 * q0 + 8 + n + 3, g)

            ln(0)
            with dve.Fori(0, 4) as g:
                mlp_round(Q_MLP0, g, 8)
            ln(1)
            for n in range(8):
                split(8 * Q_WK + n + 3)
            for n in range(8):
                split(8 * Q_WV + n + 3)
                if n >= 1:
                    dve.wait_ge(s_tp, 8 + n)
                    v_copy(n - 1, s_tv, ps[4 + (n - 1) % 2])
            dve.wait_ge(s_at, 16)

            def p_max(h):
                dve.wait_ge(s_pS, h + 1)
                if h >= 2:
                    dve.wait_ge(s_pT, h - 1)
                pl, st = PL[h % 2], pst[:, 8 * h:8 * h + 8]
                own(V.scalar_tensor_tensor(pl[:, :], dist, SLOPES[h], ps[2][:, 0:384], ALU.mult, ALU.add))
                V.tensor_reduce(st[:, 0:1], pl[:, 0:128], AX.X, ALU.max, negate=True)
                V.tensor_reduce(st[:, 1:2], pl[:, 128:384], AX.X, ALU.max, negate=True).then_inc(s_pmx, 1)

            def p_norm(h):
                dve.wait_ge(s_pex, h + 1)
                pl, st = PL[h % 2], pst[:, 8 * h:8 * h + 8]
                own(V.reciprocal(st[:, 4:6], st[:, 2:4]))
                V.tensor_scalar(pl[:, 0:128], pl[:, 0:128], st[:, 4:5], None, ALU.mult).then_inc(s_pnm, 1)
                V.tensor_scalar(pl[:, 128:384], pl[:, 128:384], st[:, 5:6], None, ALU.mult).then_inc(s_pnm, 1)

            def p_step(i):
                if 0 <= i < H:
                    p_max(i)
                if 0 <= i < H:
                    p_norm(i)

            for n in range(8):
                split(8 * Q_WQ + n + 3)
                if n == 0:
                    dve.wait_ge(s_tp, 16)
                    v_copy(7, s_tv, ps[5])
                p_step(n - 1)
            dve.wait_ge(s_own, 1)
            V.tensor_tensor(LO[:, :], ps[7][0:64, :], bias_own, ALU.add).then_inc(s_lo_, 1)
            for i in range(7, 10):
                p_step(i)
            dve.wait_ge(s_lo_, 1)
            LINKS = 11

            def own_logits(b):
                return LO[:, :].rearrange("p (h b q) -> p h b q", h=8, b=8)[:, :, bass.ds(b, 1), :]\
                    if not isinstance(b, int) else LO[:, :].rearrange("p (h b q) -> p h b q", h=8, b=8)[:, :, b:b + 1, :]

            def chain(b, own_at):
                own.n, own.shift = own_at, (LINKS * b if not isinstance(b, int) else LINKS * b)
                hnq = "p (h n q) -> p h n q"
                v4 = lambda x: x.rearrange("p (h a q) -> p h a q", h=8, q=8)
                h1q = lambda x: x.rearrange("p (h a q) -> p h a q", h=8, a=1)
                dve.wait_ge(s_sc, 8 * b + 8)
                V.tensor_copy(SL[:, :], ps[4][:, :]).then_inc(s_sl, 1)
                dve.wait_ge(s_sl, b + 1)
                V.tensor_tensor(L[:, :], SL[:, :], bias_past, ALU.add)
                dve.wait_ge(s_pg, b + 1)
                own(V.tensor_reduce(bsum.rearrange("p (m q) -> p m q", q=8),
                                    ps[5][:, :].rearrange("p (m t q) -> p m q t", t=2, q=8), AX.X, ALU.add))
                own(V.tensor_reduce(mn.rearrange("p (h q) -> p h q", h=8),
                                    bsum.rearrange("p (h n q) -> p h q n", h=8, n=4), AX.X, ALU.min))
                own(V.tensor_tensor(v4(eqs), v4(bsum), h1q(mn).to_broadcast([128, 8, 4, 8]), ALU.is_le))
                own(V.tensor_tensor(eqs, eqs, nidx, ALU.mult))
                own(V.tensor_reduce(ix.rearrange("p (h q) -> p h q", h=8),
                                    eqs.rearrange("p (h n q) -> p h q n", h=8, n=4), AX.X, ALU.max))
                own(V.tensor_tensor(v4(eqs), v4(nidx), h1q(ix).to_broadcast([128, 8, 4, 8]), ALU.is_equal))
                for t in range(2):
                    half = L[:, :].rearrange("p (m t q) -> p m t q", t=2, q=8)[:, :, t, :]
                    ins = V.scalar_tensor_tensor(half, eqs.rearrange("p (m q) -> p m q", q=8), -BIG, half,
                                                 ALU.mult, ALU.add)
                own(ins)
                own(V.tensor_reduce(Mx.rearrange("p (h q) -> p h q", h=8),
                                    L[:, :].rearrange("p (h a q) -> p h q a", h=8, q=8), AX.X, ALU.max))
                V.tensor_tensor(h1q(Mx[0:64, :]), h1q(Mx[0:64, :]), own_logits(b), ALU.max).then_inc(s_mx, 1)
                dve.wait_ge(s_mtr, b + 1)
                own(V.tensor_reduce(mcol[:, 0:1], ps[6][0:64, 0:128], AX.X, ALU.max))
                V.tensor_scalar(dg[0:64, :], ident[0:64, 0:64], mcol[:, 0:1], None, ALU.mult).then_inc(s_dg, 1)
                dve.wait_ge(s_mb, b + 1)
                mb = ps[6][:, 128:192]
                V.tensor_tensor(v4(L[:, :]), v4(L[:, :]), h1q(mb).to_broadcast([128, 8, 8, 8]), ALU.subtract)\
                    .then_inc(s_l3, 1)
                V.tensor_tensor(h1q(PO[0:64, :]), own_logits(b), h1q(mb[0:64, :]), ALU.subtract).then_inc(s_l3, 1)
                dve.wait_ge(s_pe, 2 * b + 2)
                V.tensor_reduce(Ps.rearrange("p (h q) -> p h q", h=8),
                                P[:, :].rearrange("p (h a q) -> p h q a", h=8, q=8), AX.X, ALU.add).then_inc(s_psum, 1)
                dve.wait_ge(s_den, b + 1)
                own(V.reciprocal(rc, ps[6][:, 192:256]))
                dve.wait_ge(s_pv, 8 * b + 8)
                dst = AO[:, :, :].rearrange("p h (b q) -> p h b q", q=8)
                dst = dst[:, :, b:b + 1, :] if isinstance(b, int) else dst[:, :, bass.ds(b, 1), :]
                own(V.tensor_tensor(dst, h1q(ps[7][:, 0:64]), h1q(rc), ALU.mult))

            before = own.n
            with dve.Fori(0, NB - 1) as i:
                chain(i, before)
                assert own.n - before == LINKS, own.n - before
            chain(NB - 1, before)
            V.tensor_copy(mcol[:, 1:2], mcol[:, 0:1]).then_inc(s_ao, NB)
            own.n, own.shift = before + LINKS * NB, 0
            for n in range(8):
                dve.wait_ge(s_xh, 8 * 3 + n + 1)
                V.tensor_tensor(XL[:, n, 0:TP], AT[:, n, :], XH[:, n, 0:TP].bitcast(F32), ALU.subtract)
                V.tensor_tensor(XL[:, n, TP:T], AO[:, n, :], XH[:, n, TP:T].bitcast(F32), ALU.subtract)\
                    .then_inc(s_xl, 1)
            for n in range(8):
                residual(8 * Q_WOB + n)
                split(8 * Q_WOB + n + 3)
            ln(2)
            with dve.Fori(0, 3) as g:
                mlp_round(Q_MLP1, g, 8)
            mlp_round(Q_MLP1, 3, 5)
            ln(3, True)

        @block.gpsimd
        def _(pool):
            G = nc.gpsimd
            own = Own(pool, s_p)

            def sums(l, q, n):
                pool.wait_ge(s_ev[1], evac(8 * q + n)[1])
                if n == 0:
                    G.tensor_copy(A1[:, :], X[:, 0, :])
                    own(G.tensor_tensor(A2[:, :], X[:, 0, :], X[:, 0, :], ALU.mult))
                else:
                    own(G.tensor_tensor(SQ[:, :], X[:, n, :], X[:, n, :], ALU.mult))
                    G.tensor_tensor(A1[:, :], A1[:, :], X[:, n, :], ALU.add)
                    own(G.tensor_tensor(A2[:, :], A2[:, :], SQ[:, :], ALU.add))
                if n == 7:
                    G.tensor_copy(SQ[:, 0:1], A2[:, 0:1]).then_inc(s_st, 1)

            def scaled(l):
                for n in range(8):
                    pool.wait_ge(s_F, 8 * l + n + 1)
                    G.tensor_scalar(X[:, n, :], FR[n % 2][:, :], ALPHA, 1.0, ALU.mult, ALU.mult).then_inc(s_al2, 1)

            pool.wait_ge(s_num, H)
            for j in range(4):
                c = C0[:, j, :, :]
                G.tensor_tensor(c, c, bcast(aeP[:, j, :], 2, 128), ALU.mult).then_inc(s_cae, 1)

            def masked(j):
                if j == 0:
                    pool.wait_ge(s_wk, 8)
                else:
                    pool.wait_ge(s_cp, 2 * j)
                G.tensor_tensor(wsKm[:, :, :], bcast(wsK[0:64, 2, 128 * j:128 * j + 128], 1, NB),
                                bcast(bmask[0:64, :], 2, 128), ALU.mult).then_inc(s_km, 1)

            for n in range(8):
                sums(0, Q_WOA, n)
                if n >= 3 and n < 7:
                    masked(n - 3)
            scaled(0)
            for n in range(8):
                sums(1, Q_WK - 1, n)
            scaled(1)

            pool.wait_ge(s_tab, 16)
            pool.wait_ge(s_pA, H)

            def load_v(b, p, freed=None):
                page = pool.value_load(table[0:1, bass.ds(b * PAGES + p, 1)], min_val=0, max_val=cache_v.shape[0] - 1)
                if freed is not None:
                    pool.wait_ge(s_pv, freed)
                pool.dma_start(Vp[p % 4][:, :], cache_v[bass.ds(page, 1)].rearrange("a t h d -> (a t) (h d)"))\
                    .then_inc(s_v_[p % 4], 16)

            for p in range(8):
                load_v(0, p, p - 3 if p >= 4 else None)
            with pool.Fori(0, NB - 1) as i:
                for p in range(8):
                    load_v(i + 1, p, 8 * i + 8 + p - 3)
            for n in range(8):
                sums(2, Q_WOB, n)
            scaled(2)
            for n in range(8):
                sums(3, N_QUADS - 1, n)


INS = ["x_prompt", "x_sample", "state_C", "state_n", "state_m", "cache_k", "cache_v", "page_table", "w_in_a",
       "b_gate_a", "w_out_a", "w_q_b", "w_out_b", "w_kv", "w_up", "w_down", "ln_g", "ln_b"]
OUTS = [(1, TP, DM), (NB, LS, DM), (1, 1, H, DK, 128), (1, 1, H, DK), (1, 1, H), (1, TP, H, 128), (1, TP, H, 128),
        (1, NB, H, DK, 128), (1, NB, H, DK), (1, NB, H), (NB, LS, H, 128), (NB, LS, H, 128)]


def kernel(**inputs):
    import concourse.bacc as bacc
    from concourse.bass_utils import run_bass_kernel_spmd

    nc = bacc.Bacc("TRN2", target_bir_lowering=False, num_devices=1)
    named = {n: np.ascontiguousarray(inputs[n]) for n in INS}
    named.update(constants())
    arrays, args = {}, []
    for name, a in named.items():
        arrays[f"in_{name}_dram"] = a
        args.append(nc.dram_tensor(f"in_{name}_dram", a.shape, mybir.dt.from_np(a.dtype), kind="ExternalInput").ap())
    for i, shape in enumerate(OUTS):
        args.append(nc.dram_tensor(f"out_{i}_dram", shape, F32, kind="ExternalOutput").ap())
    build(nc, *args)
    r = run_bass_kernel_spmd(nc, [arrays], core_ids=[0])
    return tuple(r.results[0][f"out_{i}_dram"] for i in range(len(OUTS)))
```

```python
import numpy as np
import concourse.bass as bass
from concourse import mybir
from contextlib import ExitStack

F32 = mybir.dt.float32
F32R = mybir.dt.float32r
I32 = mybir.dt.int32
ALU = mybir.AluOpType
ACT = mybir.ActivationFunctionType
AX = mybir.AxisListType

DM = 1024
NC8 = DM // 128
TP, TS = 256, 64
T = TP + TS
NB, LS = 8, 8
H = 8
DK = 64
PAGES = 8
PG = 128
BIG = 1.0e30
ALPHA = 4.0 ** 0.25
EPS = 1e-5
QSCALE = 128.0 ** -0.5

Q_QK, Q_V, Q_O, Q_WOA, Q_MLP0, Q_WK, Q_WV, Q_WQ, Q_WOB, Q_MLP1, N_QUADS = 0, 1, 2, 3, 4, 12, 13, 14, 15, 16, 24
UPS = [Q_MLP0 + 2 * g for g in range(4)] + [Q_MLP1 + 2 * g for g in range(4)]
ACT_QUADS = sorted([Q_QK, Q_V, Q_O, Q_WK, Q_WV, Q_WQ] + UPS)
NT = 8 * N_QUADS
RAW, SPL = 4, 4

SLOPES = [2.0 ** -(h + 1) for h in range(H)]


def constants():
    p = np.arange(128)
    ident = np.eye(128, dtype=np.float32)
    ones = np.ones((128, 128), np.float32)
    m = np.full((128, 448), 0.0, np.float32)
    t = np.arange(256)
    m[:, 0:256] = np.where(p[:, None] <= t[None, :], 0, BIG)
    m[:, 256:384] = np.where(p[:, None] <= p[None, :], 0, BIG)
    s = np.arange(64)
    m[0:64, 384:448] = np.where((s[:, None] // 8 == s[None, :] // 8) & (s[:, None] <= s[None, :]), 0, BIG)
    start = np.zeros(T, bool)
    start[0] = True
    start[TP::LS] = True
    rows = np.zeros((128, 2 * T), np.float32)
    rows[:, 0:T] = np.where(start, 0, 1)
    rows[:, T:] = np.where(start, -BIG, 0)
    sel = np.zeros((128, 12 * 128), np.float32)
    for h in range(H):
        sel[h, h * 128:(h + 1) * 128] = 1
        sel[h, (8 + h // 2) * 128 + 64 * (h % 2):(8 + h // 2) * 128 + 64 * (h % 2) + 64] = 1
    d = np.zeros((128, 384), np.float32)
    d[:, 0:128] = np.where(p[None, :] <= p[:, None], p[None, :] - p[:, None], -BIG)
    d[:, 128:384] = np.where(t[None, :] <= 128 + p[:, None], t[None, :] - 128 - p[:, None], -BIG)
    sl = np.array(SLOPES)
    key = np.tile(np.arange(PAGES * PG) - PAGES * PG, (128, 1)).astype(np.float32)
    j, rb, rq = p // 32, p % 32 // 8, p % 8
    sb, sk = s // 8, s % 8
    slope = sl[4 * np.arange(2)[None, :] + j[:, None]]
    g4 = 4 * np.arange(2)
    ok = (sb[None, None, :] == rb[:, None, None] + g4[None, :, None]) & (sk[None, None, :] <= rq[:, None, None])
    bo = np.where(ok[:, :, None, :], slope[:, None, :, None] * sk[None, None, None, :], -BIG)
    bo = bo.reshape(128, 256).astype(np.float32)
    n = np.tile(np.arange(4) + 1.0, (128, 2)).astype(np.float32)
    bm = np.zeros((128, 8), np.float32)
    bm[0:64] = (sb[:, None] == np.arange(NB)[None, :])
    base = np.concatenate([ident, ones, bm], 1)
    return {"c_base": base, "c_mlstm": np.concatenate([m, rows], 1), "c_sel": sel[0:8].copy(),
            "c_attn": np.concatenate([d, key, bo, slope.astype(np.float32), n], 1)}


def bcast(ap, axis, n):
    v = ap.unsqueeze(axis)
    shape = list(v.shape)
    shape[axis] = n
    return v.to_broadcast(shape)


class Own:

    def __init__(self, eng, sem):
        self.eng, self.sem, self.n, self.shift = eng, sem, 0, 0

    def __call__(self, ins):
        self.n += 1
        ins.then_inc(self.sem, 1)
        self.eng.wait_ge(self.sem, self.shift + self.n)


def evac(t):
    q = t // 8
    mine = q in ACT_QUADS
    before = sum(1 for x in range(q) if (x in ACT_QUADS) == mine)
    return (0 if mine else 1), 8 * before + t % 8 + 1


def build(nc, x_prompt, x_sample, state_C, state_n, state_m, cache_k, cache_v, page_table,
          w_in_a, b_gate_a, w_out_a, w_q_b, w_out_b, w_kv, w_up, w_down, ln_g, ln_b,
          c_base, c_mlstm, c_sel, c_attn,
          y_prompt, y_sample, p_C, p_n, p_m, p_k, p_v, s_C, s_n, s_m, s_k_d, s_v_d):
    ctx = ExitStack()
    with ctx:
        at = [nc.sbuf_base + (-nc.sbuf_base) % 64]
        top = nc.sbuf_usable_end

        def put(name, shape, dt=F32, where=at):
            size = 4 * int(np.prod(shape[1:]))
            t = nc.alloc_sbuf_tensor_at(name, shape, dt, offset=where[0])
            where[0] += size + (-size) % 32
            assert where[0] <= top, (name, where[0], top)
            return t

        raw2_at = at[0] + 2 * 8192
        raw = [put(f"raw{i}", [128, 8, 256]) for i in range(RAW)]
        WH = [put(f"w_hi{i}", [128, 8, 128], F32R) for i in range(SPL)]
        WL = [put(f"w_lo{i}", [128, 8, 128], F32R) for i in range(SPL)]
        X = put("x", [128, NC8, T])
        XH = put("x_hi", [128, NC8, T], F32R)
        XL = put("x_lo", [128, NC8, T], F32R)
        qk_at = [at[0]]
        HH = put("h_hi", [128, NC8, T], F32R)
        HL = put("h_lo", [128, NC8, T], F32R)
        QA = put("q_attn", [128, H, T], F32, qk_at)
        KA = put("k_attn", [128, H, T], F32, qk_at)
        VT = put("v_tok", [128, 3, DM])
        FR = [put(f"fm{i}", [128, T]) for i in range(2)]
        FS = [put(f"sq{i}", [128, T]) for i in range(2)]
        A1 = put("sum_x", [128, T])
        A2 = put("sum_xx", [128, T])
        SQ = put("xx", [128, T])
        base = put("base", [128, 264])
        ident, ones, bmask = base[:, 0:128], base[:, 128:256], base[:, 256:264]
        lnT = put("ln_cols", [128, 64])
        bg = put("b_gate", [40, 1])
        table = put("page_table", [1, NB * PAGES], I32)
        phase_const = [at[0]]
        cat = put("attn_tables", [128, 384 + 1024 + 256 + 2 + 8])
        dist, keys, bias_own = cat[:, 0:384], cat[:, 384:1408], cat[:, 1408:1664]
        slope, nidx = cat[:, 1664:1666], cat[:, 1666:1674]
        cml = put("mlstm_tables", [128, 448 + 2 * T], F32, phase_const)
        n0 = put("n0", [8, H * DK], F32, phase_const)
        assert phase_const[0] <= at[0]
        phase = at[0]

        a = [phase]
        C0 = put("C", [128, 4, NB, 128], F32, a)
        ewk = [a[0]]
        E = [put(f"decay{i}", [128, 448], F32, a) for i in range(2)]
        W = [put(f"weight{i}", [128, 448], F32, a) for i in range(2)]
        wsK = put("wsk", [128, 3, 512], F32, a)
        wgraw = put("wg_raw", [128, 8, 16], F32, ewk)
        WGH = put("wg_hi", [128, 8, 128], F32R, ewk)
        WGL = put("wg_lo", [128, 8, 128], F32R, ewk)
        lnN = put("ln_rows", [64, 128], F32, ewk)
        assert ewk[0] <= a[0]
        wk2 = [a[0] - 6144 - 7168]
        wsKm = put("wsk_masked", [64, NB, 128], F32, wk2)
        Wst = put("c_prompt", [128, 512], F32, wk2)
        kT = put("k_mlstm", [128, 4, T], F32, a)
        npr_at = [a[0]]
        npr = put("n_prompt", [1, 512], F32, npr_at)
        qT = put("q_mlstm", [128, 4, T], F32, a)
        sel = put("sel", [8, 12 * 128], F32, a)
        aqT = put("aq", [128, 4, TS], F32, a)
        an = put("aqn", [128, 4, TS], F32, a)
        eo = [put(f"exp_o{i}", [128, T], F32, a) for i in range(2)]
        emS = put("exp_neg_m", [128, T], F32, a)
        rec = put("rec", [128, T], F32, a)
        hg = put("h_gated", [128, T], F32, a)
        R = [put(f"row{i}", [8, T], F32, a) for i in range(6)]
        cols = put("cols", [128, 64], F32, a)
        small = put("small", [8, 64], F32, a)
        m0 = small[:, 0:8]
        ael = small[:, 8:16]
        mnew = small[:, 16:25]
        atr = put("a_rows", [8, TS], F32, a)
        aeP = put("ae_pairs", [128, 4, NB], F32, a)
        nout = put("n_out", [8, 512], F32, a)

        b_ = [phase]
        low = [phase]
        b_[0] += 16384
        raw_at = [raw2_at]
        Kp = [put(f"k_page{i}", [128, DM], F32, raw_at) for i in range(4)]
        vreg = b_[0]
        Vp = [put(f"v_page{i}", [128, DM], F32, b_) for i in range(4)]
        pr = [vreg]
        PL = [put(f"p_logit{i}", [128, 384], F32, pr) for i in range(2)]
        PTt = [put(f"p_turned{i}", [128, 384], F32, pr) for i in range(2)]
        pst = put("p_stats", [128, 8 * 8], F32, pr)
        assert pr[0] <= b_[0]
        ln_at = [vreg]
        LT = [put(f"ln_t{i}", [128, 2, T], F32, ln_at) for i in range(2)]
        mu = put("ln_mu", [128, T], F32, ln_at)
        var = put("ln_var", [128, T], F32, ln_at)
        rs = put("ln_rstd", [128, T], F32, ln_at)
        tmp = put("ln_tmp", [128, T], F32, ln_at)
        assert ln_at[0] <= b_[0]
        b_[0] += 0
        KT = [put(f"k_turned{i}", [128, H, 256], F32, low) for i in range(2)]
        L = put("logits", [128, 2, PAGES * PG], F32, b_)
        on_at = [b_[0] - 8192]
        ON = put("o_rows", [128, 4, 2, 128], F32, on_at)
        ko_at = [b_[0]]
        PT = put("probs_turned", [128, 16, 128], F32, b_)
        KO = [put(f"turned{i}", [128, 3, 128], F32, ko_at) for i in range(2)]
        QZ = put("q_padded", [128, H, 4, 32], F32, b_)
        PO = put("own_probs", [128, 2, 64], F32, b_)
        PTo = put("own_turned", [64, 2, 128], F32, b_)
        sm = put("soft_small", [128, 64], F32, b_)
        bsum, mxb, pen, nb = sm[:, 0:8], sm[:, 8:16], sm[:, 16:24], sm[:, 24:32]
        omx, mn, ix, m2, nbo = sm[:, 32:34], sm[:, 34:36], sm[:, 36:38], sm[:, 38:40], sm[:, 40:42]
        acc, den, rden = sm[:, 42:52], sm[:, 52:54], sm[:, 54:56]
        AT = put("attn_prompt", [128, H, TP], F32, b_)
        AO = put("attn_sample", [128, H, TS], F32, b_)

        ps = [ctx.enter_context(nc.psum_tensor(f"ps{i}", [128, 512], F32)) for i in range(8)]

        def sem(name):
            return ctx.enter_context(nc.semaphore(name))

        s_raw = [sem(f"raw_loaded{i}") for i in range(RAW)]
        s_hi, s_lo, s_mm = sem("w_hi_split"), sem("w_lo_split"), sem("tile_done")
        s_ev = [sem("act_emptied"), sem("dve_emptied")]
        s_x, s_base, s_ml, s_gw, s_ln, s_n0, s_c0, s_at, s_tab = [
            sem(n) for n in ("x_in", "base_in", "mlstm_in", "gate_w_in", "ln_in", "n0_in", "c0_in", "attn_in", "table_in")]
        s_m0 = sem("m0_in")
        s_xt, s_xh, s_xl, s_xf = sem("x_turned"), sem("x_hi_done"), sem("x_lo_done"), sem("x_copied")
        s_lnt, s_lnc = sem("ln_turned"), sem("ln_copied")
        s_d, s_a, s_p = sem("dve_own"), sem("act_own"), sem("pool_own")
        s_gz, s_gh, s_gl, s_gp = sem("gate_zeroed"), sem("gate_hi"), sem("gate_lo"), sem("gate_done")
        s_gabs, s_gln, s_mt, s_emn, s_wsl, s_ws, s_al, s_aex = [
            sem(n) for n in ("gate_abs", "gate_log", "m_rows", "emn_rows", "ws_log", "ws_rows", "a_log", "a_rows_done")]
        s_colp, s_col = sem("cols_turned"), sem("cols_copied")
        s_bcp, s_bc = sem("pairs_cast"), sem("pairs_used")
        s_vt, s_vc = sem("v_turned"), sem("v_copied")
        s_sp, s_D, s_E, s_W = sem("mS_done"), sem("decay_log"), sem("decay_exp"), sem("weights_done")
        s_emp, s_emc, s_num, s_hg, s_hh, s_hl = [
            sem(n) for n in ("emn_cast", "emn_copied", "num_done", "gated", "h_hi_done", "h_lo_done")]
        s_kt, s_wk, s_km, s_cp, s_cadd, s_np, s_nadd = [
            sem(n) for n in ("k_tokens", "wsk_done", "wsk_masked_done", "c_product", "c_added", "n_product", "n_added")]
        s_cae = sem("c_decayed")
        s_sq = sem("relu_squared")
        s_st, s_lnp, s_var, s_rs, s_t, s_F, s_al2 = [
            sem(n) for n in ("sums_done", "stats_cast", "var_done", "rstd_guess", "centred", "ln_out", "x_scaled")]
        s_tp, s_tc, s_tv = sem("turn_done"), sem("turn_copied"), sem("v_turn_copied")
        s_to = [sem(f"turn_out{i}") for i in range(2)]
        s_pS, s_pmx, s_pex, s_pnm, s_pT, s_pTc, s_pV, s_pA = [
            sem(n) for n in ("pS_done", "p_max", "p_exp", "p_norm", "p_turn", "p_turn_copied", "p_out", "p_out_copied")]
        s_k = [sem(f"k_in{i}") for i in range(4)]
        s_v_ = [sem(f"v_in{i}") for i in range(4)]
        s_qz, s_ktr, s_sc, s_own, s_Lr, s_sm, s_ex, s_rd = [
            sem(n) for n in ("q_padded_done", "k_turned_page", "pair_scored", "own_scored", "scores_read", "softmax_bias",
                             "exp_done", "rden_done")]
        s_qzz = sem("q_padded_zeroed")
        s_kA, s_kD, s_ptt, s_ptc, s_pv, s_on, s_ot, s_ao = [
            sem(n) for n in ("k_copied_act", "k_copied_dve", "probs_turned_n", "probs_copied", "page_summed",
                             "o_scaled", "o_turned", "attn_out")]
        s_nm = sem("new_m")
        s_out = sem("stored")
        s_co, s_po = sem("c_stored"), sem("prompt_state_stored")

        block = ctx.enter_context(nc.Block())

        def lhs_k(w):
            return w.rearrange("(k p) n -> p k n", p=128)

        win = w_in_a[0]

        def wsrc(u):
            q, j = u // 4, u % 4
            c = 256 * j
            w, c0 = {Q_QK: (win, 0), Q_V: (win, 1024), Q_O: (win, 2048), Q_WOA: (w_out_a[0], 0),
                     Q_WK: (w_kv, 0), Q_WV: (w_kv, 1024), Q_WQ: (w_q_b[0], 0), Q_WOB: (w_out_b[0], 0)}[q]
            return lhs_k(w[:, c0 + c:c0 + c + 256])

        @block.sync
        def _(sp):
            def load_unit(u, src, more=0):
                if isinstance(more, int) and u < RAW:
                    pass
                else:
                    sp.wait_ge(s_lo, 2 * (u - RAW) + 2 + 2 * more)
                sp.dma_start(raw[u % RAW][:, :, :], src).then_inc(s_raw[u % RAW], 16)

            sp.dma_start(base[:, :], c_base).then_inc(s_base, 16)
            sp.dma_start(VT[:, 0:2, :], x_prompt[0].rearrange("(t p) c -> p t c", p=128)).then_inc(s_x, 16)
            sp.dma_start(VT[0:64, 2, :], x_sample.rearrange("b t c -> (b t) c")).then_inc(s_x, 16)
            sp.dma_start(wgraw[:, :, :], lhs_k(win[:, 3072:3088])).then_inc(s_gw, 16)
            load_unit(0, wsrc(0))
            load_unit(1, wsrc(1))
            sp.dma_start(cml[:, :], c_mlstm).then_inc(s_ml, 16)
            sp.dma_start(sel[:, :], c_sel).then_inc(s_ml, 16)
            sp.dma_start(m0, state_m[0].rearrange("b h -> h b"), allow_slow_non_contiguous=True).then_inc(s_m0, 16)
            sp.dma_start(bg[0:8, :], b_gate_a[0:1, 0:8].rearrange("a h -> h a"), allow_slow_non_contiguous=True).then_inc(s_m0, 16)
            sp.dma_start(bg[32:40, :], b_gate_a[0:1, 8:16].rearrange("a h -> h a"), allow_slow_non_contiguous=True).then_inc(s_m0, 16)
            load_unit(2, wsrc(2))
            load_unit(3, wsrc(3))
            sp.dma_start(lnN[0:32, :], ln_g.rearrange("l w (c p) -> (l w c) p", p=128)).then_inc(s_ln, 16)
            sp.dma_start(lnN[32:64, :], ln_b.rearrange("l w (c p) -> (l w c) p", p=128)).then_inc(s_ln, 16)
            sp.dma_start(n0[:, :], state_n[0].rearrange("b h k -> b (h k)")).then_inc(s_n0, 16)
            sp.dma_start(table[:, :], page_table.rearrange("b p -> (b p)").unsqueeze(0)).then_inc(s_tab, 16)
            for j in range(4):
                for h2 in range(2):
                    sp.dma_start(C0[64 * h2:64 * h2 + 64, j, :, :],
                                 state_C[0, :, 2 * j + h2].rearrange("b k v -> k b v")).then_inc(s_c0, 16)
            for u in range(4, 16):
                load_unit(u, wsrc(u))

            def mlp_loads(first, m):
                with sp.Fori(0, 4) as g:
                    for j in range(4):
                        load_unit(4 * first + j, lhs_k(w_up[m][:, bass.ds(g * 1024 + 256 * j, 256)]), 8 * g)
                    for j in range(4):
                        load_unit(4 * first + 4 + j,
                                  lhs_k(w_down[m][bass.ds(g * 1024, 1024), 256 * j:256 * j + 256]), 8 * g)

            mlp_loads(Q_MLP0, 0)
            for u in range(4 * Q_WK, 4 * Q_WK + 4):
                load_unit(u, wsrc(u))
            sp.wait_ge(s_co, 16 * 8)
            sp.wait_ge(s_po, 16 * 4)
            sp.dma_start(cat[:, :], c_attn).then_inc(s_at, 16)

            for u in range(4 * Q_WV, 4 * Q_WOB + 2):
                load_unit(u, wsrc(u))

            def load_page(cache, dst, loaded, index, freed=None):
                page = sp.value_load(table[0:1, bass.ds(index, 1)] if not isinstance(index, int)
                                     else table[0:1, index:index + 1], min_val=0, max_val=cache_k.shape[0] - 1)
                if freed is not None:
                    sp.wait_ge(*freed)
                sp.dma_start(dst[:, :], cache[bass.ds(page, 1)].rearrange("a t h d -> (a t) (h d)"))\
                    .then_inc(loaded, 16)

            def k_pages(first, last):
                with sp.Fori(first // 4, last // 4) as i:
                    for p in range(4):
                        load_page(cache_k, Kp[p], s_k[p], 4 * i + p, (s_ktr, 4 * i + p - 3))

            def v_pages(first, last):
                with sp.Fori(first // 4, last // 4) as i:
                    for p in range(4):
                        load_page(cache_v, Vp[p], s_v_[p], 4 * i + p, (s_pv, 4 * i + p - 3))

            sp.wait_ge(s_tab, 16)
            sp.wait_ge(s_lo, 8 * Q_WOB)
            for p in range(4):
                load_page(cache_k, Kp[p], s_k[p], p)
            sp.wait_ge(s_pA, H)
            for p in range(4):
                load_page(cache_v, Vp[p], s_v_[p], p)
            k_pages(4, 36)
            v_pages(4, 36)
            k_pages(36, 64)
            for u in range(4 * Q_WOB + 2, 4 * Q_WOB + 4):
                sp.wait_ge(s_ktr, 64)
                load_unit(u, wsrc(u))
            v_pages(36, 64)
            mlp_loads(Q_MLP1, 1)

        @block.tensor
        def _(pe):
            mm = nc.tensor.matmul

            def dense(t, hi, lo, chunk_ready=None, turn=0, ev_shift=0, wait_ev=True):
                if wait_ev and t >= 2:
                    e, n = evac(t - 2)
                    pe.wait_ge(s_ev[e], n + ev_shift)
                pe.wait_ge(s_lo, t + 1 + 16 * turn)
                out = ps[t % 2][:, 0:T]
                for k in range(8):
                    if chunk_ready is not None:
                        pe.wait_ge(*chunk_ready(k))
                    mm(out, WH[t % SPL][:, k, :], hi[:, k, :], start=(k == 0), stop=False)
                    mm(out, WH[t % SPL][:, k, :], lo[:, k, :], start=False, stop=False)
                    last = mm(out, WL[t % SPL][:, k, :], hi[:, k, :], start=False, stop=(k == 7))
                last.then_inc(s_mm, 1)

            def turn3(bank, src):
                nc.tensor.transpose(bank[:, 0:128], src[:, 0:128], ident)
                nc.tensor.transpose(bank[:, 128:256], src[:, 128:256], ident)
                return nc.tensor.transpose(bank[0:64, 256:384], src[:, 256:320], ident)

            pe.wait_ge(s_base, 16)
            pe.wait_ge(s_x, 32)
            for n in range(8):
                if n >= 2:
                    pe.wait_ge(s_xf, n - 1)
                c = slice(128 * n, 128 * n + 128)
                bank = ps[2 + n % 2]
                nc.tensor.transpose(bank[:, 0:128], VT[:, 0, c], ident)
                nc.tensor.transpose(bank[:, 128:256], VT[:, 1, c], ident)
                nc.tensor.transpose(bank[:, 256:320], VT[0:64, 2, c], ident[0:64, 0:64]).then_inc(s_xt, 1)
            pe.wait_ge(s_ln, 32)
            nc.tensor.transpose(ps[4][:, 0:64], lnN[:, :], ident[0:64, 0:64]).then_inc(s_lnt, 1)
            pe.wait_ge(s_gl, 1)
            for k in range(8):
                pe.wait_ge(s_xl, k + 1)
                mm(ps[5][:, 0:T], WGH[:, k, :], XH[:, k, :], start=(k == 0), stop=False)
                mm(ps[5][:, 0:T], WGH[:, k, :], XL[:, k, :], start=False, stop=False)
                last = mm(ps[5][:, 0:T], WGL[:, k, :], XH[:, k, :], start=False, stop=(k == 7))
            last.then_inc(s_gp, 1)
            for n in range(8):
                dense(8 * Q_QK + n, XH, XL)
            pe.wait_ge(s_n0, 16)
            for j in range(4):
                last = nc.tensor.transpose(ps[7][:, 352 + 8 * j:360 + 8 * j], n0[:, 128 * j:128 * j + 128],
                                           ident[0:8, 0:8])
            pe.wait_ge(s_ws, 1)
            for i in range(3):
                w = 128 if i < 2 else 64
                nc.tensor.transpose(ps[7][0:w, 8 * i:8 * i + 8], R[4][:, 128 * i:128 * i + w], ident[0:8, 0:8])
                nc.tensor.transpose(ps[7][0:w, 24 + 8 * i:32 + 8 * i], R[5][:, 128 * i:128 * i + w], ident[0:8, 0:8])
            pe.wait_ge(s_aex, 2)
            nc.tensor.transpose(ps[7][0:8, 48:56], ael, ident[0:8, 0:8])
            for j in range(4):
                s = sel[:, (8 + j) * 128:(9 + j) * 128]
                mm(ps[7][:, 64 + 64 * j:128 + 64 * j], s, atr[:, :], start=True, stop=True)
                last = mm(ps[7][:, 320 + 8 * j:328 + 8 * j], s, ael, start=True, stop=True)
            last.then_inc(s_colp, 1)
            for n in range(8):
                dense(8 * Q_V + n, XH, XL)
                if n >= 1:
                    pe.wait_ge(*((s_ev[0]), evac(8 * Q_V + n - 1)[1]))
                    if n >= 3:
                        pe.wait_ge(s_vc, n - 2)
                    turn3(ps[4 + (n - 1) % 2], FR[(n - 1) % 2]).then_inc(s_vt, 1)
            pe.wait_ge(s_ev[0], evac(8 * Q_V + 7)[1])
            pe.wait_ge(s_vc, 6)
            turn3(ps[4 + 7 % 2], FR[7 % 2]).then_inc(s_vt, 1)

            pe.wait_ge(s_ml, 32)
            pe.wait_ge(s_col, 1)
            for h in range(H):
                j, r = h // 2, slice(64 * (h % 2), 64 * (h % 2) + 64)
                hs = sel[:, 128 * h:128 * h + 128]
                S, MB, EM, DEN, NUM = ps[2], ps[3], ps[4], ps[5], ps[6]
                if h == 0:
                    pe.wait_ge(s_bc, 2)
                if h >= 1:
                    pe.wait_ge(s_W, h)
                mm(MB[:, 0:T], hs, R[2][:, :], start=True, stop=True)
                mm(S[:, 0:256], kT[r, j, 0:128], qT[r, j, 0:256], start=True, stop=True)
                mm(S[:, 256:384], kT[r, j, 128:256], qT[r, j, 128:256], start=True, stop=True)
                mm(S[0:64, 384:448], kT[r, j, 256:320], qT[r, j, 256:320], start=True, stop=True).then_inc(s_sp, 1)
                dense(8 * Q_O + h, XH, XL)
                if h == 0:
                    pe.wait_ge(s_vc, 8)
                    pe.wait_ge(s_c0, 16 * 8)
                if h >= 1:
                    pe.wait_ge(s_emc, h)
                mm(EM[:, 0:T], hs, R[1][:, :], start=True, stop=True).then_inc(s_emp, 1)
                if h >= 1:
                    pe.wait_ge(s_hg, h)
                w = W[h % 2]
                pe.wait_ge(s_W, h + 1)
                c = slice(128 * h, 128 * h + 128)
                for dst, v0, v1, v2 in ((NUM, VT[:, 0, c], VT[:, 1, c], VT[:, 2, c]), (DEN, ones, ones, ones)):
                    mm(dst[:, 0:256], v0, w[:, 0:256], start=True, stop=True)
                    mm(dst[:, 128:256], v1, w[:, 256:384], start=False, stop=True, skip_group_check=True)
                    mm(dst[:, 256:320], v2, w[:, 384:448], start=False, stop=True, skip_group_check=True)
                for b in range(NB):
                    mm(NUM[:, 256 + 8 * b:264 + 8 * b], C0[r, j, b, :], aqT[r, j, 8 * b:8 * b + 8],
                       start=False, stop=True, skip_group_check=True)
                mm(DEN[:, 256:320], ones[r, :], an[r, j, :], start=False, stop=True, skip_group_check=True)\
                    .then_inc(s_num, 1)

            def state_step(i):
                if i < 4:
                    pe.wait_ge(s_num, H)
                    if i >= 1:
                        pe.wait_ge(s_wk, 2 * i)
                    turn3(ps[2], kT[:, i, :]).then_inc(s_kt, 1)
                if i == 4:
                    pe.wait_ge(s_wk, 8)
                    for h in range(H):
                        o = ps[3][64 * (h % 2):64 * (h % 2) + 64, 128 * (h // 2):128 * (h // 2) + 128]
                        for q in range(2):
                            mm(o, wsK[:, q, 64 * h:64 * h + 64], VT[:, q, 128 * h:128 * h + 128],
                               start=(q == 0), stop=(q == 1), skip_group_check=True)
                    for q in range(2):
                        mm(ps[4][0:1, :], ones[:, 0:1], wsK[:, q, :], start=(q == 0), stop=(q == 1))
                    mm(ps[5][0:8, :], bmask[0:64, :], wsK[0:64, 2, :], start=True, stop=True).then_inc(s_np, 1)
                if 4 <= i < 8:
                    j = i - 4
                    pe.wait_ge(s_km, j + 1)
                    for half in range(2):
                        bank = ps[6 + half]
                        if j >= 1:
                            pe.wait_ge(s_cadd, 2 * j - 1 + half)
                        for bb in range(4):
                            b = 4 * half + bb
                            for h2 in range(2):
                                h = 2 * j + h2
                                last = mm(bank[64 * h2:64 * h2 + 64, 128 * bb:128 * bb + 128],
                                          wsKm[:, b, 64 * h2:64 * h2 + 64], VT[0:64, 2, 128 * h:128 * h + 128],
                                          start=True, stop=True, skip_group_check=True)
                        last.then_inc(s_cp, 1)

            for n in range(8):
                dense(8 * Q_WOA + n, HH, HL, (lambda k: (s_hl, k + 1)) if n == 0 else None)
                state_step(n)

            def ln_stats(l):
                pe.wait_ge(s_st, l + 1)
                if l == 0:
                    pe.wait_ge(s_nadd, 2)
                mm(ps[2][:, 0:T], ones, A1[:, :], start=True, stop=True)
                mm(ps[3][:, 0:T], ones, A2[:, :], start=True, stop=True).then_inc(s_lnp, 1)

            def mlp(q0, xl0, hl0):
                up0, dn0 = 8 * q0, 8 * q0 + 8
                with pe.Fori(0, 4) as g:
                    for n in range(8):
                        dense(up0 + n, XH, XL, (lambda k: (s_xl, xl0 + k + 1)) if n == 0 else None, g, 8 * g)
                    for n in range(8):
                        t = dn0 + n
                        dense(t, HH, HL, (lambda k: (s_hl, hl0 + k + 1 + 8 * g)) if n == 0 else None, g, 8 * g)

            ln_stats(0)
            mlp(Q_MLP0, 8, 8)
            ln_stats(1)

            def kv_turn(i):
                n = i % 8
                if i < 8:
                    pe.wait_ge(s_ev[0], evac(8 * Q_WK + n)[1])
                    src = KA[:, n, :]
                else:
                    pe.wait_ge(s_ev[0], evac(8 * Q_WV + n)[1])
                    src = FR[n % 2]
                if i >= 2:
                    pe.wait_ge(*((s_tc, i - 1) if i < 10 else (s_tv, i - 9)))
                turn3(ps[4 + i % 2], src).then_inc(s_tp, 1)

            for n in range(8):
                dense(8 * Q_WK + n, XH, XL, (lambda k: (s_xl, 16 + k + 1)) if n == 0 else None)
                if n >= 1:
                    kv_turn(n - 1)
            for n in range(8):
                dense(8 * Q_WV + n, XH, XL)
                kv_turn(7 + n)

            def p_scores(h):
                if h >= 1:
                    pe.wait_ge(s_pmx, h)
                pe.wait_ge(s_ev[0], evac(8 * Q_WQ + h)[1])
                mm(ps[2][:, 0:128], QA[:, h, 0:128], KA[:, h, 0:128], start=True, stop=True)
                mm(ps[2][:, 128:384], QA[:, h, 128:256], KA[:, h, 0:256], start=True, stop=True).then_inc(s_pS, 1)

            def p_turn(h):
                pe.wait_ge(s_pnm, 2 * h + 2)
                if h >= 1:
                    pe.wait_ge(s_pTc, h)
                pl = PL[h % 2]
                nc.tensor.transpose(ps[3][:, 0:128], pl[:, 0:128], ident)
                nc.tensor.transpose(ps[3][:, 128:256], pl[:, 128:256], ident)
                nc.tensor.transpose(ps[3][:, 256:384], pl[:, 256:384], ident).then_inc(s_pT, 1)

            def p_out(h):
                pe.wait_ge(s_pTc, h + 1)
                pe.wait_ge(s_tv, 8)
                if h >= 1:
                    pe.wait_ge(s_pA, h)
                c = slice(128 * h, 128 * h + 128)
                mm(ps[6][:, 0:256], VT[:, 0, c], PTt[h % 2][:, 0:256], start=True, stop=True)
                mm(ps[6][:, 128:256], VT[:, 1, c], PTt[h % 2][:, 256:384], start=False, stop=True,
                   skip_group_check=True).then_inc(s_pV, 1)

            def p_step(i):
                if 0 <= i - 2 < H:
                    p_out(i - 2)
                if 0 <= i - 1 < H:
                    p_turn(i - 1)
                if 0 <= i < H:
                    p_scores(i)

            for n in range(8):
                dense(8 * Q_WQ + n, XH, XL)
                if n == 0:
                    kv_turn(15)
                p_step(n - 1)
            pe.wait_ge(s_ev[0], evac(8 * Q_WQ + 7)[1])
            for i in range(7, 10):
                p_step(i)
            pe.wait_ge(s_pA, H)

            def turn_page(P):
                pe.wait_ge(s_k[P % 4], 16 * (P // 4 + 1))
                if P >= 2:
                    pe.wait_ge(s_kA, P - 1)
                    pe.wait_ge(s_kD, P - 1)
                for h in range(H):
                    last = nc.tensor.transpose(ps[2 * (P % 2) + h // 4][:, 128 * (h % 4):128 * (h % 4) + 128],
                                               Kp[P % 4][:, 128 * h:128 * h + 128], ident)
                last.then_inc(s_ktr, 1)

            def score_pair(pair):
                G, bb, r = pair // 16, pair // 4 % 4, pair % 4
                pe.wait_ge(s_kA, 2 * pair + 2)
                pe.wait_ge(s_kD, 2 * pair + 2)
                for a_ in range(2):
                    for j in range(4):
                        last = mm(ps[4 + 2 * a_ + r // 2][32 * j:32 * j + 32, 256 * (r % 2):256 * (r % 2) + 256],
                                  QZ[:, 4 * a_ + j, bb, :], KT[pair % 2][:, 4 * a_ + j, :],
                                  start=(bb == 0 and r % 2 == 0), stop=True, skip_group_check=True)
                last.then_inc(s_sc, 1)

            def probs_turn(G):
                pe.wait_ge(s_kA, 32 * G + 32)
                for a_ in range(2):
                    for j in range(4):
                        h = 4 * a_ + j
                        last = mm(ps[0][32 * j:32 * j + 32, 64 * a_:64 * a_ + 64],
                                  QA[:, h, TP + 32 * G:TP + 32 * G + 32], KA[:, h, TP:T], start=True, stop=True,
                                  skip_group_check=True)
                last.then_inc(s_own, 1)
                pe.wait_ge(s_ex, 10 * G + 2)
                for a_ in range(2):
                    last = nc.tensor.transpose(ps[1][0:64, 128 * a_:128 * a_ + 128], PO[:, a_, :], ident)
                last.then_inc(s_ptt, 1)
                for c in range(4):
                    for i in range(4):
                        m = 4 * c + i
                        pe.wait_ge(s_ex, 10 * G + 2 + m // 2 + 1)
                        if c >= 2 and i == 0:
                            pe.wait_ge(s_ptc, 5 * G + c)
                        last = nc.tensor.transpose(ps[4 + c % 2][:, 128 * i:128 * i + 128],
                                                   L[:, m // 8, 128 * (m % 8):128 * (m % 8) + 128], ident)
                    last.then_inc(s_ptt, 1)

            def values(G):
                def o(bb, a_, j):
                    c = 256 * (bb % 2) + 128 * a_
                    return ps[6 + bb // 2][32 * j:32 * j + 32, c:c + 128]

                pe.wait_ge(s_ptc, 5 * G + 1)
                for bb in range(4):
                    for a_ in range(2):
                        for j in range(4):
                            h = 4 * a_ + j
                            mm(o(bb, a_, j), PTo[:, a_, 32 * j:32 * j + 32], VT[0:64, 2, 128 * h:128 * h + 128],
                               start=(bb % 2 == 0 and a_ == 0), stop=True, skip_group_check=True)
                pe.wait_ge(s_ptc, 5 * G + 5)
                for bb in range(4):
                    for p in range(PAGES):
                        P = 32 * G + 8 * bb + p
                        pe.wait_ge(s_v_[P % 4], 16 * (P // 4 + 1))
                        for a_ in range(2):
                            for j in range(4):
                                h = 4 * a_ + j
                                last = mm(o(bb, a_, j), PT[:, 8 * a_ + p, 32 * j:32 * j + 32],
                                          Vp[P % 4][:, 128 * h:128 * h + 128], start=False, stop=True,
                                          skip_group_check=True)
                        last.then_inc(s_pv, 1)

            def out_turn(G):
                pe.wait_ge(s_on, G + 1)
                for bb in range(4):
                    for a_ in range(2):
                        last = nc.tensor.transpose(
                            ps[6 + bb // 2][:, 256 * (bb % 2) + 128 * a_:256 * (bb % 2) + 128 * a_ + 128],
                            ON[:, bb, a_, :], ident)
                last.then_inc(s_ot, 1)

            for G in range(2):
                for pair in range(16 * G, 16 * G + 16):
                    turn_page(2 * pair)
                    turn_page(2 * pair + 1)
                    if pair == 16:
                        out_turn(0)
                        pe.wait_ge(s_ao, 1)
                    if pair % 16 == 1:
                        pe.wait_ge(s_qz, G + 1)
                    if pair % 16 >= 1:
                        score_pair(pair - 1)
                score_pair(16 * G + 15)
                probs_turn(G)
                values(G)
            out_turn(1)
            for n in range(8):
                dense(8 * Q_WOB + n, XH, XL, (lambda k: (s_xl, 24 + k + 1)) if n == 0 else None)
            ln_stats(2)
            mlp(Q_MLP1, 32, 40)
            ln_stats(3)
            for n in range(8):
                pe.wait_ge(s_F, 24 + n + 1)
                if n >= 2:
                    pe.wait_ge(s_tc, 8 + n - 1)
                turn3(ps[4 + n % 2], X[:, n, :]).then_inc(s_tp, 1)

        @block.scalar
        def _(act):
            A = nc.scalar.activation
            own = Own(act, s_a)

            def split(t, turn=0):
                u = t // 2
                if t % 2 == 0:
                    act.wait_ge(s_raw[u % RAW], 16 * (u // RAW + 1) + 32 * turn)
                if t >= SPL:
                    act.wait_ge(s_mm, t - SPL + 1 + 16 * turn)
                A(WH[t % SPL][:, :, :], raw[u % RAW][:, :, 128 * (t % 2):128 * (t % 2) + 128], ACT.Copy)\
                    .then_inc(s_hi, 1)

            def tile(t, turn=0):
                act.wait_ge(s_mm, t + 1 + 16 * turn)
                return ps[t % 2][:, 0:T]

            act.wait_ge(s_gw, 16)
            act.wait_ge(s_gz, 1)
            A(WGH[:, :, 0:8], wgraw[:, :, 0:8], ACT.Copy)
            A(WGH[:, :, 32:40], wgraw[:, :, 8:16], ACT.Copy).then_inc(s_gh, 1)
            for n in range(8):
                act.wait_ge(s_xf, n + 1)
                A(XH[:, n, :], X[:, n, :], ACT.Copy).then_inc(s_xh, 1)
                if n < 4:
                    split(n)
            def rows_log():
                act.wait_ge(s_gabs, 1)
                own(A(R[2][:, :], R[2][:, :], ACT.Exp, scale=-1.0))
                A(R[2][:, :], R[2][:, :], ACT.Ln, bias=1.0).then_inc(s_gln, 1)

            def rows_exp():
                act.wait_ge(s_mt, 1)
                A(R[1][:, :], R[1][:, :], ACT.Exp, scale=-1.0).then_inc(s_emn, 1)
                act.wait_ge(s_wsl, 1)
                A(R[5][:, :], R[5][:, :], ACT.Exp).then_inc(s_ws, 1)
                act.wait_ge(s_al, 2)
                A(atr[:, :], atr[:, :], ACT.Exp).then_inc(s_aex, 1)
                A(ael, ael, ACT.Exp).then_inc(s_aex, 1)

            for n in range(8):
                t = 8 * Q_QK + n
                if n == 0:
                    rows_log()
                if n == 2:
                    rows_exp()
                if n < 4:
                    A(qT[:, n, :], tile(t), ACT.Copy).then_inc(s_ev[0], 1)
                else:
                    A(kT[:, n - 4, :], tile(t), ACT.Copy, scale=DK ** -0.5).then_inc(s_ev[0], 1)
                split(t + 4)
            for n in range(8):
                t = 8 * Q_V + n
                o = tile(t)
                if n >= 2:
                    act.wait_ge(s_vt, n - 1)
                A(FR[n % 2][:, :], o, ACT.Copy).then_inc(s_ev[0], 1)
                split(t + 4)

            def h_rounded(h):
                act.wait_ge(s_hg, h + 1)
                A(HH[:, h, :], hg[:, :], ACT.Copy).then_inc(s_hh, 1)

            for h in range(H):
                t = 8 * Q_O + h
                act.wait_ge(s_D, h + 1)
                e = E[h % 2]
                A(e[:, 0:256], e[:, 0:256], ACT.Exp, bias=cols[:, h:h + 1], scale=-1.0)
                A(e[:, 256:384], e[:, 256:384], ACT.Exp, bias=cols[:, 8 + h:9 + h], scale=-1.0)
                A(e[0:64, 384:448], e[0:64, 384:448], ACT.Exp, bias=cols[0:64, 16 + h:17 + h], scale=-1.0)\
                    .then_inc(s_E, 1)
                if h >= 1:
                    h_rounded(h - 1)
                o = tile(t)
                if h >= 2:
                    act.wait_ge(s_hg, h - 1)
                A(eo[h % 2][:, :], o, ACT.Exp, scale=-1.0).then_inc(s_ev[0], 1)
                act.wait_ge(s_emp, h + 1)
                if h >= 1:
                    act.wait_ge(s_hg, h)
                A(emS[:, :], ps[4][:, 0:T], ACT.Copy).then_inc(s_emc, 1)
                split(t + 4)
            h_rounded(H - 1)
            outs = [0]

            def store(dst, src):
                act.dma_start(dst, src, allow_slow_non_contiguous=True).then_inc(s_out, 16)
                outs[0] += 1

            for n in range(8):
                t = 8 * Q_WOA + n
                split(t + 4)
                if n == 5:
                    act.wait_ge(s_np, 1)
                    A(npr[:, :], ps[4][0:1, :], ACT.Copy)
                    A(Wst[:, :], ps[3][:, :], ACT.Copy).then_inc(s_nadd, 1)
                    act.wait_ge(s_nadd, 2)
                    for h2 in range(2):
                        act.dma_start(p_C[0, 0].rearrange("(j t) k v -> t k j v", t=2)[h2],
                                      Wst[64 * h2:64 * h2 + 64, :].rearrange("p (j v) -> p j v", j=4)).then_inc(s_po, 16)
                    act.dma_start(p_n[0, 0].rearrange("h k -> (h k)").unsqueeze(0), npr[:, :]).then_inc(s_po, 16)
                    act.dma_start(s_n[0].rearrange("b h k -> b (h k)"), nout[:, :]).then_inc(s_po, 16)
                if n == 2:
                    act.wait_ge(s_nm, 1)
                    store(p_m[0, 0:1, :].rearrange("a h -> h a"), mnew[:, 0:1])
                    store(s_m[0].rearrange("b h -> h b"), mnew[:, 1:9])
            for j in range(4):
                act.wait_ge(s_cadd, 2 * j + 2)
                for h2 in range(2):
                    act.dma_start(s_C[0, :, 2 * j + h2].rearrange("b k v -> k b v"),
                                  C0[64 * h2:64 * h2 + 64, j, :, :]).then_inc(s_co, 16)

            def ln(l, last=False):
                act.wait_ge(s_var, l + 1)
                own(A(rs[:, :], var[:, :], ACT.Ln))
                A(rs[:, :], rs[:, :], ACT.Exp, scale=-0.5).then_inc(s_rs, 1)
                for n in range(8):
                    if n % 2 == 0:
                        act.wait_ge(s_t, 4 * l + n // 2 + 1)
                    g, b = lnT[:, 8 * l + n:8 * l + n + 1], lnT[:, 32 + 8 * l + n:33 + 8 * l + n]
                    src = LT[(n // 2) % 2][:, n % 2, :]
                    if last:
                        A(X[:, n, :], src, ACT.Identity, bias=b, scale=g).then_inc(s_F, 1)
                    else:
                        A(XH[:, n, :], src, ACT.Identity, bias=b, scale=g).then_inc(s_xh, 1)
                        if n >= 2:
                            act.wait_ge(s_al2, 8 * l + n - 1)
                            act.wait_ge(s_xl, (8, 16, 32)[l] + n - 1)
                        A(FR[n % 2][:, :], src, ACT.Identity, bias=b, scale=g).then_inc(s_F, 1)

            def mlp(q0):
                with act.Fori(0, 4) as g:
                    mlp_round(8 * q0, q0, g, 8)

            def mlp_last(q0):
                with act.Fori(0, 3) as g:
                    mlp_round(8 * q0, q0, g, 8)
                mlp_round(8 * q0, q0, 3, 4)

            def mlp_round(up0, q0, g, splits):
                sq0 = 8 * UPS.index(q0)
                for n in range(8):
                    t = up0 + n
                    o = tile(t, g)
                    if n >= 2:
                        act.wait_ge(s_sq, (sq0 + n - 1) + 8 * g)
                    A(FR[n % 2][:, :], o, ACT.Relu).then_inc(s_ev[0], 1)
                    split(t + 4, g)
                    act.wait_ge(s_sq, sq0 + n + 1 + 8 * g)
                    A(HH[:, n, :], FS[n % 2][:, :], ACT.Copy).then_inc(s_hh, 1)
                for n in range(splits):
                    split(up0 + 8 + n + 4, g)

            ln(0)
            act.wait_ge(s_al2, 8)
            mlp(Q_MLP0)
            ln(1)
            act.wait_ge(s_al2, 16)
            act.wait_ge(s_po, 16 * 4)
            act.wait_ge(s_out, 16 * outs[0])

            def kv_out(i):
                act.wait_ge(s_tp, i + 1)
                if i >= 2:
                    act.wait_ge(s_to[i % 2], 32 * (i // 2))
                A(KO[i % 2][:, 0:2, :], ps[4 + i % 2][:, 0:256].rearrange("p (t c) -> p t c", t=2), ACT.Copy)
                A(KO[i % 2][0:64, 2, :], ps[4 + i % 2][0:64, 256:384], ACT.Copy).then_inc(s_tc, 1)
                act.wait_ge(s_tc, i + 1)
                act.dma_start(p_k[0, :, i, :].rearrange("(t p) d -> p t d", p=128), KO[i % 2][:, 0:2, :])\
                    .then_inc(s_to[i % 2], 16)
                act.dma_start(s_k_rows[:, i, :], KO[i % 2][0:64, 2, :]).then_inc(s_to[i % 2], 16)

            s_k_rows = s_k_d.rearrange("b t h d -> (b t) h d")
            for n in range(8):
                t = 8 * Q_WK + n
                A(KA[:, n, :], tile(t), ACT.Copy).then_inc(s_ev[0], 1)
                split(t + 4)
                if n >= 1:
                    kv_out(n - 1)
            for n in range(8):
                t = 8 * Q_WV + n
                o = tile(t)
                if n >= 2:
                    act.wait_ge(s_tp, 8 + n - 1)
                A(FR[n % 2][:, :], o, ACT.Copy).then_inc(s_ev[0], 1)
                split(t + 4)
                if n == 0:
                    kv_out(7)

            def p_exp(h):
                act.wait_ge(s_pmx, h + 1)
                pl, st = PL[h % 2], pst[:, 8 * h:8 * h + 8]
                A(pl[:, 0:128], pl[:, 0:128], ACT.Exp, bias=st[:, 0:1], accum_out=st[:, 2:3])
                A(pl[:, 128:384], pl[:, 128:384], ACT.Exp, bias=st[:, 1:2], accum_out=st[:, 3:4]).then_inc(s_pex, 1)

            def p_copy(h):
                act.wait_ge(s_pT, h + 1)
                if h >= 2:
                    act.wait_ge(s_pV, h - 1)
                A(PTt[h % 2][:, :], ps[3][:, 0:384], ACT.Copy).then_inc(s_pTc, 1)

            def p_step(i):
                if 0 <= i - 2 < H:
                    act.wait_ge(s_pV, i - 2 + 1)
                    A(AT[:, i - 2, :], ps[6][:, 0:256], ACT.Copy).then_inc(s_pA, 1)
                if 0 <= i - 1 < H:
                    p_copy(i - 1)
                if 0 <= i < H:
                    p_exp(i)

            for n in range(8):
                t = 8 * Q_WQ + n
                A(QA[:, n, :], tile(t), ACT.Copy, scale=QSCALE).then_inc(s_ev[0], 1)
                split(t + 4)
                p_step(n - 1)
                if n == 3:
                    act.wait_ge(s_tv, 8)
                    store(p_v[0].rearrange("(t p) h d -> p t (h d)", p=128), VT[:, 0:2, :])
                    store(s_v_d.rearrange("b t h d -> (b t) (h d)"), VT[0:64, 2, :])
            for i in range(7, 10):
                p_step(i)

            def q_lay(G):
                if G == 0:
                    act.wait_ge(s_qzz, 1)
                else:
                    act.wait_ge(s_sc, 16 * G)
                for bb in range(4):
                    ins = A(QZ[:, :, bb, 8 * bb:8 * bb + 8],
                            QA[:, :, TP + 32 * G + 8 * bb:TP + 32 * G + 8 * bb + 8], ACT.Copy)
                ins.then_inc(s_qz, 1)

            def k_copy(P):
                act.wait_ge(s_ktr, P + 1)
                if P >= 4:
                    act.wait_ge(s_sc, P // 2 - 1)
                A(KT[P // 2 % 2][:, 0:4, 128 * (P % 2):128 * (P % 2) + 128],
                  ps[2 * (P % 2)][:, :].rearrange("p (h t) -> p h t", h=4), ACT.Copy).then_inc(s_kA, 1)

            def exps(G):
                act.wait_ge(s_sm, G + 1)
                for a_ in range(2):
                    A(PO[:, a_, :], PO[:, a_, :], ACT.Exp, bias=nbo[:, a_:a_ + 1],
                      accum_out=acc[:, 5 * a_ + 4:5 * a_ + 5]).then_inc(s_ex, 1)
                for m in range(8):
                    a_, n = m // 4, m % 4
                    c = L[:, a_, 256 * n:256 * n + 256]
                    A(c, c, ACT.Exp, bias=nb[:, m:m + 1], accum_out=acc[:, 5 * a_ + n:5 * a_ + n + 1])\
                        .then_inc(s_ex, 1)

            def out_copy(G):
                act.wait_ge(s_ot, G + 1)
                for bb in range(4):
                    b = 4 * G + bb
                    src = ps[6 + bb // 2][:, 256 * (bb % 2):256 * (bb % 2) + 256]\
                        .rearrange("p (h r) -> p h r", h=8)[:, :, 8 * bb:8 * bb + 8]
                    ins = A(AO[:, :, 8 * b:8 * b + 8], src, ACT.Copy)
                ins.then_inc(s_ao, 1)

            for G in range(2):
                q_lay(G)
                for P in range(32 * G, 32 * G + 32):
                    k_copy(P)
                    if P == 33:
                        out_copy(0)
                exps(G)
            out_copy(1)
            act.wait_ge(s_ao, 2)
            for n in range(8):
                A(XH[:, n, 0:TP], AT[:, n, :], ACT.Copy)
                A(XH[:, n, TP:T], AO[:, n, :], ACT.Copy).then_inc(s_xh, 1)
            for n in range(8):
                split(8 * Q_WOB + n + 4)
            ln(2)
            act.wait_ge(s_al2, 24)
            mlp_last(Q_MLP1)
            ln(3, True)
            ys = y_sample.rearrange("b t c -> (b t) c")
            for n in range(8):
                i = 16 + n
                act.wait_ge(s_tp, i + 1)
                act.wait_ge(s_to[n % 2], 32 * 4 + 32 * (n // 2))
                A(KO[n % 2][:, 0:2, :], ps[4 + n % 2][:, 0:256].rearrange("p (t c) -> p t c", t=2), ACT.Copy)
                A(KO[n % 2][0:64, 2, :], ps[4 + n % 2][0:64, 256:384], ACT.Copy).then_inc(s_tc, 1)
                act.wait_ge(s_tc, 8 + n + 1)
                act.dma_start(y_prompt[0, :, 128 * n:128 * n + 128].rearrange("(t p) d -> p t d", p=128),
                              KO[n % 2][:, 0:2, :]).then_inc(s_to[n % 2], 16)
                act.dma_start(ys[:, 128 * n:128 * n + 128], KO[n % 2][0:64, 2, :]).then_inc(s_to[n % 2], 16)
            for i in range(2):
                act.wait_ge(s_to[i], 32 * 8)
            act.wait_ge(s_out, 16 * outs[0])

        @block.vector
        def _(dve):
            V = nc.vector
            own = Own(dve, s_d)

            def split(t, turn=0):
                dve.wait_ge(s_hi, t + 1 + 16 * turn)
                V.tensor_tensor(WL[t % SPL][:, :, :], raw[(t // 2) % RAW][:, :, 128 * (t % 2):128 * (t % 2) + 128],
                                WH[t % SPL][:, :, :].bitcast(F32), ALU.subtract).then_inc(s_lo, 1)

            V.memset(VT[64:128, 2, :], 0.0)
            V.memset(WGH[:, :, :].bitcast(F32), 0.0)
            V.memset(WGL[:, :, :].bitcast(F32), 0.0).then_inc(s_gz, 1)
            for n in range(8):
                dve.wait_ge(s_xt, n + 1)
                V.tensor_copy(X[:, n, :], ps[2 + n % 2][:, 0:T]).then_inc(s_xf, 1)
                dve.wait_ge(s_xf, n + 1)
                dve.wait_ge(s_xh, n + 1)
                V.tensor_tensor(XL[:, n, :], X[:, n, :], XH[:, n, :].bitcast(F32), ALU.subtract).then_inc(s_xl, 1)
                if n == 3:
                    dve.wait_ge(s_gh, 1)
                    dve.wait_ge(s_gz, 1)
                    V.tensor_tensor(WGL[:, :, 0:8], wgraw[:, :, 0:8], WGH[:, :, 0:8].bitcast(F32), ALU.subtract)
                    V.tensor_tensor(WGL[:, :, 32:40], wgraw[:, :, 8:16], WGH[:, :, 32:40].bitcast(F32),
                                    ALU.subtract).then_inc(s_gl, 1)
            for t in range(3):
                split(t)
            dve.wait_ge(s_lnt, 1)
            V.tensor_copy(lnT[:, :], ps[4][:, 0:64]).then_inc(s_lnc, 1)

            dve.wait_ge(s_gp, 1)
            for w in W:
                V.memset(w[64:128, 384:448], 0.0)
            dve.wait_ge(s_m0, 48)
            dve.wait_ge(s_ml, 32)
            ends = slice(TP + LS - 1, T, LS)
            starts = slice(TP, T, LS)
            V.tensor_scalar(R[0][:, :], ps[5][0:8, 0:T], bg[0:8, 0:1], None, ALU.add)
            own(V.tensor_scalar(R[1][:, :], ps[5][32:40, 0:T], bg[32:40, 0:1], None, ALU.add))
            V.scalar_tensor_tensor(R[2][:, :], R[1][:, :], -1.0, R[1][:, :], ALU.mult, ALU.max).then_inc(s_gabs, 1)
            dve.wait_ge(s_gln, 1)
            own(V.scalar_tensor_tensor(R[1][:, :], R[1][:, :], 0.0, R[2][:, :], ALU.min, ALU.subtract))
            rst, neg = cml[0:8, 448:448 + T], cml[0:8, 448 + T:448 + 2 * T]
            own(V.tensor_tensor_scan(R[3][:, :], rst, R[1][:, :], 0.0, ALU.mult, ALU.add))
            own(V.tensor_tensor(R[4][:, :], R[0][:, :], R[3][:, :], ALU.subtract))
            own(V.tensor_copy(R[0][:, :], R[4][:, :]))
            V.tensor_scalar(R[0][:, 0:1], R[4][:, 0:1], 0.0, None, ALU.max)
            own(V.tensor_tensor(R[0][:, starts], R[4][:, starts], m0, ALU.max))
            own(V.tensor_tensor_scan(R[2][:, :], neg, R[0][:, :], 0.0, ALU.add, ALU.max))
            V.tensor_tensor(R[1][:, :], R[3][:, :], R[2][:, :], ALU.add).then_inc(s_mt, 1)
            V.tensor_scalar(R[5][:, 0:TP], R[4][:, 0:TP], R[2][:, TP - 1:TP], None, ALU.subtract)
            V.tensor_tensor(R[5][:, TP:T].rearrange("p (b t) -> p b t", t=LS),
                            R[4][:, TP:T].rearrange("p (b t) -> p b t", t=LS),
                            bcast(R[2][:, ends], 2, LS), ALU.subtract).then_inc(s_wsl, 1)
            V.tensor_tensor(atr[:, :].rearrange("p (b t) -> p b t", t=LS), bcast(m0, 2, LS),
                            R[2][:, TP:T].rearrange("p (b t) -> p b t", t=LS), ALU.subtract).then_inc(s_al, 1)
            V.tensor_tensor(ael, m0, R[2][:, ends], ALU.subtract).then_inc(s_al, 1)
            V.tensor_tensor(mnew[:, 0:1], R[3][:, TP - 1:TP], R[2][:, TP - 1:TP], ALU.add)
            V.tensor_tensor(mnew[:, 1:9], R[3][:, ends], R[2][:, ends], ALU.add).then_inc(s_nm, 1)

            for n in range(8):
                split(8 * Q_QK + n + 3)
            dve.wait_ge(s_colp, 1)
            c7 = ps[7]
            V.tensor_copy(cols[:, 0:16], c7[:, 0:16])
            V.tensor_copy(cols[0:64, 16:24], c7[0:64, 16:24])
            V.tensor_copy(cols[:, 24:40], c7[:, 24:40])
            V.tensor_copy(cols[0:64, 40:48], c7[0:64, 40:48])
            V.tensor_copy(cols[0:8, 48:56], c7[0:8, 48:56]).then_inc(s_col, 1)
            V.tensor_copy(aeP[:, :, :], c7[:, 320:352].rearrange("p (j b) -> p j b", j=4))
            dve.wait_ge(s_ev[0], evac(8 * Q_QK + 3)[1])
            V.tensor_tensor(aqT[:, :, :], qT[:, :, TP:T], c7[:, 64:320].rearrange("p (j t) -> p j t", j=4),
                            ALU.mult).then_inc(s_bc, 1)
            dve.wait_ge(s_bc, 1)
            V.tensor_tensor(an[:, :, :].rearrange("p j (b t) -> p (j b) t", t=LS),
                            aqT[:, :, :].rearrange("p j (b t) -> p (j b) t", t=LS),
                            bcast(c7[:, 352:384], 2, LS), ALU.mult).then_inc(s_bc, 1)

            def v_copy(n, done, bank):
                c = slice(128 * n, 128 * n + 128)
                V.tensor_copy(VT[:, 0:2, c], bank[:, 0:256].rearrange("p (t c) -> p t c", t=2))
                V.tensor_copy(VT[0:64, 2, c], bank[0:64, 256:384]).then_inc(done, 1)

            for n in range(8):
                split(8 * Q_V + n + 3)
                if n >= 1:
                    dve.wait_ge(s_vt, n)
                    v_copy(n - 1, s_vc, ps[4 + (n - 1) % 2])
            dve.wait_ge(s_vt, 8)
            v_copy(7, s_vc, ps[5])

            def decay(h):
                dve.wait_ge(s_sp, h + 1)
                e = E[h % 2]
                V.tensor_tensor(e[:, 0:256], ps[3][:, 0:256], cml[:, 0:256], ALU.add)
                V.tensor_tensor(e[:, 256:384], ps[3][:, 128:256], cml[:, 256:384], ALU.add)
                V.tensor_tensor(e[0:64, 384:448], ps[3][0:64, 256:320], cml[0:64, 384:448], ALU.add)\
                    .then_inc(s_D, 1)

            def weights(h):
                dve.wait_ge(s_E, h + 1)
                if h >= 2:
                    dve.wait_ge(s_num, h - 1)
                w, e = W[h % 2], E[h % 2]
                V.tensor_tensor(w[:, 0:384], ps[2][:, 0:384], e[:, 0:384], ALU.mult)
                V.tensor_tensor(w[0:64, 384:448], ps[2][0:64, 384:448], e[0:64, 384:448], ALU.mult)\
                    .then_inc(s_W, 1)

            def gated(h):
                dve.wait_ge(s_emc, h + 1)
                dve.wait_ge(s_num, h + 1)
                own(V.scalar_tensor_tensor(rec[:, :], ps[5][:, 0:T], -1.0, emS[:, :], ALU.mult, ALU.max))
                own(V.tensor_tensor(rec[:, :], ps[5][:, 0:T], rec[:, :], ALU.max))
                own(V.scalar_tensor_tensor(rec[:, :], eo[h % 2][:, :], 1.0, rec[:, :], ALU.add, ALU.mult))
                own(V.reciprocal(rec[:, :], rec[:, :]))
                if h >= 1:
                    dve.wait_ge(s_hh, h)
                V.tensor_tensor(hg[:, :], ps[6][:, 0:T], rec[:, :], ALU.mult).then_inc(s_hg, 1)

            def h_rest(h):
                dve.wait_ge(s_hh, h + 1)
                V.tensor_tensor(HL[:, h, :], hg[:, :], HH[:, h, :].bitcast(F32), ALU.subtract).then_inc(s_hl, 1)

            for h in range(H):
                decay(h)
                if h >= 1:
                    gated(h - 1)
                weights(h)
                if h >= 1:
                    h_rest(h - 1)
                split(8 * Q_O + h + 3)
            gated(H - 1)
            h_rest(H - 1)

            def residual(t, turn=0, scale=None):
                n = t % 8
                dve.wait_ge(s_mm, t + 1 + 16 * turn)
                if scale is None:
                    ins = V.tensor_tensor(X[:, n, :], X[:, n, :], ps[t % 2][:, 0:T], ALU.add)
                else:
                    ins = V.scalar_tensor_tensor(X[:, n, :], X[:, n, :], scale, ps[t % 2][:, 0:T], ALU.mult, ALU.add)
                ins.then_inc(s_ev[1], 1)

            def state(i):
                if i < 4:
                    dve.wait_ge(s_kt, i + 1)
                    for w, bt, lo in ((128, slice(0, 2), 24), (64, slice(2, 3), 40)):
                        nt = bt.stop - bt.start
                        V.tensor_tensor(
                            wsK[0:w, bt, 128 * i:128 * i + 128].rearrange("p t (h d) -> p t h d", h=2),
                            ps[2][0:w, 128 * bt.start:128 * bt.stop].rearrange("p (t h d) -> p t h d", t=nt, h=2),
                            bcast(cols[0:w, lo:lo + 8 * nt].rearrange("p (t h) -> p t h", t=nt)[:, :, 2 * i:2 * i + 2],
                                  3, 64), ALU.mult).then_inc(s_wk, 1)
                if i == 5:
                    dve.wait_ge(s_np, 1)
                    own(V.tensor_tensor(nout[:, :].rearrange("p (h k) -> p h k", h=8),
                                        n0[:, :].rearrange("p (h k) -> p h k", h=8),
                                        bcast(cols[0:8, 48:56], 2, DK), ALU.mult))
                    V.tensor_tensor(nout[:, :], nout[:, :], ps[5][0:8, :], ALU.add).then_inc(s_nadd, 1)
                if i >= 5:
                    c_add(i - 5)

            def c_add(j):
                dve.wait_ge(s_cae, 4)
                for half in range(2):
                    dve.wait_ge(s_cp, 2 * j + half + 1)
                    c = C0[:, j, 4 * half:4 * half + 4, :]
                    V.tensor_tensor(c, c, ps[6 + half][:, :].rearrange("p (b v) -> p b v", b=4), ALU.add)\
                        .then_inc(s_cadd, 1)

            for n in range(8):
                residual(8 * Q_WOA + n, 0, ALPHA)
                split(8 * Q_WOA + n + 3)
                state(n)
            c_add(3)

            def ln(l, last=False):
                dve.wait_ge(s_lnp, l + 1)
                if l == 0:
                    dve.wait_ge(s_po, 16 * 4)
                own(V.tensor_scalar(mu[:, :], ps[2][:, 0:T], 1.0 / DM, None, ALU.mult))
                own(V.tensor_tensor(tmp[:, :], mu[:, :], mu[:, :], ALU.mult))
                own(V.scalar_tensor_tensor(var[:, :], ps[3][:, 0:T], 1.0 / DM, tmp[:, :], ALU.mult, ALU.subtract))
                V.tensor_scalar(var[:, :], var[:, :], 0.0, EPS, ALU.max, ALU.add).then_inc(s_var, 1)
                dve.wait_ge(s_rs, l + 1)
                own(V.scalar_tensor_tensor(tmp[:, :], rs[:, :], -0.5, var[:, :], ALU.mult, ALU.mult))
                own(V.tensor_tensor(tmp[:, :], tmp[:, :], rs[:, :], ALU.mult))
                own(V.scalar_tensor_tensor(rs[:, :], tmp[:, :], 1.5, rs[:, :], ALU.add, ALU.mult))

                def rest(n):
                    dve.wait_ge(s_F, 8 * l + n + 1)
                    V.tensor_tensor(XL[:, n, :], FR[n % 2][:, :], XH[:, n, :].bitcast(F32), ALU.subtract)\
                        .then_inc(s_xl, 1)

                for m in range(4):
                    if m >= 2:
                        dve.wait_ge(s_F, 8 * l + 2 * m - 2)
                    own(V.tensor_tensor(LT[m % 2][:, :, :], X[:, 2 * m:2 * m + 2, :], bcast(mu[:, :], 1, 2),
                                        ALU.subtract))
                    V.tensor_tensor(LT[m % 2][:, :, :], LT[m % 2][:, :, :], bcast(rs[:, :], 1, 2), ALU.mult)\
                        .then_inc(s_t, 1)
                    if m >= 1 and not last:
                        rest(2 * m - 2)
                        rest(2 * m - 1)
                if not last:
                    rest(6)
                    rest(7)
                    dve.wait_ge(s_al2, 8 * l + 8)

            def mlp_round(q0, g, splits):
                c0 = 8 * UPS.index(q0)
                for n in range(8):
                    t = 8 * q0 + n
                    dve.wait_ge(s_ev[0], evac(t)[1] + 8 * g)
                    if n >= 2:
                        dve.wait_ge(s_hh, 8 + c0 + n - 1 + 8 * g)
                    V.tensor_tensor(FS[n % 2][:, :], FR[n % 2][:, :], FR[n % 2][:, :], ALU.mult).then_inc(s_sq, 1)
                    split(t + 3, g)
                    dve.wait_ge(s_hh, 8 + c0 + n + 1 + 8 * g)
                    V.tensor_tensor(HL[:, n, :], FS[n % 2][:, :], HH[:, n, :].bitcast(F32), ALU.subtract)\
                        .then_inc(s_hl, 1)
                for n in range(8):
                    residual(8 * q0 + 8 + n, g)
                    if n < splits:
                        split(8 * q0 + 8 + n + 3, g)

            ln(0)
            with dve.Fori(0, 4) as g:
                mlp_round(Q_MLP0, g, 8)
            ln(1)
            for n in range(8):
                split(8 * Q_WK + n + 3)
            for n in range(8):
                split(8 * Q_WV + n + 3)
                if n >= 1:
                    dve.wait_ge(s_tp, 8 + n)
                    v_copy(n - 1, s_tv, ps[4 + (n - 1) % 2])
            dve.wait_ge(s_at, 16)

            def p_max(h):
                dve.wait_ge(s_pS, h + 1)
                if h >= 2:
                    dve.wait_ge(s_pT, h - 1)
                pl, st = PL[h % 2], pst[:, 8 * h:8 * h + 8]
                own(V.scalar_tensor_tensor(pl[:, :], dist, SLOPES[h], ps[2][:, 0:384], ALU.mult, ALU.add))
                V.tensor_reduce(st[:, 0:1], pl[:, 0:128], AX.X, ALU.max, negate=True)
                V.tensor_reduce(st[:, 1:2], pl[:, 128:384], AX.X, ALU.max, negate=True).then_inc(s_pmx, 1)

            def p_norm(h):
                dve.wait_ge(s_pex, h + 1)
                pl, st = PL[h % 2], pst[:, 8 * h:8 * h + 8]
                own(V.reciprocal(st[:, 4:6], st[:, 2:4]))
                V.tensor_scalar(pl[:, 0:128], pl[:, 0:128], st[:, 4:5], None, ALU.mult).then_inc(s_pnm, 1)
                V.tensor_scalar(pl[:, 128:384], pl[:, 128:384], st[:, 5:6], None, ALU.mult).then_inc(s_pnm, 1)

            def p_step(i):
                if 0 <= i < H:
                    p_max(i)
                if 0 <= i < H:
                    p_norm(i)

            for n in range(8):
                split(8 * Q_WQ + n + 3)
                if n == 0:
                    dve.wait_ge(s_tp, 16)
                    v_copy(7, s_tv, ps[5])
                p_step(n - 1)
            for i in range(7, 10):
                p_step(i)
            V.memset(QZ[:, :, :, :], 0.0).then_inc(s_qzz, 1)

            def k_copy(P):
                dve.wait_ge(s_ktr, P + 1)
                if P >= 4:
                    dve.wait_ge(s_sc, P // 2 - 1)
                V.tensor_copy(KT[P // 2 % 2][:, 4:8, 128 * (P % 2):128 * (P % 2) + 128],
                              ps[2 * (P % 2) + 1][:, :].rearrange("p (h t) -> p h t", h=4)).then_inc(s_kD, 1)

            def softmax(G):
                dve.wait_ge(s_sc, 16 * G + 16)
                for c in range(4):
                    V.tensor_reduce(bsum[:, 2 * c:2 * c + 2], ps[4 + c][:, :].rearrange("p (n k) -> p n k", n=2),
                                    AX.X, ALU.add)
                    V.scalar_tensor_tensor(L[:, c // 2, 512 * (c % 2):512 * (c % 2) + 512],
                                           keys[:, 512 * (c % 2):512 * (c % 2) + 512], slope[:, c // 2:c // 2 + 1],
                                           ps[4 + c][:, :], ALU.mult, ALU.add)
                dve.wait_ge(s_own, G + 1)
                own(V.tensor_tensor(PO[:, :, :].rearrange("p a k -> p (a k)"), ps[0][:, 0:128],
                                    bias_own[:, 128 * G:128 * G + 128], ALU.add))
                an_ = "p (a n) -> p a n"
                V.tensor_reduce(mxb, L[:, :, :].rearrange("p a (n k) -> p (a n) k", n=4), AX.X, ALU.max)
                V.tensor_reduce(omx, PO[:, :, :], AX.X, ALU.max)
                own(V.tensor_reduce(mn, bsum.rearrange(an_, a=2), AX.X, ALU.min))
                own(V.tensor_tensor(pen.rearrange(an_, a=2), bsum.rearrange(an_, a=2), bcast(mn, 2, 4), ALU.is_le))
                own(V.tensor_tensor(pen, pen, nidx, ALU.mult))
                own(V.tensor_reduce(ix, pen.rearrange(an_, a=2), AX.X, ALU.max))
                own(V.tensor_tensor(pen.rearrange(an_, a=2), nidx.rearrange(an_, a=2), bcast(ix, 2, 4), ALU.is_equal))
                own(V.tensor_scalar(pen, pen, -BIG, None, ALU.mult))
                own(V.tensor_tensor(mxb, mxb, pen, ALU.add))
                own(V.tensor_reduce(m2, mxb.rearrange(an_, a=2), AX.X, ALU.max))
                own(V.tensor_tensor(m2, m2, omx, ALU.max))
                V.tensor_scalar(nbo, m2, -1.0, None, ALU.mult)
                V.tensor_tensor(nb.rearrange(an_, a=2), pen.rearrange(an_, a=2), bcast(m2, 2, 4), ALU.subtract)\
                    .then_inc(s_sm, 1)
                if G == 0:
                    for i in range(2):
                        dve.wait_ge(s_to[i], 32 * 4)
                dve.wait_ge(s_ptt, 5 * G + 1)
                V.tensor_copy(PTo[:, :, :], ps[1][0:64, 0:256].rearrange("p (a r) -> p a r", a=2)).then_inc(s_ptc, 1)
                for c in range(4):
                    dve.wait_ge(s_ptt, 5 * G + c + 2)
                    V.tensor_copy(PT[:, 4 * c:4 * c + 4, :], ps[4 + c % 2][:, :].rearrange("p (m r) -> p m r", m=4))\
                        .then_inc(s_ptc, 1)
                own(V.tensor_reduce(den, acc.rearrange("p (a n) -> p a n", a=2), AX.X, ALU.add))
                own(V.reciprocal(rden, den))
                dve.wait_ge(s_pv, 32 * G + 32)
                for c in range(4):
                    bb, a_ = 2 * (c // 2), c % 2
                    ins = V.tensor_scalar(ON[:, bb:bb + 2, a_, :],
                                          ps[6 + c // 2][:, :].rearrange("p (b a d) -> p b a d", b=2, a=2)[:, :, a_, :],
                                          rden[:, a_:a_ + 1], None, ALU.mult)
                ins.then_inc(s_on, 1)

            for G in range(2):
                for P in range(32 * G, 32 * G + 32):
                    k_copy(P)
                softmax(G)
            for n in range(8):
                dve.wait_ge(s_xh, 8 * 3 + n + 1)
                V.tensor_tensor(XL[:, n, 0:TP], AT[:, n, :], XH[:, n, 0:TP].bitcast(F32), ALU.subtract)
                V.tensor_tensor(XL[:, n, TP:T], AO[:, n, :], XH[:, n, TP:T].bitcast(F32), ALU.subtract)\
                    .then_inc(s_xl, 1)
            for n in range(8):
                residual(8 * Q_WOB + n)
                split(8 * Q_WOB + n + 3)
            ln(2)
            with dve.Fori(0, 3) as g:
                mlp_round(Q_MLP1, g, 8)
            mlp_round(Q_MLP1, 3, 5)
            ln(3, True)

        @block.gpsimd
        def _(pool):
            G = nc.gpsimd
            own = Own(pool, s_p)

            def sums(l, q, n):
                pool.wait_ge(s_ev[1], evac(8 * q + n)[1])
                if n == 0:
                    G.tensor_copy(A1[:, :], X[:, 0, :])
                    own(G.tensor_tensor(A2[:, :], X[:, 0, :], X[:, 0, :], ALU.mult))
                else:
                    own(G.tensor_tensor(SQ[:, :], X[:, n, :], X[:, n, :], ALU.mult))
                    G.tensor_tensor(A1[:, :], A1[:, :], X[:, n, :], ALU.add)
                    own(G.tensor_tensor(A2[:, :], A2[:, :], SQ[:, :], ALU.add))
                if n == 7:
                    G.tensor_copy(SQ[:, 0:1], A2[:, 0:1]).then_inc(s_st, 1)

            def scaled(l):
                for n in range(8):
                    pool.wait_ge(s_F, 8 * l + n + 1)
                    G.tensor_scalar(X[:, n, :], FR[n % 2][:, :], ALPHA, 1.0, ALU.mult, ALU.mult).then_inc(s_al2, 1)

            pool.wait_ge(s_num, H)
            for j in range(4):
                c = C0[:, j, :, :]
                G.tensor_tensor(c, c, bcast(aeP[:, j, :], 2, 128), ALU.mult).then_inc(s_cae, 1)

            def masked(j):
                if j == 0:
                    pool.wait_ge(s_wk, 8)
                else:
                    pool.wait_ge(s_cp, 2 * j)
                G.tensor_tensor(wsKm[:, :, :], bcast(wsK[0:64, 2, 128 * j:128 * j + 128], 1, NB),
                                bcast(bmask[0:64, :], 2, 128), ALU.mult).then_inc(s_km, 1)

            for n in range(8):
                sums(0, Q_WOA, n)
                if n >= 3 and n < 7:
                    masked(n - 3)
            scaled(0)
            for n in range(8):
                sums(1, Q_WK - 1, n)
            scaled(1)

            for n in range(8):
                sums(2, Q_WOB, n)
            scaled(2)
            for n in range(8):
                sums(3, N_QUADS - 1, n)


INS = ["x_prompt", "x_sample", "state_C", "state_n", "state_m", "cache_k", "cache_v", "page_table", "w_in_a",
       "b_gate_a", "w_out_a", "w_q_b", "w_out_b", "w_kv", "w_up", "w_down", "ln_g", "ln_b"]
OUTS = [(1, TP, DM), (NB, LS, DM), (1, 1, H, DK, 128), (1, 1, H, DK), (1, 1, H), (1, TP, H, 128), (1, TP, H, 128),
        (1, NB, H, DK, 128), (1, NB, H, DK), (1, NB, H), (NB, LS, H, 128), (NB, LS, H, 128)]


def kernel(**inputs):
    import concourse.bacc as bacc
    from concourse.bass_utils import run_bass_kernel_spmd

    nc = bacc.Bacc("TRN2", target_bir_lowering=False, num_devices=1)
    named = {n: np.ascontiguousarray(inputs[n]) for n in INS}
    named.update(constants())
    arrays, args = {}, []
    for name, a in named.items():
        arrays[f"in_{name}_dram"] = a
        args.append(nc.dram_tensor(f"in_{name}_dram", a.shape, mybir.dt.from_np(a.dtype), kind="ExternalInput").ap())
    for i, shape in enumerate(OUTS):
        args.append(nc.dram_tensor(f"out_{i}_dram", shape, F32, kind="ExternalOutput").ap())
    build(nc, *args)
    r = run_bass_kernel_spmd(nc, [arrays], core_ids=[0])
    return tuple(r.results[0][f"out_{i}_dram"] for i in range(len(OUTS)))
```

```python
import numpy as np
import concourse.bass as bass
from concourse import mybir
from contextlib import ExitStack

F32 = mybir.dt.float32
F32R = mybir.dt.float32r
I32 = mybir.dt.int32
ALU = mybir.AluOpType
ACT = mybir.ActivationFunctionType
AX = mybir.AxisListType

DM = 1024
NC8 = DM // 128
TP, TS = 256, 64
T = TP + TS
RING = 12
NB, LS = 8, 8
H = 8
DK = 64
PAGES = 8
PG = 128
NPG = NB * PAGES
BIG = 1.0e30
ALPHA = 4.0 ** 0.25
EPS = 1e-5
QSCALE = 128.0 ** -0.5

Q_QK, Q_V, Q_O, Q_WOA, Q_MLP0, Q_WK, Q_WV, Q_WQ, Q_WOB, Q_MLP1, N_QUADS = 0, 1, 2, 3, 4, 12, 13, 14, 15, 16, 24
FIRST = 2
SIDE_BY_SIDE = (Q_MLP0, Q_WK, Q_MLP1)
UPS = [Q_MLP0 + 2 * g for g in range(4)] + [Q_MLP1 + 2 * g for g in range(4)]
ACT_QUADS = sorted([Q_QK, Q_V, Q_O, Q_WK, Q_WV, Q_WQ] + UPS)
NT = 8 * N_QUADS
RAW, SPL = 4, 4

SLOPES = [2.0 ** -(h + 1) for h in range(H)]


def constants():
    p = np.arange(128)
    ident = np.eye(128, dtype=np.float32)
    ones = np.ones((128, 128), np.float32)
    m = np.full((128, 448), 0.0, np.float32)
    t = np.arange(256)
    m[:, 0:256] = np.where(p[:, None] <= t[None, :], 0, BIG)
    m[:, 256:384] = np.where(p[:, None] <= p[None, :], 0, BIG)
    s = np.arange(64)
    m[0:64, 384:448] = np.where((s[:, None] // 8 == s[None, :] // 8) & (s[:, None] <= s[None, :]), 0, BIG)
    start = np.zeros(T, bool)
    start[0] = True
    start[TP::LS] = True
    rows = np.zeros((128, 2 * T), np.float32)
    rows[:, 0:T] = np.where(start, 0, 1)
    rows[:, T:] = np.where(start, -BIG, 0)
    sel = np.zeros((128, 12 * 128), np.float32)
    for h in range(H):
        sel[h, h * 128:(h + 1) * 128] = 1
        sel[h, (8 + h // 2) * 128 + 64 * (h % 2):(8 + h // 2) * 128 + 64 * (h % 2) + 64] = 1
    d = np.zeros((128, 384), np.float32)
    d[:, 0:128] = np.where(p[None, :] <= p[:, None], p[None, :] - p[:, None], -BIG)
    d[:, 128:384] = np.where(t[None, :] <= 128 + p[:, None], t[None, :] - 128 - p[:, None], -BIG)
    sl = np.array(SLOPES)
    key = np.tile(np.arange(PAGES * PG) - PAGES * PG, (128, 1)).astype(np.float32)
    j, rb, rq = p // 32, p % 32 // 8, p % 8
    sb, sk = s // 8, s % 8
    slope = sl[4 * np.arange(2)[None, :] + j[:, None]]
    g4 = 4 * np.arange(2)
    ok = (sb[None, None, :] == rb[:, None, None] + g4[None, :, None]) & (sk[None, None, :] <= rq[:, None, None])
    bo = np.where(ok[:, :, None, :], slope[:, None, :, None] * sk[None, None, None, :], -BIG)
    bo = bo.reshape(128, 256).astype(np.float32)
    n = np.tile(np.arange(4) + 1.0, (128, 2)).astype(np.float32)
    bm = np.zeros((128, 8), np.float32)
    bm[0:64] = (sb[:, None] == np.arange(NB)[None, :])
    bm4 = np.zeros((128, 4), np.float32)
    bm4[0:64] = (sb[:, None] % 4 == np.arange(4)[None, :])
    base = np.concatenate([ident, ones, bm, bm4], 1)
    return {"c_base": base, "c_mlstm": np.concatenate([m, rows], 1), "c_sel": sel[0:8].copy(),
            "c_attn": np.concatenate([d, key, bo, slope.astype(np.float32), n], 1)}


def bcast(ap, axis, n):
    v = ap.unsqueeze(axis)
    shape = list(v.shape)
    shape[axis] = n
    return v.to_broadcast(shape)


class Own:

    def __init__(self, eng, sem):
        self.eng, self.sem, self.n, self.shift = eng, sem, 0, 0

    def __call__(self, ins):
        self.n += 1
        ins.then_inc(self.sem, 1)
        self.eng.wait_ge(self.sem, self.shift + self.n)


def evac(t):
    q = t // 8
    mine = q in ACT_QUADS
    before = sum(1 for x in range(q) if (x in ACT_QUADS) == mine)
    return (0 if mine else 1), 8 * before + t % 8 + 1


def build(nc, x_prompt, x_sample, state_C, state_n, state_m, cache_k, cache_v, page_table,
          w_in_a, b_gate_a, w_out_a, w_q_b, w_out_b, w_kv, w_up, w_down, ln_g, ln_b,
          c_base, c_mlstm, c_sel, c_attn,
          y_prompt, y_sample, p_C, p_n, p_m, p_k, p_v, s_C, s_n, s_m, s_k_d, s_v_d):
    ctx = ExitStack()
    with ctx:
        at = [nc.sbuf_base + (-nc.sbuf_base) % 64]
        top = nc.sbuf_usable_end

        def put(name, shape, dt=F32, where=at):
            size = 4 * int(np.prod(shape[1:]))
            t = nc.alloc_sbuf_tensor_at(name, shape, dt, offset=where[0])
            where[0] += size + (-size) % 32
            assert where[0] <= top, (name, where[0], top)
            return t

        raw2_at = at[0] + 2 * 8192
        raw = [put(f"raw{i}", [128, 8, 256]) for i in range(RAW)]
        WH = [put(f"w_hi{i}", [128, 8, 128], F32R) for i in range(SPL)]
        WL = [put(f"w_lo{i}", [128, 8, 128], F32R) for i in range(SPL)]
        X = put("x", [128, NC8, T])
        xh_at = at[0]
        XH = put("x_hi", [128, NC8, T], F32R)
        XL = put("x_lo", [128, NC8, T], F32R)
        qk_at = [at[0]]
        hh_at = at[0]
        HH = put("h_hi", [128, NC8, T], F32R)
        HL = put("h_lo", [128, NC8, T], F32R)
        QA = put("q_attn", [128, H, T], F32, qk_at)
        KA = put("k_attn", [128, H, T], F32, qk_at)
        VT = put("v_tok", [128, 3, DM])
        FR = [put(f"fm{i}", [128, T]) for i in range(2)]
        fs_at = at[0]
        FS = [put(f"sq{i}", [128, T]) for i in range(2)]
        A1 = put("sum_x", [128, T])
        A2 = put("sum_xx", [128, T])
        SQ = put("xx", [128, T])
        base = put("base", [128, 268])
        ident, ones, bmask = base[:, 0:128], base[:, 128:256], base[:, 256:264]
        bmask4 = base[:, 264:268]
        lnT = put("ln_cols", [128, 64])
        bg = put("b_gate", [40, 1])
        table = put("page_table", [1, NB * PAGES], I32)
        phase_const = [at[0]]
        cat = put("attn_tables", [128, 384 + 1024 + 256 + 2 + 8])
        dist, keys, bias_own = cat[:, 0:384], cat[:, 384:1408], cat[:, 1408:1664]
        slope, nidx = cat[:, 1664:1666], cat[:, 1666:1674]
        cml = put("mlstm_tables", [128, 448 + 2 * T], F32, phase_const)
        n0 = put("n0", [8, H * DK], F32, phase_const)
        assert phase_const[0] <= at[0]
        phase = at[0]

        a = [phase]
        C0 = put("C", [128, 4, NB, 128], F32, a)
        ewk = [a[0]]
        E = [put(f"decay{i}", [128, 448], F32, a) for i in range(2)]
        W = [put(f"weight{i}", [128, 448], F32, a) for i in range(2)]
        wsK = put("wsk", [128, 3, 512], F32, a)
        wgraw = put("wg_raw", [128, 8, 16], F32, ewk)
        WGH = put("wg_hi", [128, 8, 128], F32R, ewk)
        WGL = put("wg_lo", [128, 8, 128], F32R, ewk)
        lnN = put("ln_rows", [64, 128], F32, ewk)
        assert ewk[0] <= a[0]
        wst_at = [a[0]]
        Wst = put("c_prompt", [128, 512], F32, wst_at)
        kT = put("k_mlstm", [128, 4, T], F32, a)
        npr_at = [a[0]]
        npr = put("n_prompt", [1, 512], F32, npr_at)
        qT = put("q_mlstm", [128, 4, T], F32, a)
        sel = put("sel", [8, 12 * 128], F32, a)
        vm_at, az_at, cq_at = [xh_at], [hh_at], [fs_at]
        Vm = put("v_masked", [64, H, 4, 128], F32, vm_at)
        aqZ = put("aq_padded", [128, 4, NB, 32], F32, az_at)
        CQ = put("state_times_q", [128, 4, 128], F32, cq_at)
        aqT = put("aq", [128, 4, TS], F32, a)
        an = put("aqn", [128, 4, TS], F32, a)
        eo = [put(f"exp_o{i}", [128, T], F32, a) for i in range(2)]
        emS = put("exp_neg_m", [128, T], F32, a)
        rec = put("rec", [128, T], F32, a)
        hg = put("h_gated", [128, T], F32, a)
        R = [put(f"row{i}", [8, T], F32, a) for i in range(6)]
        cols = put("cols", [128, 64], F32, a)
        small = put("small", [8, 64], F32, a)
        m0 = small[:, 0:8]
        ael = small[:, 8:16]
        mnew = small[:, 16:25]
        atr = put("a_rows", [8, TS], F32, a)
        aeP = put("ae_pairs", [128, 4, NB], F32, a)
        nout = put("n_out", [8, 512], F32, a)

        b_ = [phase]
        KT = [put(f"k_turned{i}", [128, H, 256], F32, b_) for i in range(2)]
        pt_at = [phase]
        PT = [put(f"probs_turned{i}", [128, 16, 128], F32, pt_at) for i in range(2)]
        vreg = b_[0]
        raw_at, xhl_at = [raw2_at], [xh_at]
        page = [put(f"page{i}", [128, DM], F32, w_) for i, w_ in enumerate([b_] * 4 + [raw_at] * 4 + [xhl_at] * 4)]
        ln_at = [vreg]
        mu = put("ln_mu", [128, T], F32, ln_at)
        var = put("ln_var", [128, T], F32, ln_at)
        rs = put("ln_rstd", [128, T], F32, ln_at)
        tmp = put("ln_tmp", [128, T], F32, ln_at)
        assert ln_at[0] <= b_[0]
        pr, on_at = [b_[0]], [b_[0]]
        L = [put(f"logits{i}", [128, 2, PAGES * PG], F32, b_) for i in range(2)]
        PL = [put(f"p_logit{i}", [128, 384], F32, pr) for i in range(2)]
        PTt = [put(f"p_turned{i}", [128, 384], F32, pr) for i in range(2)]
        pst = put("p_stats", [128, 8 * 8], F32, pr)
        ON = []
        for i in range(2):
            on_at[0] = b_[0] - 8192 * (2 - i)
            ON.append(put(f"o_rows{i}", [128, 4, 2, 128], F32, on_at))
        ko_at, yo_at = [b_[0] - 8192], [b_[0] - 16384]
        YO = [put(f"y_out{i}", [128, 3, 256], F32, yo_at) for i in range(4)]
        KO = [put(f"turned{i}", [128, 3, 128], F32, ko_at) for i in range(2)]
        free_at = [fs_at]
        PTo = [put("own_turned1", [64, 2, 128], F32, free_at)]
        free_at = [fs_at + 4 * T]
        QZ = [put("q_padded0", [128, H, 4, 32], F32, b_), put("q_padded1", [128, H, 4, 32], F32, free_at)]
        PTo.insert(0, put("own_turned0", [64, 2, 128], F32, b_))
        PO = put("own_probs", [128, 2, 2, 64], F32, b_)
        sm = put("soft_small", [128, 2, 56], F32, b_)
        AT = put("attn_prompt", [128, H, TP], F32, b_)
        AO = put("attn_sample", [128, H, TS], F32, b_)

        ps = [ctx.enter_context(nc.psum_tensor(f"ps{i}", [128, 512], F32)) for i in range(8)]

        def sem(name):
            return ctx.enter_context(nc.semaphore(name))

        s_raw = [sem(f"raw_loaded{i}") for i in range(RAW)]
        s_hi, s_lo, s_mm = sem("w_hi_split"), sem("w_lo_split"), sem("tile_done")
        s_ev = [sem("act_emptied"), sem("dve_emptied")]
        s_x = sem("x_in")
        s_base, s_ml, s_gw, s_ln, s_n0, s_c0, s_at, s_tab = [
            sem(n) for n in ("base_in", "mlstm_in", "gate_w_in", "ln_in", "n0_in", "c0_in", "attn_in", "table_in")]
        s_m0 = sem("m0_in")
        s_xt, s_xh, s_xl, s_xf = sem("x_turned"), sem("x_hi_done"), sem("x_lo_done"), sem("x_copied")
        s_lnt, s_lnc = sem("ln_turned"), sem("ln_copied")
        s_d, s_a, s_p = sem("dve_own"), sem("act_own"), sem("pool_own")
        s_gz, s_gh, s_gl, s_gp = sem("gate_zeroed"), sem("gate_hi"), sem("gate_lo"), sem("gate_done")
        s_gabs, s_gln, s_mt, s_emn, s_wsl, s_ws, s_al, s_aex = [
            sem(n) for n in ("gate_abs", "gate_log", "m_rows", "emn_rows", "ws_log", "ws_rows", "a_log", "a_rows_done")]
        s_colp, s_col = sem("cols_turned"), sem("cols_copied")
        s_bc = sem("aq_products")
        s_vt, s_vc = sem("v_turned"), sem("v_copied")
        s_sp, s_D, s_E, s_W = sem("mS_done"), sem("decay_log"), sem("decay_exp"), sem("weights_done")
        s_emp, s_emc, s_num, s_hg, s_hh, s_hl = [
            sem(n) for n in ("emn_cast", "emn_copied", "num_done", "gated", "h_hi_done", "h_lo_done")]
        s_kt, s_wk, s_cp, s_cadd, s_np, s_nadd = [
            sem(n) for n in ("k_tokens", "wsk_done", "c_product", "c_added", "n_product", "n_added")]
        s_den, s_abs, s_pd = sem("den_done"), sem("abs_den"), sem("divisor_done")
        s_yt, s_yA, s_yD, s_ys, s_yp = [
            sem(n) for n in ("y_turned", "y_copied_act", "y_copied_dve", "y_sample_out", "y_prompt_out")]
        s_vm, s_aqz, s_cq, s_cqc = [
            sem(n) for n in ("v_masked_done", "aq_padded_done", "cq_cast", "cq_copied")]
        s_sq = sem("relu_squared")
        s_sq7, s_pc = sem("last_square"), sem("pool_centred")
        s_st, s_lnp, s_var, s_rs, s_t, s_F, s_al2 = [
            sem(n) for n in ("sums_done", "stats_cast", "var_done", "rstd_guess", "centred", "ln_out", "x_scaled")]
        s_tp, s_tc, s_tv = sem("turn_done"), sem("turn_copied"), sem("v_turn_copied")
        s_to = [sem(f"turn_out{i}") for i in range(2)]
        s_pS, s_pmx, s_pex, s_pnm, s_pT, s_pTc, s_pV, s_pA = [
            sem(n) for n in ("pS_done", "p_max", "p_exp", "p_norm", "p_turn", "p_turn_copied", "p_out", "p_out_copied")]
        s_in = [sem(f"page_in{i}") for i in range(RING)]
        s_used = sem("page_used")
        s_qz, s_sc, s_own, s_ownr, s_Lr, s_sm, s_ex = [
            sem(n) for n in ("q_padded_done", "pair_scored", "own_scored", "own_read", "scores_read", "softmax_bias",
                             "exp_done")]
        s_qzz = sem("q_padded_zeroed")
        s_kA, s_kD, s_ptt, s_ptc, s_xhp, s_on, s_ot, s_ao = [
            sem(n) for n in ("k_copied_act", "k_copied_dve", "probs_turned_n", "probs_copied", "x_hi_prompt",
                             "o_scaled", "o_turned", "attn_out")]
        s_nm = sem("new_m")
        s_out = sem("stored")
        s_co, s_po = sem("c_stored"), sem("prompt_state_stored")

        SCORE_BANK = (4, 7, 5, 6)
        TURN_BANK = (2, 3, 0, 2)

        def dense_bank(t):
            if t % 8 == 4 and t // 8 in (Q_MLP0, Q_MLP1):
                return ps[5]
            return ps[9 - t % 8] if t % 8 in (2, 3) and t // 8 in SIDE_BY_SIDE else ps[t % 2]

        def c_bank(j, half):
            return ps[6 - 2 * (j % 2) + half]

        def soft(G):
            return sm[:, G, 0:8], sm[:, G, 8:10], sm[:, G, 10:20]

        def page_banks(P):
            return (2, 3) if P % 2 else (0, 1)

        block = ctx.enter_context(nc.Block())

        def lhs_k(w):
            return w.rearrange("(k p) n -> p k n", p=128)

        win = w_in_a[0]

        def wsrc(u):
            q, j = u // 4, u % 4
            c = 256 * j
            w, c0 = {Q_QK: (win, 0), Q_V: (win, 1024), Q_O: (win, 2048), Q_WOA: (w_out_a[0], 0),
                     Q_WK: (w_kv, 0), Q_WV: (w_kv, 1024), Q_WQ: (w_q_b[0], 0), Q_WOB: (w_out_b[0], 0)}[q]
            return lhs_k(w[:, c0 + c:c0 + c + 256])

        def y_copy(m, odd, eng, copy, done):
            n = 2 * m + odd
            eng.wait_ge(s_yt, n + 1)
            c = slice(128 * odd, 128 * odd + 128)
            copy(YO[m][:, 0:2, c], ps[4 + n % 4][:, 0:256].rearrange("p (t c) -> p t c", t=2))
            copy(YO[m][0:64, 2, c], ps[4 + n % 4][0:64, 256:384]).then_inc(done, 1)

        @block.sync
        def _(sp):
            def load_unit(u, src, more=0):
                if isinstance(more, int) and u < RAW:
                    pass
                else:
                    sp.wait_ge(s_lo, 2 * (u - RAW) + 2 + 2 * more)
                sp.dma_start(raw[u % RAW][:, :, :], src).then_inc(s_raw[u % RAW], 16)

            sp.dma_start(base[:, :], c_base).then_inc(s_base, 16)
            sp.dma_start(VT[:, 0:2, :], x_prompt[0].rearrange("(t p) c -> p t c", p=128)).then_inc(s_x, 16)
            sp.dma_start(VT[0:64, 2, :], x_sample.rearrange("b t c -> (b t) c")).then_inc(s_x, 16)
            sp.dma_start(wgraw[:, :, :], lhs_k(win[:, 3072:3088])).then_inc(s_gw, 16)
            load_unit(0, wsrc(0))
            load_unit(1, wsrc(1))
            sp.dma_start(cml[:, :], c_mlstm).then_inc(s_ml, 16)
            sp.dma_start(sel[:, :], c_sel).then_inc(s_ml, 16)
            sp.dma_start(m0, state_m[0].rearrange("b h -> h b"), allow_slow_non_contiguous=True).then_inc(s_m0, 16)
            sp.dma_start(bg[0:8, :], b_gate_a[0:1, 0:8].rearrange("a h -> h a"), allow_slow_non_contiguous=True).then_inc(s_m0, 16)
            sp.dma_start(bg[32:40, :], b_gate_a[0:1, 8:16].rearrange("a h -> h a"), allow_slow_non_contiguous=True).then_inc(s_m0, 16)
            load_unit(2, wsrc(2))
            load_unit(3, wsrc(3))
            sp.dma_start(lnN[0:32, :], ln_g.rearrange("l w (c p) -> (l w c) p", p=128)).then_inc(s_ln, 16)
            sp.dma_start(lnN[32:64, :], ln_b.rearrange("l w (c p) -> (l w c) p", p=128)).then_inc(s_ln, 16)
            sp.dma_start(n0[:, :], state_n[0].rearrange("b h k -> b (h k)")).then_inc(s_n0, 16)
            sp.dma_start(table[:, :], page_table.rearrange("b p -> (b p)").unsqueeze(0)).then_inc(s_tab, 16)
            for j in range(4):
                for h2 in range(2):
                    sp.dma_start(C0[64 * h2:64 * h2 + 64, j, :, :],
                                 state_C[0, :, 2 * j + h2].rearrange("b k v -> k b v")).then_inc(s_c0, 16)
            for u in range(4, 16):
                load_unit(u, wsrc(u))

            def mlp_loads(first, m):
                with sp.Fori(0, 4) as g:
                    for j in range(4):
                        load_unit(4 * first + j, lhs_k(w_up[m][:, bass.ds(g * 1024 + 256 * j, 256)]), 8 * g)
                    for j in range(4):
                        load_unit(4 * first + 4 + j,
                                  lhs_k(w_down[m][bass.ds(g * 1024, 1024), 256 * j:256 * j + 256]), 8 * g)

            mlp_loads(Q_MLP0, 0)
            for u in range(4 * Q_WK, 4 * Q_WK + 4):
                load_unit(u, wsrc(u))
            sp.wait_ge(s_co, 16 * 8)
            sp.wait_ge(s_po, 16 * 4)
            sp.dma_start(cat[:, :], c_attn).then_inc(s_at, 16)

            def load_page(cache, g, slot, index):
                number = sp.value_load(table[0:1, bass.ds(index, 1)] if not isinstance(index, int)
                                       else table[0:1, index:index + 1], min_val=0, max_val=cache_k.shape[0] - 1)
                if not isinstance(g, int) or g >= RING:
                    sp.wait_ge(s_used, g - RING + 1)
                sp.dma_start(page[slot][:, :], cache[bass.ds(number, 1)].rearrange("a t h d -> (a t) (h d)"))\
                    .then_inc(s_in[slot], 16)

            def pages(first, last):
                g = first
                while g < last:
                    cache, off = (cache_k, 0) if g < NPG else (cache_v, NPG)
                    end = min(last, NPG if g < NPG else 2 * NPG)
                    rounds = (end - g) // RING
                    if g % RING == 0 and rounds >= 2:
                        with sp.Fori(g // RING, g // RING + rounds) as i:
                            for p in range(RING):
                                load_page(cache, RING * i + p, p, RING * i + p - off)
                        g += RING * rounds
                    else:
                        load_page(cache, g, g % RING, g - off)
                        g += 1

            for u in range(4 * Q_WV, 4 * Q_WV + 4):
                load_unit(u, wsrc(u))
            sp.wait_ge(s_tab, 16)
            sp.wait_ge(s_al2, 16)
            pages(0, 4)
            for u in range(4 * Q_WQ, 4 * Q_WOB + 2):
                load_unit(u, wsrc(u))
            sp.wait_ge(s_lo, 8 * Q_WOB)
            pages(4, 8)
            sp.wait_ge(s_mm, 8 * Q_WQ + 8)
            pages(8, 2 * NPG)
            for u in range(4 * Q_WOB + 2, 4 * Q_WOB + 4):
                sp.wait_ge(s_used, 2 * NPG)
                load_unit(u, wsrc(u))
            mlp_loads(Q_MLP1, 1)
            for m in range(4):
                sp.wait_ge(s_yA, m + 1)
                sp.wait_ge(s_yD, m + 1)
                sp.dma_start(y_prompt[0, :, 256 * m:256 * m + 256].rearrange("(t p) d -> p t d", p=128),
                             YO[m][:, 0:2, :]).then_inc(s_yp, 16)
            sp.wait_ge(s_yp, 16 * 4)

        @block.tensor
        def _(pe):
            mm = nc.tensor.matmul

            def dense(t, hi, lo, chunk_ready=None, turn=0, ev_shift=0):
                if t >= 2 and dense_bank(t) in (ps[0], ps[1]):
                    e, n = evac(t - 2)
                    pe.wait_ge(s_ev[e], n + ev_shift)
                pe.wait_ge(s_lo, t + 1 + 16 * turn)
                out = dense_bank(t)[:, 0:T]
                for k in range(8):
                    if chunk_ready is not None:
                        pe.wait_ge(*chunk_ready(k))
                    mm(out, WH[t % SPL][:, k, :], hi[:, k, :], start=(k == 0), stop=False)
                    mm(out, WH[t % SPL][:, k, :], lo[:, k, :], start=False, stop=False)
                    last = mm(out, WL[t % SPL][:, k, :], hi[:, k, :], start=False, stop=(k == 7))
                last.then_inc(s_mm, 1)

            def dense3(t0, hi, lo, chunks, turn=0, ev_shift=0):
                for i in range(2):
                    e, n = evac(t0 + i - 2)
                    pe.wait_ge(s_ev[e], n + ev_shift)
                for k in range(8):
                    pe.wait_ge(s_xh, chunks + k + 1)
                    for i in range(3):
                        t = t0 + i
                        if k == 0:
                            pe.wait_ge(s_lo, t + 1 + 16 * turn)
                        out = dense_bank(t)[:, 0:T]
                        mm(out, WL[t % SPL][:, k, :], hi[:, k, :], start=(k == 0), stop=False)
                        mm(out, WH[t % SPL][:, k, :], hi[:, k, :], start=False, stop=False)
                        if i == 0:
                            pe.wait_ge(s_xl, chunks + k + 1)
                        last = mm(out, WH[t % SPL][:, k, :], lo[:, k, :], start=False, stop=(k == 7))
                        if k == 7:
                            last.then_inc(s_mm, 1)

            def turn3(bank, src):
                nc.tensor.transpose(bank[:, 0:128], src[:, 0:128], ident)
                nc.tensor.transpose(bank[:, 128:256], src[:, 128:256], ident)
                return nc.tensor.transpose(bank[0:64, 256:384], src[:, 256:320], ident)

            pe.wait_ge(s_base, 16)
            for n in range(8):
                if n == 0:
                    pe.wait_ge(s_x, 32)
                if n >= 2:
                    pe.wait_ge(s_xf, n - 1)
                c = slice(128 * n, 128 * n + 128)
                bank = ps[2 + n % 2]
                nc.tensor.transpose(bank[:, 0:128], VT[:, 0, c], ident)
                nc.tensor.transpose(bank[:, 128:256], VT[:, 1, c], ident)
                nc.tensor.transpose(bank[:, 256:320], VT[0:64, 2, c], ident[0:64, 0:64]).then_inc(s_xt, 1)
            pe.wait_ge(s_gl, 1)
            for k in range(8):
                pe.wait_ge(s_xl, k + 1)
                mm(ps[5][:, 0:T], WGH[:, k, :], XH[:, k, :], start=(k == 0), stop=False)
                mm(ps[5][:, 0:T], WGH[:, k, :], XL[:, k, :], start=False, stop=False)
                last = mm(ps[5][:, 0:T], WGL[:, k, :], XH[:, k, :], start=False, stop=(k == 7))
            last.then_inc(s_gp, 1)
            for n in range(8):
                dense(8 * Q_QK + n, XH, XL)
            pe.wait_ge(s_n0, 16)
            for j in range(4):
                last = nc.tensor.transpose(ps[7][:, 352 + 8 * j:360 + 8 * j], n0[:, 128 * j:128 * j + 128],
                                           ident[0:8, 0:8])
            pe.wait_ge(s_ln, 32)
            nc.tensor.transpose(ps[4][:, 0:64], lnN[:, :], ident[0:64, 0:64]).then_inc(s_lnt, 1)
            pe.wait_ge(s_ws, 1)
            for i in range(3):
                w = 128 if i < 2 else 64
                nc.tensor.transpose(ps[7][0:w, 8 * i:8 * i + 8], R[4][:, 128 * i:128 * i + w], ident[0:8, 0:8])
                nc.tensor.transpose(ps[7][0:w, 24 + 8 * i:32 + 8 * i], R[5][:, 128 * i:128 * i + w], ident[0:8, 0:8])
            pe.wait_ge(s_aex, 2)
            nc.tensor.transpose(ps[7][0:8, 48:56], ael, ident[0:8, 0:8])
            for j in range(4):
                s = sel[:, (8 + j) * 128:(9 + j) * 128]
                mm(ps[7][:, 64 + 64 * j:128 + 64 * j], s, atr[:, :], start=True, stop=True)
                last = mm(ps[7][:, 320 + 8 * j:328 + 8 * j], s, ael, start=True, stop=True)
            last.then_inc(s_colp, 1)
            def state_times_q():
                pe.wait_ge(s_c0, 16 * 8)
                pe.wait_ge(s_aqz, 1)
                for j in range(4):
                    for bb in range(4):
                        for h2 in range(2):
                            for half in range(2):
                                b, row = 4 * half + bb, 64 * h2 + 32 * half
                                last = mm(ps[2 + 4 * h2][row:row + 32, 128 * j:128 * j + 128],
                                          aqZ[64 * h2:64 * h2 + 64, j, b, :], C0[64 * h2:64 * h2 + 64, j, b, :],
                                          start=(j == 0 and bb == 0), stop=True, skip_group_check=True)
                last.then_inc(s_cq, 1)

            for n in range(8):
                if n == 6:
                    state_times_q()
                dense(8 * Q_V + n, XH, XL)
                if n >= 1:
                    pe.wait_ge(*((s_ev[0]), evac(8 * Q_V + n - 1)[1]))
                    if n == 1:
                        pe.wait_ge(s_lnc, 1)
                    if n >= 3:
                        pe.wait_ge(s_vc, n - 2)
                    turn3(ps[4 + (n - 1) % 2], FR[(n - 1) % 2]).then_inc(s_vt, 1)
            pe.wait_ge(s_ev[0], evac(8 * Q_V + 7)[1])
            pe.wait_ge(s_vc, 6)
            turn3(ps[4 + 7 % 2], FR[7 % 2]).then_inc(s_vt, 1)

            pe.wait_ge(s_ml, 32)
            pe.wait_ge(s_col, 1)
            for h in range(H):
                j, r = h // 2, slice(64 * (h % 2), 64 * (h % 2) + 64)
                hs = sel[:, 128 * h:128 * h + 128]
                S, MB, EM, DEN, NUM = ps[2], ps[3], ps[4], ps[5], ps[6 + h % 2]
                if h == 0:
                    pe.wait_ge(s_bc, 2)
                    pe.wait_ge(s_cqc, 2)
                if h >= 1:
                    pe.wait_ge(s_W, h)
                mm(MB[:, 0:T], hs, R[2][:, :], start=True, stop=True)
                mm(S[:, 0:256], kT[r, j, 0:128], qT[r, j, 0:256], start=True, stop=True)
                mm(S[:, 256:384], kT[r, j, 128:256], qT[r, j, 128:256], start=True, stop=True)
                mm(S[0:64, 384:448], kT[r, j, 256:320], qT[r, j, 256:320], start=True, stop=True).then_inc(s_sp, 1)
                dense(8 * Q_O + h, XH, XL)
                if h == 0:
                    pe.wait_ge(s_vc, 8)
                if h >= 1:
                    pe.wait_ge(s_emc, h)
                mm(EM[:, 0:T], hs, R[1][:, :], start=True, stop=True).then_inc(s_emp, 1)
                w = W[h % 2]
                pe.wait_ge(s_W, h + 1)
                c = slice(128 * h, 128 * h + 128)

                def weighted(dst, v0, v1, v2):
                    mm(dst[:, 0:256], v0, w[:, 0:256], start=True, stop=True)
                    mm(dst[:, 128:256], v1, w[:, 256:384], start=False, stop=True, skip_group_check=True)
                    mm(dst[:, 256:320], v2, w[:, 384:448], start=False, stop=True, skip_group_check=True)

                if h >= 1:
                    pe.wait_ge(s_abs, h)
                weighted(DEN, ones, ones, ones)
                mm(DEN[:, 256:320], ones[r, :], an[r, j, :], start=False, stop=True, skip_group_check=True)\
                    .then_inc(s_den, 1)
                if h >= 2:
                    pe.wait_ge(s_hg, h - 1)
                weighted(NUM, VT[:, 0, c], VT[:, 1, c], VT[:, 2, c])
                mm(NUM[:, 256:320], CQ[r, j, :], ident[r, r], start=False, stop=True, skip_group_check=True)\
                    .then_inc(s_num, 1)

            def state_step(n):
                if n < 2:
                    pe.wait_ge(s_W, H)
                    for i in (2 * n, 2 * n + 1):
                        if i >= 2:
                            pe.wait_ge(s_wk, 2 * i - 2)
                        turn3(ps[2 + i % 2], kT[:, i, :]).then_inc(s_kt, 1)
                if 2 <= n < 6:
                    j = n - 2
                    pe.wait_ge(s_wk, 8)
                    pe.wait_ge(s_hg, H)
                    pe.wait_ge(s_vm, 2 * j + 2)
                    for half in range(2):
                        if j >= 2:
                            pe.wait_ge(s_cadd, 2 * j - 3 + half)
                        rows = slice(32 * half, 32 * half + 32)
                        for c in range(4):
                            h, k0 = 2 * j + c // 2, 128 * j + 32 * c
                            last = mm(c_bank(j, half)[32 * c:32 * c + 32, :], wsK[rows, 2, k0:k0 + 32],
                                      Vm[rows, h, :, :].rearrange("p b v -> p (b v)"), start=True, stop=True,
                                      skip_group_check=True)
                        last.then_inc(s_cp, 1)

            state_step(0)
            for n in range(8):
                dense(8 * Q_WOA + n, HH, HL, (lambda k: (s_hl, k + 1)) if n == 0 else None)
                state_step(n + 1)

            def prompt_state():
                pe.wait_ge(s_cadd, 8)
                for h in range(H):
                    o = ps[4][64 * (h % 2):64 * (h % 2) + 64, 128 * (h // 2):128 * (h // 2) + 128]
                    for q in range(2):
                        mm(o, wsK[:, q, 64 * h:64 * h + 64], VT[:, q, 128 * h:128 * h + 128],
                           start=(q == 0), stop=(q == 1), skip_group_check=True)
                for q in range(2):
                    mm(ps[5][0:1, :], ones[:, 0:1], wsK[:, q, :], start=(q == 0), stop=(q == 1))
                mm(ps[6][0:8, :], bmask[0:64, :], wsK[0:64, 2, :], start=True, stop=True).then_inc(s_np, 1)

            def ln_stats(l):
                q = (Q_WOA, Q_WK - 1, Q_WOB, N_QUADS - 1)[l]
                pe.wait_ge(s_st, l + 1)
                mm(ps[2][:, 0:T], ones, A1[:, :], start=True, stop=False)
                mm(ps[3][:, 0:T], ones, A2[:, :], start=True, stop=False)
                pe.wait_ge(s_ev[1], evac(8 * q + 7)[1])
                mm(ps[2][:, 0:T], ones, X[:, 7, :], start=False, stop=True).then_inc(s_lnp, 1)
                pe.wait_ge(s_sq7, l + 1)
                mm(ps[3][:, 0:T], ones, FS[0][:, :], start=False, stop=True).then_inc(s_lnp, 1)

            def mlp(q0, xl0, hl0):
                up0, dn0 = 8 * q0, 8 * q0 + 8

                def down(g):
                    for n in range(8):
                        dense(dn0 + n, HH, HL, (lambda k: (s_hl, hl0 + k + 1 + 8 * g)) if n == 0 else None, g, 8 * g)

                dense3(up0, XH, XL, xl0)
                pe.wait_ge(s_nadd, 2)
                for n in range(3, 8):
                    dense(up0 + n, XH, XL)
                down(0)
                with pe.Fori(1, 4) as g:
                    for n in range(8):
                        dense(up0 + n, XH, XL, None, g, 8 * g)
                    down(g)

            ln_stats(0)
            prompt_state()
            mlp(Q_MLP0, 8, 8)
            ln_stats(1)

            def kv_turn(i):
                n = i % 8
                if i < 8:
                    pe.wait_ge(s_ev[0], evac(8 * Q_WK + n)[1])
                    src = KA[:, n, :]
                else:
                    pe.wait_ge(s_ev[0], evac(8 * Q_WV + n)[1])
                    src = FR[n % 2]
                if i >= 2:
                    pe.wait_ge(*((s_tc, i - 1) if i < 10 else (s_tv, i - 9)))
                turn3(ps[4 + i % 2], src).then_inc(s_tp, 1)

            dense3(8 * Q_WK, XH, XL, 16)
            kv_turn(0)
            kv_turn(1)
            for n in range(3, 8):
                dense(8 * Q_WK + n, XH, XL)
                kv_turn(n - 1)
            for n in range(8):
                dense(8 * Q_WV + n, XH, XL)
                kv_turn(7 + n)

            def p_scores(h):
                if h >= 1:
                    pe.wait_ge(s_pmx, h)
                mm(ps[2][:, 0:128], QA[:, h, 0:128], KA[:, h, 0:128], start=True, stop=True)
                mm(ps[2][:, 128:384], QA[:, h, 128:256], KA[:, h, 0:256], start=True, stop=True).then_inc(s_pS, 1)

            def p_turn(h):
                pe.wait_ge(s_pnm, 2 * h + 2)
                if h >= 1:
                    pe.wait_ge(s_pTc, h)
                pl = PL[h % 2]
                nc.tensor.transpose(ps[3][:, 0:128], pl[:, 0:128], ident)
                nc.tensor.transpose(ps[3][:, 128:256], pl[:, 128:256], ident)
                nc.tensor.transpose(ps[3][:, 256:384], pl[:, 256:384], ident).then_inc(s_pT, 1)

            def p_out(h):
                pe.wait_ge(s_pTc, h + 1)
                pe.wait_ge(s_Lr, 8)
                if h >= 1:
                    pe.wait_ge(s_pA, h)
                c = slice(128 * h, 128 * h + 128)
                mm(ps[6][:, 0:256], VT[:, 0, c], PTt[h % 2][:, 0:256], start=True, stop=True)
                mm(ps[6][:, 128:256], VT[:, 1, c], PTt[h % 2][:, 256:384], start=False, stop=True,
                   skip_group_check=True).then_inc(s_pV, 1)

            def p_step(i):
                if 0 <= i < H:
                    p_scores(i)
                if 0 <= i - 2 < H:
                    p_out(i - 2)
                if 0 <= i - 1 < H:
                    p_turn(i - 1)

            for n in range(8):
                dense(8 * Q_WQ + n, XH, XL)
                if n == 0:
                    kv_turn(15)
            pe.wait_ge(s_ev[0], evac(8 * Q_WQ + 7)[1])

            def turn_page(P):
                pe.wait_ge(s_in[P % RING], 16 * (P // RING + 1))
                if P >= 2:
                    pe.wait_ge(s_kA, P - 1)
                    pe.wait_ge(s_kD, P - 1)
                for h in range(H):
                    last = nc.tensor.transpose(ps[page_banks(P)[h // 4]][:, 128 * (h % 4):128 * (h % 4) + 128],
                                               page[P % RING][:, 128 * h:128 * h + 128], ident)
                last.then_inc(s_used, 1)

            def own_scores():
                pe.wait_ge(s_tv, 8)
                for G in range(2):
                    for a_ in range(2):
                        for j in range(4):
                            h, c = 4 * a_ + j, 128 * G + 64 * a_
                            last = mm(ps[7][32 * j:32 * j + 32, c:c + 64],
                                      QA[:, h, TP + 32 * G:TP + 32 * G + 32], KA[:, h, TP:T], start=True, stop=True,
                                      skip_group_check=True)
                last.then_inc(s_own, 1)

            def score_pair(pair):
                G, bb, r = pair // 16, pair // 4 % 4, pair % 4
                pe.wait_ge(s_kA, 2 * pair + 2)
                pe.wait_ge(s_kD, 2 * pair + 2)
                if pair % 16 == 0:
                    pe.wait_ge(s_qz, G + 1)
                if pair == 2:
                    pe.wait_ge(s_ownr, 1)
                if pair in (16, 18):
                    pe.wait_ge(s_Lr, 2 + pair - 16)
                for a_ in range(2):
                    for j in range(4):
                        last = mm(ps[SCORE_BANK[2 * a_ + r // 2]][32 * j:32 * j + 32,
                                                                  256 * (r % 2):256 * (r % 2) + 256],
                                  QZ[G][:, 4 * a_ + j, bb, :], KT[pair % 2][:, 4 * a_ + j, :],
                                  start=(bb == 0 and r % 2 == 0), stop=True, skip_group_check=True)
                last.then_inc(s_sc, 1)

            def probs_turn(G):
                pe.wait_ge(s_kA, NPG)
                pe.wait_ge(s_kD, NPG)
                pe.wait_ge(s_ex, 10 * G + 2)
                for a_ in range(2):
                    last = nc.tensor.transpose(ps[1][0:64, 128 * a_:128 * a_ + 128], PO[:, G, a_, :], ident)
                last.then_inc(s_ptt, 1)
                for c in range(4):
                    for i in range(4):
                        m = 4 * c + i
                        pe.wait_ge(s_ex, 10 * G + 2 + m // 2 + 1)
                        if c == 3 and i == 0:
                            pe.wait_ge(s_ptc, 5 * G + 2)
                        last = nc.tensor.transpose(ps[TURN_BANK[c]][:, 128 * i:128 * i + 128],
                                                   L[G][:, m // 8, 128 * (m % 8):128 * (m % 8) + 128], ident)
                    last.then_inc(s_ptt, 1)

            def o_bank(G, bb):
                return ps[4 + 2 * G + bb // 2]

            def own_values(G):
                pe.wait_ge(s_ptc, 5 * G + 1)
                pe.wait_ge(s_Lr, 6 if G == 0 else 8)
                if G == 1:
                    pe.wait_ge(s_pA, H)
                for bb in range(4):
                    for a_ in range(2):
                        for j in range(4):
                            h, c = 4 * a_ + j, 256 * (bb % 2) + 128 * a_
                            mm(o_bank(G, bb)[32 * j:32 * j + 32, c:c + 128],
                               PTo[G][:, a_, 32 * j:32 * j + 32], VT[0:64, 2, 128 * h:128 * h + 128],
                               start=(bb % 2 == 0 and a_ == 0), stop=True, skip_group_check=True)
                pe.wait_ge(s_ptc, 5 * G + 5)

            def page_values(G, bb):
                for p in range(PAGES):
                    g = NPG + 32 * G + 8 * bb + p
                    pe.wait_ge(s_in[g % RING], 16 * (g // RING + 1))
                    for a_ in range(2):
                        for j in range(4):
                            h, c = 4 * a_ + j, 256 * (bb % 2) + 128 * a_
                            last = mm(o_bank(G, bb)[32 * j:32 * j + 32, c:c + 128],
                                      PT[G][:, 8 * a_ + p, 32 * j:32 * j + 32],
                                      page[g % RING][:, 128 * h:128 * h + 128], start=False, stop=True,
                                      skip_group_check=True)
                    last.then_inc(s_used, 1)
                    i = 8 * bb + p - FIRST
                    if G == 0 and i >= 0 and i % 3 == 0:
                        p_step(i // 3)

            def out_turn(G, half):
                pe.wait_ge(s_on, 2 * G + half + 1)
                for bb in (2 * half, 2 * half + 1):
                    for a_ in range(2):
                        c = 256 * (bb % 2) + 128 * a_
                        last = nc.tensor.transpose(o_bank(G, bb)[:, c:c + 128], ON[G][:, bb, a_, :], ident)
                last.then_inc(s_ot, 1)

            own_scores()
            for pair in range(NPG // 2):
                turn_page(2 * pair)
                turn_page(2 * pair + 1)
                if pair >= 1:
                    score_pair(pair - 1)
            score_pair(NPG // 2 - 1)
            for G in range(2):
                probs_turn(G)
                own_values(G)
                for bb in range(4):
                    page_values(G, bb)
                    if G == 1 and bb == 0:
                        out_turn(0, 0)
                        out_turn(0, 1)
                    if G == 1 and bb == 2:
                        out_turn(1, 0)
            out_turn(1, 1)
            for n in range(8):
                dense(8 * Q_WOB + n, XH, XL, (lambda k: (s_xl, 24 + k + 1)) if n == 0 else None)
            ln_stats(2)
            mlp(Q_MLP1, 32, 40)
            ln_stats(3)
            for n in range(8):
                pe.wait_ge(s_t, 15 + n // 2 + 1)
                if n % 2:
                    pe.wait_ge(s_F, n // 2 + 1)
                if n >= 4:
                    pe.wait_ge((s_yA, s_yD)[n % 2], n // 2 - 1)
                turn3(ps[4 + n % 4], X[:, n, :]).then_inc(s_yt, 1)

        @block.scalar
        def _(act):
            A = nc.scalar.activation
            own = Own(act, s_a)

            def split(t, turn=0):
                u = t // 2
                if t % 2 == 0:
                    act.wait_ge(s_raw[u % RAW], 16 * (u // RAW + 1) + 32 * turn)
                if t >= SPL:
                    act.wait_ge(s_mm, t - SPL + 1 + 16 * turn)
                A(WH[t % SPL][:, :, :], raw[u % RAW][:, :, 128 * (t % 2):128 * (t % 2) + 128], ACT.Copy)\
                    .then_inc(s_hi, 1)

            def tile(t, turn=0):
                act.wait_ge(s_mm, t + 1 + 16 * turn)
                return dense_bank(t)[:, 0:T]

            act.wait_ge(s_gw, 16)
            act.wait_ge(s_gz, 1)
            A(WGH[:, :, 0:8], wgraw[:, :, 0:8], ACT.Copy)
            A(WGH[:, :, 32:40], wgraw[:, :, 8:16], ACT.Copy).then_inc(s_gh, 1)
            for n in range(8):
                act.wait_ge(s_xf, n + 1)
                A(XH[:, n, :], X[:, n, :], ACT.Copy).then_inc(s_xh, 1)
                if n in (3, 5):
                    split((n - 3) // 2)
            split(2)
            split(3)
            def rows_log():
                act.wait_ge(s_gabs, 1)
                own(A(R[2][:, :], R[2][:, :], ACT.Exp, scale=-1.0))
                A(R[2][:, :], R[2][:, :], ACT.Ln, bias=1.0).then_inc(s_gln, 1)

            def rows_exp():
                act.wait_ge(s_mt, 1)
                A(R[1][:, :], R[1][:, :], ACT.Exp, scale=-1.0).then_inc(s_emn, 1)
                act.wait_ge(s_wsl, 1)
                A(R[5][:, :], R[5][:, :], ACT.Exp).then_inc(s_ws, 1)
                act.wait_ge(s_al, 2)
                A(atr[:, :], atr[:, :], ACT.Exp).then_inc(s_aex, 1)
                A(ael, ael, ACT.Exp).then_inc(s_aex, 1)

            for n in range(8):
                t = 8 * Q_QK + n
                if n == 0:
                    rows_log()
                if n == 2:
                    rows_exp()
                if n < 4:
                    A(qT[:, n, :], tile(t), ACT.Copy).then_inc(s_ev[0], 1)
                else:
                    A(kT[:, n - 4, :], tile(t), ACT.Copy, scale=DK ** -0.5).then_inc(s_ev[0], 1)
                split(t + 4)
            for n in range(8):
                t = 8 * Q_V + n
                if n == 7:
                    act.wait_ge(s_cq, 1)
                    A(CQ[0:64, :, :], ps[2][0:64, :].rearrange("p (j v) -> p j v", j=4), ACT.Copy).then_inc(s_cqc, 1)
                    A(CQ[64:128, :, :], ps[6][64:128, :].rearrange("p (j v) -> p j v", j=4), ACT.Copy)\
                        .then_inc(s_cqc, 1)
                o = tile(t)
                if n >= 2:
                    act.wait_ge(s_vt, n - 1)
                A(FR[n % 2][:, :], o, ACT.Copy).then_inc(s_ev[0], 1)
                split(t + 4)

            def h_rounded(h):
                act.wait_ge(s_hg, h + 1)
                A(HH[:, h, :], hg[:, :], ACT.Copy).then_inc(s_hh, 1)

            def abs_den(h):
                act.wait_ge(s_den, h + 1)
                if h >= 2:
                    act.wait_ge(s_hg, h - 1)
                A((A1, A2)[h % 2][:, :], ps[5][:, 0:T], ACT.Abs).then_inc(s_abs, 1)

            for h in range(H):
                t = 8 * Q_O + h
                if h >= 1:
                    abs_den(h - 1)
                act.wait_ge(s_D, h + 1)
                e = E[h % 2]
                A(e[:, 0:256], e[:, 0:256], ACT.Exp, bias=cols[:, h:h + 1], scale=-1.0)
                A(e[:, 256:384], e[:, 256:384], ACT.Exp, bias=cols[:, 8 + h:9 + h], scale=-1.0)
                A(e[0:64, 384:448], e[0:64, 384:448], ACT.Exp, bias=cols[0:64, 16 + h:17 + h], scale=-1.0)\
                    .then_inc(s_E, 1)
                o = tile(t)
                if h >= 2:
                    act.wait_ge(s_pd, h - 1)
                A(eo[h % 2][:, :], o, ACT.Exp, scale=-1.0).then_inc(s_ev[0], 1)
                act.wait_ge(s_emp, h + 1)
                if h >= 1:
                    act.wait_ge(s_pd, h)
                A(emS[:, :], ps[4][:, 0:T], ACT.Copy).then_inc(s_emc, 1)
                if h >= 1:
                    h_rounded(h - 1)
                split(t + 4)
            abs_den(H - 1)
            h_rounded(H - 1)
            outs = [0]

            def store(dst, src):
                act.dma_start(dst, src, allow_slow_non_contiguous=True).then_inc(s_out, 16)
                outs[0] += 1

            for n in range(8):
                t = 8 * Q_WOA + n
                split(t + 4)
                if n == 1:
                    act.wait_ge(s_nm, 1)
                    store(p_m[0, 0:1, :].rearrange("a h -> h a"), mnew[:, 0:1])
                    store(s_m[0].rearrange("b h -> h b"), mnew[:, 1:9])

            def ln(l, last=False):
                q = (Q_WOA, Q_WK - 1, Q_WOB, N_QUADS - 1)[l]
                act.wait_ge(s_ev[1], evac(8 * q + 7)[1])
                A(FS[0][:, :], X[:, 7, :], ACT.Square).then_inc(s_sq7, 1)
                act.wait_ge(s_var, l + 1)
                own(A(rs[:, :], var[:, :], ACT.Ln))
                A(rs[:, :], rs[:, :], ACT.Exp, scale=-0.5).then_inc(s_rs, 1)
                if not last:
                    for n in range(2):
                        act.wait_ge(s_t, 5 * l + n + 1)
                        A(XH[:, n, :], X[:, n, :], ACT.Copy).then_inc(s_xh, 1)
                for m in range(0 if last else 1, 4):
                    n = 2 * m + 1
                    act.wait_ge(s_t, 5 * l + m + 2 - last)
                    ins = A(X[:, n, :], X[:, n, :], ACT.Identity, bias=lnT[:, 32 + 8 * l + n:33 + 8 * l + n],
                            scale=lnT[:, 8 * l + n:8 * l + n + 1])
                    if last:
                        ins.then_inc(s_F, 1)
                    else:
                        own(ins)
                        A(XH[:, n - 1:n + 1, :], X[:, n - 1:n + 1, :], ACT.Copy).then_inc(s_xh, 2)

            def mlp(q0):
                with act.Fori(0, 4) as g:
                    mlp_round(8 * q0, q0, g, 8)

            def mlp_last(q0):
                with act.Fori(0, 3) as g:
                    mlp_round(8 * q0, q0, g, 8)
                mlp_round(8 * q0, q0, 3, 4)

            def mlp_round(up0, q0, g, splits):
                sq0 = 8 * UPS.index(q0)
                for n in range(8):
                    t = up0 + n
                    o = tile(t, g)
                    if n >= 2:
                        act.wait_ge(s_sq, (sq0 + n - 1) + 8 * g)
                    A(FR[n % 2][:, :], o, ACT.Relu).then_inc(s_ev[0], 1)
                    split(t + 4, g)
                    act.wait_ge(s_sq, sq0 + n + 1 + 8 * g)
                    A(HH[:, n, :], FS[n % 2][:, :], ACT.Copy).then_inc(s_hh, 1)
                for n in range(splits):
                    split(up0 + 8 + n + 4, g)

            ln(0)
            act.wait_ge(s_np, 1)
            A(npr[:, :], ps[5][0:1, :], ACT.Copy)
            A(Wst[:, :], ps[4][:, :], ACT.Copy).then_inc(s_nadd, 1)
            act.wait_ge(s_nadd, 2)
            for h2 in range(2):
                act.dma_start(p_C[0, 0].rearrange("(j t) k v -> t k j v", t=2)[h2],
                              Wst[64 * h2:64 * h2 + 64, :].rearrange("p (j v) -> p j v", j=4)).then_inc(s_po, 16)
            act.dma_start(p_n[0, 0].rearrange("h k -> (h k)").unsqueeze(0), npr[:, :]).then_inc(s_po, 16)
            act.dma_start(s_n[0].rearrange("b h k -> b (h k)"), nout[:, :]).then_inc(s_po, 16)
            mlp(Q_MLP0)
            ln(1)
            act.wait_ge(s_po, 16 * 4)
            act.wait_ge(s_out, 16 * outs[0])

            def kv_out(i):
                act.wait_ge(s_tp, i + 1)
                if i >= 2:
                    act.wait_ge(s_to[i % 2], 32 * (i // 2))
                A(KO[i % 2][:, 0:2, :], ps[4 + i % 2][:, 0:256].rearrange("p (t c) -> p t c", t=2), ACT.Copy)
                A(KO[i % 2][0:64, 2, :], ps[4 + i % 2][0:64, 256:384], ACT.Copy).then_inc(s_tc, 1)
                act.wait_ge(s_tc, i + 1)
                act.dma_start(p_k[0, :, i, :].rearrange("(t p) d -> p t d", p=128), KO[i % 2][:, 0:2, :])\
                    .then_inc(s_to[i % 2], 16)
                act.dma_start(s_k_rows[:, i, :], KO[i % 2][0:64, 2, :]).then_inc(s_to[i % 2], 16)

            s_k_rows = s_k_d.rearrange("b t h d -> (b t) h d")
            for n in range(8):
                t = 8 * Q_WK + n
                A(KA[:, n, :], tile(t), ACT.Copy).then_inc(s_ev[0], 1)
                split(t + 4)
                if n >= 1:
                    kv_out(n - 1)
            for n in range(8):
                t = 8 * Q_WV + n
                o = tile(t)
                if n >= 2:
                    act.wait_ge(s_tp, 8 + n - 1)
                A(FR[n % 2][:, :], o, ACT.Copy).then_inc(s_ev[0], 1)
                split(t + 4)
                if n == 0:
                    kv_out(7)

            def p_exp(h):
                act.wait_ge(s_pmx, h + 1)
                pl, st = PL[h % 2], pst[:, 8 * h:8 * h + 8]
                A(pl[:, 0:128], pl[:, 0:128], ACT.Exp, bias=st[:, 0:1], accum_out=st[:, 2:3])
                A(pl[:, 128:384], pl[:, 128:384], ACT.Exp, bias=st[:, 1:2], accum_out=st[:, 3:4]).then_inc(s_pex, 1)

            def p_copy(h):
                act.wait_ge(s_pT, h + 1)
                if h >= 2:
                    act.wait_ge(s_pV, h - 1)
                A(PTt[h % 2][:, :], ps[3][:, 0:384], ACT.Copy).then_inc(s_pTc, 1)

            def p_step(i):
                if 0 <= i < H:
                    p_exp(i)
                if 0 <= i - 2 < H:
                    act.wait_ge(s_pV, i - 2 + 1)
                    A(AT[:, i - 2, :], ps[6][:, 0:256], ACT.Copy).then_inc(s_pA, 1)
                if 0 <= i - 1 < H:
                    p_copy(i - 1)

            for n in range(8):
                t = 8 * Q_WQ + n
                A(QA[:, n, :], tile(t), ACT.Copy, scale=QSCALE).then_inc(s_ev[0], 1)
                split(t + 4)
                if n == 3:
                    act.wait_ge(s_tv, 8)
                    store(p_v[0].rearrange("(t p) h d -> p t (h d)", p=128), VT[:, 0:2, :])
                    store(s_v_d.rearrange("b t h d -> (b t) (h d)"), VT[0:64, 2, :])

            def q_lay(G):
                act.wait_ge(s_qzz, G + 1)
                act.wait_ge(s_ev[0], evac(8 * Q_WQ + 7)[1])
                for bb in range(4):
                    ins = A(QZ[G][:, :, bb, 8 * bb:8 * bb + 8],
                            QA[:, :, TP + 32 * G + 8 * bb:TP + 32 * G + 8 * bb + 8], ACT.Copy)
                ins.then_inc(s_qz, 1)

            def k_copy(P):
                act.wait_ge(s_used, P + 1)
                if P >= 4:
                    act.wait_ge(s_sc, P // 2 - 1)
                A(KT[P // 2 % 2][:, 0:4, 128 * (P % 2):128 * (P % 2) + 128],
                  ps[page_banks(P)[0]][:, :].rearrange("p (h t) -> p h t", h=4), ACT.Copy).then_inc(s_kA, 1)

            def exp_step(G, i):
                nb, nbo, acc = soft(G)
                if i == 0:
                    act.wait_ge(s_sm, G + 1)
                if i < 2:
                    A(PO[:, G, i, :], PO[:, G, i, :], ACT.Exp, bias=nbo[:, i:i + 1],
                      accum_out=acc[:, 5 * i + 4:5 * i + 5]).then_inc(s_ex, 1)
                else:
                    m = i - 2
                    a_, n = m // 4, m % 4
                    c = L[G][:, a_, 256 * n:256 * n + 256]
                    A(c, c, ACT.Exp, bias=nb[:, m:m + 1], accum_out=acc[:, 5 * a_ + n:5 * a_ + n + 1])\
                        .then_inc(s_ex, 1)

            def probs_copy(G):
                act.wait_ge(s_ptt, 5 * G + 1)
                A(PTo[G][:, :, :], ps[1][0:64, 0:256].rearrange("p (a r) -> p a r", a=2), ACT.Copy).then_inc(s_ptc, 1)
                for c in range(4):
                    act.wait_ge(s_ptt, 5 * G + c + 2)
                    A(PT[G][:, 4 * c:4 * c + 4, :], ps[TURN_BANK[c]][:, :].rearrange("p (m r) -> p m r", m=4),
                      ACT.Copy).then_inc(s_ptc, 1)

            def out_copy(G, half):
                act.wait_ge(s_ot, 2 * G + half + 1)
                for bb in (2 * half, 2 * half + 1):
                    b = 4 * G + bb
                    src = ps[4 + 2 * G + bb // 2][:, 256 * (bb % 2):256 * (bb % 2) + 256]\
                        .rearrange("p (h r) -> p h r", h=8)[:, :, 8 * bb:8 * bb + 8]
                    ins = A(AO[:, :, 8 * b:8 * b + 8], src, ACT.Copy)
                ins.then_inc(s_ao, 1)

            q_lay(0)
            for P in range(NPG):
                k_copy(P)
                if P == 5:
                    q_lay(1)
                if 41 <= P < 51:
                    exp_step(0, P - 41)
            probs_copy(0)
            for i in range(H + 2):
                p_step(i)
                if 5 <= i:
                    for m in (2 * i - 10, 2 * i - 9):
                        exp_step(1, m)
            probs_copy(1)
            out_copy(0, 0)
            out_copy(0, 1)
            act.wait_ge(s_used, 2 * NPG - 8)
            for n in range(8):
                A(XH[:, n, 0:TP], AT[:, n, :], ACT.Copy).then_inc(s_xhp, 1)
            out_copy(1, 0)
            out_copy(1, 1)
            act.wait_ge(s_ao, 4)
            for n in range(8):
                A(XH[:, n, TP:T], AO[:, n, :], ACT.Copy).then_inc(s_xh, 1)
            for n in range(8):
                split(8 * Q_WOB + n + 4)
            ln(2)
            mlp_last(Q_MLP1)
            ln(3, True)
            for m in range(4):
                y_copy(m, 0, act, lambda dst, src: A(dst, src, ACT.Copy), s_yA)
                act.wait_ge(s_yA, m + 1)
                act.wait_ge(s_yD, m + 1)
                act.dma_start(y_sample.rearrange("b t c -> (b t) c")[:, 256 * m:256 * m + 256],
                              YO[m][0:64, 2, :]).then_inc(s_ys, 16)
            act.wait_ge(s_ys, 16 * 4)
            act.wait_ge(s_out, 16 * outs[0])

        @block.vector
        def _(dve):
            V = nc.vector
            own = Own(dve, s_d)

            def split(t, turn=0):
                dve.wait_ge(s_hi, t + 1 + 16 * turn)
                V.tensor_tensor(WL[t % SPL][:, :, :], raw[(t // 2) % RAW][:, :, 128 * (t % 2):128 * (t % 2) + 128],
                                WH[t % SPL][:, :, :].bitcast(F32), ALU.subtract).then_inc(s_lo, 1)

            V.memset(VT[64:128, 2, :], 0.0)
            V.memset(WGH[:, :, :].bitcast(F32), 0.0)
            V.memset(WGL[:, :, :].bitcast(F32), 0.0).then_inc(s_gz, 1)
            def x_rest(n):
                dve.wait_ge(s_xf, n + 1)
                dve.wait_ge(s_xh, n + 1)
                V.tensor_tensor(XL[:, n, :], X[:, n, :], XH[:, n, :].bitcast(F32), ALU.subtract).then_inc(s_xl, 1)

            for n in range(8):
                dve.wait_ge(s_xt, n + 1)
                V.tensor_copy(X[:, n, :], ps[2 + n % 2][:, 0:T]).then_inc(s_xf, 1)
                if n >= 1:
                    x_rest(n - 1)
                if n == 3:
                    dve.wait_ge(s_gh, 1)
                    dve.wait_ge(s_gz, 1)
                    V.tensor_tensor(WGL[:, :, 0:8], wgraw[:, :, 0:8], WGH[:, :, 0:8].bitcast(F32), ALU.subtract)
                    V.tensor_tensor(WGL[:, :, 32:40], wgraw[:, :, 8:16], WGH[:, :, 32:40].bitcast(F32),
                                    ALU.subtract).then_inc(s_gl, 1)
            x_rest(7)
            for t in range(3):
                split(t)
            dve.wait_ge(s_gp, 1)
            for w in W:
                V.memset(w[64:128, 384:448], 0.0)
            dve.wait_ge(s_m0, 48)
            dve.wait_ge(s_ml, 32)
            ends = slice(TP + LS - 1, T, LS)
            starts = slice(TP, T, LS)
            V.tensor_scalar(R[0][:, :], ps[5][0:8, 0:T], bg[0:8, 0:1], None, ALU.add)
            own(V.tensor_scalar(R[1][:, :], ps[5][32:40, 0:T], bg[32:40, 0:1], None, ALU.add))
            V.scalar_tensor_tensor(R[2][:, :], R[1][:, :], -1.0, R[1][:, :], ALU.mult, ALU.max).then_inc(s_gabs, 1)
            dve.wait_ge(s_gln, 1)
            own(V.scalar_tensor_tensor(R[1][:, :], R[1][:, :], 0.0, R[2][:, :], ALU.min, ALU.subtract))
            rst, neg = cml[0:8, 448:448 + T], cml[0:8, 448 + T:448 + 2 * T]
            own(V.tensor_tensor_scan(R[3][:, :], rst, R[1][:, :], 0.0, ALU.mult, ALU.add))
            own(V.tensor_tensor(R[4][:, :], R[0][:, :], R[3][:, :], ALU.subtract))
            own(V.tensor_copy(R[0][:, :], R[4][:, :]))
            V.tensor_scalar(R[0][:, 0:1], R[4][:, 0:1], 0.0, None, ALU.max)
            own(V.tensor_tensor(R[0][:, starts], R[4][:, starts], m0, ALU.max))
            own(V.tensor_tensor_scan(R[2][:, :], neg, R[0][:, :], 0.0, ALU.add, ALU.max))
            V.tensor_tensor(R[1][:, :], R[3][:, :], R[2][:, :], ALU.add).then_inc(s_mt, 1)
            V.tensor_scalar(R[5][:, 0:TP], R[4][:, 0:TP], R[2][:, TP - 1:TP], None, ALU.subtract)
            V.tensor_tensor(R[5][:, TP:T].rearrange("p (b t) -> p b t", t=LS),
                            R[4][:, TP:T].rearrange("p (b t) -> p b t", t=LS),
                            bcast(R[2][:, ends], 2, LS), ALU.subtract).then_inc(s_wsl, 1)
            V.tensor_tensor(atr[:, :].rearrange("p (b t) -> p b t", t=LS), bcast(m0, 2, LS),
                            R[2][:, TP:T].rearrange("p (b t) -> p b t", t=LS), ALU.subtract).then_inc(s_al, 1)
            V.tensor_tensor(ael, m0, R[2][:, ends], ALU.subtract).then_inc(s_al, 1)
            V.tensor_tensor(mnew[:, 0:1], R[3][:, TP - 1:TP], R[2][:, TP - 1:TP], ALU.add)
            V.tensor_tensor(mnew[:, 1:9], R[3][:, ends], R[2][:, ends], ALU.add).then_inc(s_nm, 1)

            for n in range(8):
                split(8 * Q_QK + n + 3)
            dve.wait_ge(s_lnt, 1)
            V.tensor_copy(lnT[:, :], ps[4][:, 0:64]).then_inc(s_lnc, 1)
            dve.wait_ge(s_colp, 1)
            c7 = ps[7]
            V.tensor_copy(cols[:, 0:16], c7[:, 0:16])
            V.tensor_copy(cols[0:64, 16:24], c7[0:64, 16:24])
            V.tensor_copy(cols[:, 24:40], c7[:, 24:40])
            V.tensor_copy(cols[0:64, 40:48], c7[0:64, 40:48])
            V.tensor_copy(cols[0:8, 48:56], c7[0:8, 48:56]).then_inc(s_col, 1)
            V.tensor_copy(aeP[:, :, :], c7[:, 320:352].rearrange("p (j b) -> p j b", j=4))
            dve.wait_ge(s_ev[0], evac(8 * Q_QK + 3)[1])
            V.tensor_tensor(aqT[:, :, :], qT[:, :, TP:T], c7[:, 64:320].rearrange("p (j t) -> p j t", j=4),
                            ALU.mult).then_inc(s_bc, 1)
            dve.wait_ge(s_bc, 1)
            V.tensor_tensor(an[:, :, :].rearrange("p j (b t) -> p (j b) t", t=LS),
                            aqT[:, :, :].rearrange("p j (b t) -> p (j b) t", t=LS),
                            bcast(c7[:, 352:384], 2, LS), ALU.mult).then_inc(s_bc, 1)

            def v_copy(n, done, bank):
                c = slice(128 * n, 128 * n + 128)
                V.tensor_copy(VT[:, 0:2, c], bank[:, 0:256].rearrange("p (t c) -> p t c", t=2))
                V.tensor_copy(VT[0:64, 2, c], bank[0:64, 256:384]).then_inc(done, 1)

            for n in range(8):
                split(8 * Q_V + n + 3)
                if n >= 1:
                    dve.wait_ge(s_vt, n)
                    v_copy(n - 1, s_vc, ps[4 + (n - 1) % 2])
            dve.wait_ge(s_vt, 8)
            v_copy(7, s_vc, ps[5])

            def decay(h):
                dve.wait_ge(s_sp, h + 1)
                e = E[h % 2]
                V.tensor_tensor(e[:, 0:256], ps[3][:, 0:256], cml[:, 0:256], ALU.add)
                V.tensor_tensor(e[:, 256:384], ps[3][:, 128:256], cml[:, 256:384], ALU.add)
                V.tensor_tensor(e[0:64, 384:448], ps[3][0:64, 256:320], cml[0:64, 384:448], ALU.add)\
                    .then_inc(s_D, 1)

            def weights(h):
                dve.wait_ge(s_E, h + 1)
                if h >= 2:
                    dve.wait_ge(s_num, h - 1)
                w, e = W[h % 2], E[h % 2]
                V.tensor_tensor(w[:, 0:384], ps[2][:, 0:384], e[:, 0:384], ALU.mult)
                V.tensor_tensor(w[0:64, 384:448], ps[2][0:64, 384:448], e[0:64, 384:448], ALU.mult)\
                    .then_inc(s_W, 1)

            def divisor(h):
                d = (A1, A2)[h % 2][:, :]
                dve.wait_ge(s_abs, h + 1)
                dve.wait_ge(s_emc, h + 1)
                own(V.tensor_tensor(d, d, emS[:, :], ALU.max))
                V.scalar_tensor_tensor(d, eo[h % 2][:, :], 1.0, d, ALU.add, ALU.mult).then_inc(s_pd, 1)

            def gated(h):
                dve.wait_ge(s_pd, h + 1)
                own(V.reciprocal(rec[:, :], (A1, A2)[h % 2][:, :]))
                dve.wait_ge(s_num, h + 1)
                if h >= 1:
                    dve.wait_ge(s_hh, h)
                V.tensor_tensor(hg[:, :], ps[6 + h % 2][:, 0:T], rec[:, :], ALU.mult).then_inc(s_hg, 1)

            def h_rest(h):
                dve.wait_ge(s_hh, h + 1)
                V.tensor_tensor(HL[:, h, :], hg[:, :], HH[:, h, :].bitcast(F32), ALU.subtract).then_inc(s_hl, 1)

            for h in range(H):
                decay(h)
                if h >= 1:
                    divisor(h - 1)
                weights(h)
                if h >= 1:
                    gated(h - 1)
                split(8 * Q_O + h + 3)
                if h >= 1:
                    h_rest(h - 1)
            divisor(H - 1)
            gated(H - 1)
            h_rest(H - 1)

            def residual(t, turn=0, scale=None):
                n = t % 8
                dve.wait_ge(s_mm, t + 1 + 16 * turn)
                if scale is None:
                    ins = V.tensor_tensor(X[:, n, :], X[:, n, :], ps[t % 2][:, 0:T], ALU.add)
                else:
                    ins = V.scalar_tensor_tensor(X[:, n, :], X[:, n, :], scale, ps[t % 2][:, 0:T], ALU.mult, ALU.add)
                ins.then_inc(s_ev[1], 1)

            def state(n):
                if n < 2:
                    for i in (2 * n, 2 * n + 1):
                        dve.wait_ge(s_kt, i + 1)
                        for w, bt, lo in ((128, slice(0, 2), 24), (64, slice(2, 3), 40)):
                            nt = bt.stop - bt.start
                            V.tensor_tensor(
                                wsK[0:w, bt, 128 * i:128 * i + 128].rearrange("p t (h d) -> p t h d", h=2),
                                ps[2 + i % 2][0:w, 128 * bt.start:128 * bt.stop]
                                .rearrange("p (t h d) -> p t h d", t=nt, h=2),
                                bcast(cols[0:w, lo:lo + 8 * nt].rearrange("p (t h) -> p t h", t=nt)
                                      [:, :, 2 * i:2 * i + 2], 3, 64), ALU.mult).then_inc(s_wk, 1)
                if n >= 3:
                    j = n - 3
                    for half in range(2):
                        dve.wait_ge(s_cp, 2 * j + half + 1)
                        for bb in range(4):
                            b = 4 * half + bb
                            ins = V.scalar_tensor_tensor(C0[:, j, b, :], C0[:, j, b, :], aeP[:, j, b:b + 1],
                                                         c_bank(j, half)[:, 128 * bb:128 * bb + 128], ALU.mult, ALU.add)
                        ins.then_inc(s_cadd, 1)

            state(0)
            for n in range(8):
                split(8 * Q_WOA + n + 3)
                residual(8 * Q_WOA + n, 0, ALPHA)
                if n < 6:
                    state(n + 1)

            def ln(l, last=False):
                dve.wait_ge(s_lnp, 2 * l + 1)
                own(V.tensor_scalar(mu[:, :], ps[2][:, 0:T], 1.0 / DM, None, ALU.mult))
                own(V.tensor_tensor(tmp[:, :], mu[:, :], mu[:, :], ALU.mult))
                dve.wait_ge(s_lnp, 2 * l + 2)
                own(V.scalar_tensor_tensor(var[:, :], ps[3][:, 0:T], 1.0 / DM, tmp[:, :], ALU.mult, ALU.subtract))
                V.tensor_scalar(var[:, :], var[:, :], 0.0, EPS, ALU.max, ALU.add).then_inc(s_var, 1)
                for m in range(2):
                    pair = X[:, 2 * m:2 * m + 2, :]
                    own(V.tensor_tensor(pair, pair, bcast(mu[:, :], 1, 2), ALU.subtract))
                dve.wait_ge(s_rs, l + 1)
                own(V.scalar_tensor_tensor(tmp[:, :], rs[:, :], -0.5, var[:, :], ALU.mult, ALU.mult))
                own(V.tensor_tensor(tmp[:, :], tmp[:, :], rs[:, :], ALU.mult))
                own(V.scalar_tensor_tensor(rs[:, :], tmp[:, :], 1.5, rs[:, :], ALU.add, ALU.mult))

                def rest(m):
                    dve.wait_ge(s_xh, (8, 16, 32)[l] + 2 * m + 2)
                    V.tensor_tensor(XL[:, 2 * m:2 * m + 2, :], X[:, 2 * m:2 * m + 2, :],
                                    XH[:, 2 * m:2 * m + 2, :].bitcast(F32), ALU.subtract).then_inc(s_xl, 2)

                def gain(n):
                    return V.tensor_scalar(X[:, n, :], X[:, n, :], lnT[:, 8 * l + n:8 * l + n + 1],
                                           lnT[:, 32 + 8 * l + n:33 + 8 * l + n], ALU.mult, ALU.add)

                if not last:
                    for n in range(2):
                        own(V.tensor_tensor(X[:, n, :], X[:, n, :], rs[:, :], ALU.mult))
                        gain(n).then_inc(s_t, 1)
                    for n in range(2):
                        dve.wait_ge(s_xh, (8, 16, 32)[l] + n + 1)
                        V.tensor_tensor(XL[:, n, :], X[:, n, :], XH[:, n, :].bitcast(F32), ALU.subtract)\
                            .then_inc(s_xl, 1)
                for m in range(0 if last else 1, 4):
                    pair = X[:, 2 * m:2 * m + 2, :]
                    if m >= 2:
                        dve.wait_ge(s_pc, 2 * l + m - 1)
                    own(V.tensor_tensor(pair, pair, bcast(rs[:, :], 1, 2), ALU.mult))
                    gain(2 * m).then_inc(s_t, 1)
                    if m >= 2 and not last:
                        rest(m - 1)
                if not last:
                    rest(3)

            def mlp_round(q0, g, splits):
                c0 = 8 * UPS.index(q0)
                for n in range(8):
                    t = 8 * q0 + n
                    split(t + 3, g)
                    dve.wait_ge(s_ev[0], evac(t)[1] + 8 * g)
                    if n >= 2:
                        dve.wait_ge(s_hh, 8 + c0 + n - 1 + 8 * g)
                    V.tensor_tensor(FS[n % 2][:, :], FR[n % 2][:, :], FR[n % 2][:, :], ALU.mult).then_inc(s_sq, 1)
                    dve.wait_ge(s_hh, 8 + c0 + n + 1 + 8 * g)
                    V.tensor_tensor(HL[:, n, :], FS[n % 2][:, :], HH[:, n, :].bitcast(F32), ALU.subtract)\
                        .then_inc(s_hl, 1)
                dve.wait_ge(s_al2, 8 if q0 == Q_MLP0 else 24)
                for n in range(8):
                    if n < splits:
                        split(8 * q0 + 8 + n + 3, g)
                    residual(8 * q0 + 8 + n, g)

            ln(0)
            dve.wait_ge(s_np, 1)
            own(V.tensor_tensor(nout[:, :].rearrange("p (h k) -> p h k", h=8),
                                n0[:, :].rearrange("p (h k) -> p h k", h=8), bcast(cols[0:8, 48:56], 2, DK), ALU.mult))
            V.tensor_tensor(nout[:, :], nout[:, :], ps[6][0:8, :], ALU.add).then_inc(s_nadd, 1)
            with dve.Fori(0, 4) as g:
                mlp_round(Q_MLP0, g, 8)
            ln(1)
            for n in range(8):
                split(8 * Q_WK + n + 3)
            for n in range(8):
                split(8 * Q_WV + n + 3)
                if n >= 1:
                    dve.wait_ge(s_tp, 8 + n)
                    v_copy(n - 1, s_tv, ps[4 + (n - 1) % 2])
            dve.wait_ge(s_at, 16)

            def p_max(h):
                dve.wait_ge(s_pS, h + 1)
                if h >= 2:
                    dve.wait_ge(s_pT, h - 1)
                pl, st = PL[h % 2], pst[:, 8 * h:8 * h + 8]
                own(V.scalar_tensor_tensor(pl[:, :], dist, SLOPES[h], ps[2][:, 0:384], ALU.mult, ALU.add))
                V.tensor_reduce(st[:, 0:1], pl[:, 0:128], AX.X, ALU.max, negate=True)
                V.tensor_reduce(st[:, 1:2], pl[:, 128:384], AX.X, ALU.max, negate=True).then_inc(s_pmx, 1)

            def p_norm(h):
                dve.wait_ge(s_pex, h + 1)
                pl, st = PL[h % 2], pst[:, 8 * h:8 * h + 8]
                own(V.reciprocal(st[:, 4:6], st[:, 2:4]))
                V.tensor_scalar(pl[:, 0:128], pl[:, 0:128], st[:, 4:5], None, ALU.mult).then_inc(s_pnm, 1)
                V.tensor_scalar(pl[:, 128:384], pl[:, 128:384], st[:, 5:6], None, ALU.mult).then_inc(s_pnm, 1)

            def p_step(i):
                if 0 <= i < H:
                    p_max(i)
                if 0 <= i < H:
                    p_norm(i)

            for n in range(8):
                split(8 * Q_WQ + n + 3)
                if n == 0:
                    dve.wait_ge(s_tp, 16)
                    v_copy(7, s_tv, ps[5])

            def k_copy(P):
                dve.wait_ge(s_used, P + 1)
                if P >= 4:
                    dve.wait_ge(s_sc, P // 2 - 1)
                V.tensor_copy(KT[P // 2 % 2][:, 4:8, 128 * (P % 2):128 * (P % 2) + 128],
                              ps[page_banks(P)[1]][:, :].rearrange("p (h t) -> p h t", h=4)).then_inc(s_kD, 1)

            def parts(G):
                s = sm[:, G, :]
                return s[:, 22:30], s[:, 30:38], s[:, 38:46], s[:, 46:48], s[:, 48:50], s[:, 50:52], s[:, 52:54]

            def logits(G, c):
                bsum = parts(G)[0]
                bank = ps[SCORE_BANK[c]]
                V.tensor_reduce(bsum[:, 2 * c:2 * c + 2], bank[:, :].rearrange("p (n k) -> p n k", n=2),
                                AX.X, ALU.add)
                V.scalar_tensor_tensor(L[G][:, c // 2, 512 * (c % 2):512 * (c % 2) + 512],
                                       keys[:, 512 * (c % 2):512 * (c % 2) + 512], slope[:, c // 2:c // 2 + 1],
                                       bank[:, :], ALU.mult, ALU.add).then_inc(s_Lr, 1)

            def block_max(G):
                _, mxb, _, omx, _, _, _ = parts(G)
                dve.wait_ge(s_Lr, 4 * G + 4)
                V.tensor_reduce(mxb, L[G][:, :, :].rearrange("p a (n k) -> p (a n) k", n=4), AX.X, ALU.max)
                own(V.tensor_reduce(omx, PO[:, G, :, :], AX.X, ALU.max))

            def left_out(G):
                bsum, _, pen, _, mn, ix, _ = parts(G)
                an_ = "p (a n) -> p a n"
                own(V.tensor_reduce(mn, bsum.rearrange(an_, a=2), AX.X, ALU.min))
                own(V.tensor_tensor(pen.rearrange(an_, a=2), bsum.rearrange(an_, a=2), bcast(mn, 2, 4), ALU.is_le))
                own(V.tensor_tensor(pen, pen, nidx, ALU.mult))
                own(V.tensor_reduce(ix, pen.rearrange(an_, a=2), AX.X, ALU.max))
                own(V.tensor_tensor(pen.rearrange(an_, a=2), nidx.rearrange(an_, a=2), bcast(ix, 2, 4), ALU.is_equal))
                own(V.tensor_scalar(pen, pen, -BIG, None, ALU.mult))

            def biases(G):
                _, mxb, pen, omx, _, _, m2 = parts(G)
                nb, nbo, _ = soft(G)
                an_ = "p (a n) -> p a n"
                own(V.tensor_tensor(mxb, mxb, pen, ALU.add))
                own(V.tensor_reduce(m2, mxb.rearrange(an_, a=2), AX.X, ALU.max))
                own(V.tensor_tensor(m2, m2, omx, ALU.max))
                V.tensor_scalar(nbo, m2, -1.0, None, ALU.mult)
                V.tensor_tensor(nb.rearrange(an_, a=2), pen.rearrange(an_, a=2), bcast(m2, 2, 4), ALU.subtract)\
                    .then_inc(s_sm, 1)

            def reciprocals(G):
                den, rden = sm[:, G, 20:22], sm[:, G, 54:56]
                dve.wait_ge(s_ex, 10 * G + 10)
                own(V.tensor_reduce(den, soft(G)[2].rearrange("p (a n) -> p a n", a=2), AX.X, ALU.add))
                own(V.reciprocal(rden, den))

            def scale_out(G, half):
                rden = sm[:, G, 54:56]
                for c in (2 * half, 2 * half + 1):
                    bb, a_ = 2 * (c // 2), c % 2
                    if a_ == 0:
                        dve.wait_ge(s_used, NPG + 32 * G + 8 * bb + 16)
                    ins = V.tensor_scalar(ON[G][:, bb:bb + 2, a_, :],
                                          ps[4 + 2 * G + c // 2][:, :]
                                          .rearrange("p (b a d) -> p b a d", b=2, a=2)[:, :, a_, :],
                                          rden[:, a_:a_ + 1], None, ALU.mult)
                    if a_ == 1:
                        ins.then_inc(s_on, 1)

            dve.wait_ge(s_own, 1)
            V.tensor_tensor(PO[:, :, :, :].rearrange("p g a k -> p (g a k)"), ps[7][:, 0:256], bias_own, ALU.add)\
                .then_inc(s_ownr, 1)
            dve.wait_ge(s_ownr, 1)
            for P in range(NPG):
                k_copy(P)
                if P == 33:
                    dve.wait_ge(s_sc, 16)
                    logits(0, 0)
                    logits(0, 2)
                elif P == 35:
                    logits(0, 1)
                    logits(0, 3)
                elif P == 37:
                    block_max(0)
                elif P == 39:
                    left_out(0)
                    biases(0)
            for i in range(2):
                dve.wait_ge(s_to[i], 32 * 4)
            dve.wait_ge(s_sc, 32)
            for c in (0, 2, 1, 3):
                logits(1, c)
            for i in range(H):
                p_step(i)
                if i == 1:
                    block_max(1)
                elif i == 2:
                    left_out(1)
                elif i == 3:
                    biases(1)
            dve.wait_ge(s_pA, H)
            reciprocals(0)
            scale_out(0, 0)
            scale_out(0, 1)
            reciprocals(1)
            scale_out(1, 0)
            for n in range(8):
                dve.wait_ge(s_xhp, n + 1)
                V.tensor_tensor(XL[:, n, 0:TP], AT[:, n, :], XH[:, n, 0:TP].bitcast(F32), ALU.subtract)
            scale_out(1, 1)
            for n in range(8):
                dve.wait_ge(s_xh, 8 * 3 + n + 1)
                V.tensor_tensor(XL[:, n, TP:T], AO[:, n, :], XH[:, n, TP:T].bitcast(F32), ALU.subtract)\
                    .then_inc(s_xl, 1)
            dve.wait_ge(s_al2, 16)
            for n in range(8):
                split(8 * Q_WOB + n + 3)
                residual(8 * Q_WOB + n)
            ln(2)
            with dve.Fori(0, 3) as g:
                mlp_round(Q_MLP1, g, 8)
            mlp_round(Q_MLP1, 3, 5)
            ln(3, True)
            for m in range(4):
                y_copy(m, 1, dve, V.tensor_copy, s_yD)

        @block.gpsimd
        def _(pool):
            G = nc.gpsimd
            own = Own(pool, s_p)

            def sums(l, q, n):
                pool.wait_ge(s_ev[1], evac(8 * q + n)[1])
                if n == 0:
                    G.tensor_copy(A1[:, :], X[:, 0, :])
                    own(G.tensor_tensor(A2[:, :], X[:, 0, :], X[:, 0, :], ALU.mult))
                else:
                    own(G.tensor_tensor(SQ[:, :], X[:, n, :], X[:, n, :], ALU.mult))
                    G.tensor_tensor(A1[:, :], A1[:, :], X[:, n, :], ALU.add)
                    own(G.tensor_tensor(A2[:, :], A2[:, :], SQ[:, :], ALU.add))
                if n == 6:
                    G.tensor_copy(SQ[:, 0:1], A2[:, 0:1]).then_inc(s_st, 1)

            def centred(l):
                pool.wait_ge(s_var, l + 1)
                for m in range(2, 4):
                    pair = X[:, 2 * m:2 * m + 2, :]
                    G.tensor_tensor(pair, pair, bcast(mu[:, :], 1, 2), ALU.subtract).then_inc(s_pc, 1)

            def scaled(l):
                for m in range(4):
                    pair = X[:, 2 * m:2 * m + 2, :]
                    pool.wait_ge(s_xl, (8, 16, 32)[l] + 2 * m + 2)
                    G.tensor_scalar(pair, pair, ALPHA, 1.0, ALU.mult, ALU.mult).then_inc(s_al2, 2)

            own(G.memset(aqZ[:, :, :, :], 0.0))
            pool.wait_ge(s_bc, 1)
            for b in range(NB):
                ins = G.tensor_copy(aqZ[:, :, b, 8 * (b % 4):8 * (b % 4) + 8], aqT[:, :, 8 * b:8 * b + 8])
            ins.then_inc(s_aqz, 1)
            pool.wait_ge(s_mm, 8 * Q_O + 8)
            pool.wait_ge(s_vc, 8)
            for h in range(H):
                G.tensor_tensor(Vm[:, h, :, :], bcast(VT[0:64, 2, 128 * h:128 * h + 128], 1, 4),
                                bcast(bmask4[0:64, :], 2, 128), ALU.mult).then_inc(s_vm, 1)
            for n in range(7):
                sums(0, Q_WOA, n)
            centred(0)
            scaled(0)
            for j in range(4):
                pool.wait_ge(s_cadd, 2 * j + 2)
                for h2 in range(2):
                    pool.dma_start(s_C[0, :, 2 * j + h2].rearrange("b k v -> k b v"),
                                  C0[64 * h2:64 * h2 + 64, j, :, :]).then_inc(s_co, 16)
            for n in range(7):
                sums(1, Q_WK - 1, n)
            centred(1)
            scaled(1)
            for group in range(2):
                G.memset(QZ[group][:, :, :, :], 0.0).then_inc(s_qzz, 1)

            for n in range(7):
                sums(2, Q_WOB, n)
            centred(2)
            scaled(2)
            for n in range(7):
                sums(3, N_QUADS - 1, n)
            centred(3)


INS = ["x_prompt", "x_sample", "state_C", "state_n", "state_m", "cache_k", "cache_v", "page_table", "w_in_a",
       "b_gate_a", "w_out_a", "w_q_b", "w_out_b", "w_kv", "w_up", "w_down", "ln_g", "ln_b"]
OUTS = [(1, TP, DM), (NB, LS, DM), (1, 1, H, DK, 128), (1, 1, H, DK), (1, 1, H), (1, TP, H, 128), (1, TP, H, 128),
        (1, NB, H, DK, 128), (1, NB, H, DK), (1, NB, H), (NB, LS, H, 128), (NB, LS, H, 128)]


def kernel(**inputs):
    import concourse.bacc as bacc
    from concourse.bass_utils import run_bass_kernel_spmd

    nc = bacc.Bacc("TRN2", target_bir_lowering=False, num_devices=1)
    named = {n: np.ascontiguousarray(inputs[n]) for n in INS}
    named.update(constants())
    arrays, args = {}, []
    for name, a in named.items():
        arrays[f"in_{name}_dram"] = a
        args.append(nc.dram_tensor(f"in_{name}_dram", a.shape, mybir.dt.from_np(a.dtype), kind="ExternalInput").ap())
    for i, shape in enumerate(OUTS):
        args.append(nc.dram_tensor(f"out_{i}_dram", shape, F32, kind="ExternalOutput").ap())
    build(nc, *args)
    r = run_bass_kernel_spmd(nc, [arrays], core_ids=[0])
    return tuple(r.results[0][f"out_{i}_dram"] for i in range(len(OUTS)))
```
